# Optimizing a Trainium2 kernel written in Bass

```python
import math
import jax
import jax.numpy as jnp
from jax import lax
import numpy as np
import jax, jax.numpy as jnp

D_MODEL = 1024
BATCH = 1
SEQ = 256
DEPTH = 2

N_A_LAYERS = DEPTH // 2
N_B_LAYERS = DEPTH - N_A_LAYERS
PLE_DIM = 256
D_FF = 2816
EPS = 1e-6
N_SUBNORMS = 8

MLSTM_HEADS = 4
MLSTM_DV = D_MODEL // MLSTM_HEADS
MLSTM_DK = MLSTM_DV // 2
MLSTM_CHUNK = 128
MLSTM_QK_W = MLSTM_HEADS * MLSTM_DK
MLSTM_IN = 2 * MLSTM_QK_W + 2 * D_MODEL + 2 * MLSTM_HEADS

DIFF_HEAD_DIM = 64
DIFF_HEADS = D_MODEL // (2 * DIFF_HEAD_DIM)
Q_BLOCK = 128


def rms_norm(x, g):
    xf = x.astype(jnp.float32)
    y = xf * lax.rsqrt(jnp.mean(xf * xf, axis=-1, keepdims=True) + EPS)
    return (y * g.astype(jnp.float32)).astype(x.dtype)

def swiglu(x, w_in, w_out):
    gate, up = jnp.split(x @ w_in, 2, axis=-1)
    return (jax.nn.silu(gate) * up) @ w_out

def mlstm_chunkwise(q, k, v, log_i, log_f):
    B, H, S, DK = q.shape
    DV = v.shape[-1]
    L = MLSTM_CHUNK
    NC = S // L
    q, k, v = (t.astype(jnp.float32) for t in (q, k, v))

    def chunks(t):
        return jnp.moveaxis(t.reshape(B, H, NC, L, *t.shape[3:]), 2, 0)

    xs = tuple(chunks(t) for t in (q, k, v, log_i, log_f))
    causal = jnp.tril(jnp.ones((L, L), dtype=bool))

    def step(carry, inp):
        C, n, m = carry
        qj, kj, vj, li, lf = inp
        b = jnp.cumsum(lf, axis=-1)
        d = b[..., :, None] - b[..., None, :] + li[..., None, :]
        d = jnp.where(causal, d, -jnp.inf)
        inter = b + m[..., None]
        m_t = jnp.maximum(inter, jnp.max(d, axis=-1))
        w = jnp.exp(d - m_t[..., None])
        s_inter = jnp.exp(inter - m_t)
        qk = jnp.einsum('bhtd,bhsd->bhts', qj, kj) * w
        num = (jnp.einsum('bhts,bhsv->bhtv', qk, vj)
               + s_inter[..., None] * jnp.einsum('bhtd,bhdv->bhtv', qj, C))
        den = jnp.sum(qk, axis=-1) + s_inter * jnp.einsum('bhtd,bhd->bht', qj, n)
        h = num / jnp.maximum(jnp.abs(den), jnp.exp(-m_t))[..., None]
        bL = b[..., -1]
        g = bL[..., None] - b + li
        m_new = jnp.maximum(bL + m, jnp.max(g, axis=-1))
        sc = jnp.exp(g - m_new[..., None])
        decay = jnp.exp(bL + m - m_new)
        C_new = decay[..., None, None] * C + jnp.einsum('bhs,bhsd,bhsv->bhdv', sc, kj, vj)
        n_new = decay[..., None] * n + jnp.einsum('bhs,bhsd->bhd', sc, kj)
        return (C_new, n_new, m_new), h

    init = (jnp.zeros((B, H, DK, DV), jnp.float32),
            jnp.zeros((B, H, DK), jnp.float32),
            jnp.full((B, H), -jnp.inf, jnp.float32))
    _, hs = lax.scan(step, init, xs)
    return jnp.moveaxis(hs, 0, 2).reshape(B, H, S, DV)

def mlstm_mixer(x, w_in, b_gates, head_norm, w_out):
    B, S, _ = x.shape
    proj = x @ w_in
    q, k, v, o, gates = jnp.split(
        proj, [MLSTM_QK_W, 2 * MLSTM_QK_W, 2 * MLSTM_QK_W + D_MODEL,
               2 * MLSTM_QK_W + 2 * D_MODEL], axis=-1)

    def heads(t, d):
        return t.reshape(B, S, MLSTM_HEADS, d).transpose(0, 2, 1, 3)

    q = heads(q, MLSTM_DK)
    k = heads(k, MLSTM_DK) * (MLSTM_DK ** -0.5)
    v = heads(v, MLSTM_DV)
    gates = gates.astype(jnp.float32) + b_gates.astype(jnp.float32)
    log_i = gates[..., :MLSTM_HEADS].transpose(0, 2, 1)
    log_f = jax.nn.log_sigmoid(gates[..., MLSTM_HEADS:]).transpose(0, 2, 1)
    h = mlstm_chunkwise(q, k, v, log_i, log_f)
    h = rms_norm(h, head_norm[:, None, :])
    h = h.transpose(0, 2, 1, 3).reshape(B, S, D_MODEL).astype(x.dtype)
    return (jax.nn.sigmoid(o) * h) @ w_out

def shared_kv(x, kv_norm, w_kv):
    B, S, _ = x.shape
    kv = rms_norm(x, kv_norm) @ w_kv
    k, v = jnp.split(kv, 2, axis=-1)
    k = k.reshape(B, S, 2 * DIFF_HEADS, DIFF_HEAD_DIM).transpose(0, 2, 1, 3)
    v = v.reshape(B, S, DIFF_HEADS, 2 * DIFF_HEAD_DIM).transpose(0, 2, 1, 3)
    return k, v

def diff_attention(x, k_sh, v_sh, w_q, lam_vecs, subln, w_out, lam_init):
    B, S, _ = x.shape
    H, DH = DIFF_HEADS, DIFF_HEAD_DIM
    q = (x @ w_q).reshape(B, S, 2 * H, DH).transpose(0, 2, 1, 3) * (DH ** -0.5)
    lv = lam_vecs.astype(jnp.float32)
    lam = jnp.exp(jnp.sum(lv[0] * lv[1])) - jnp.exp(jnp.sum(lv[2] * lv[3])) + lam_init
    nb = S // Q_BLOCK
    qb = jnp.moveaxis(q.reshape(B, 2 * H, nb, Q_BLOCK, DH), 2, 0)
    key_pos = jnp.arange(S)

    def block(args):
        qi, start = args
        s = jnp.einsum('bhqd,bhkd->bhqk', qi, k_sh).astype(jnp.float32)
        qpos = start + jnp.arange(Q_BLOCK)
        s = jnp.where(key_pos[None, :] <= qpos[:, None], s, -jnp.inf)
        a = jax.nn.softmax(s, axis=-1).reshape(B, H, 2, Q_BLOCK, S)
        diff = a[:, :, 0] - lam * a[:, :, 1]
        return jnp.einsum('bhqk,bhkv->bhqv', diff.astype(v_sh.dtype), v_sh)

    o = lax.map(block, (qb, jnp.arange(nb) * Q_BLOCK))
    o = o.transpose(1, 2, 0, 3, 4).reshape(B, H, S, 2 * DH)
    o = rms_norm(o, subln) * (1.0 - lam_init)
    o = o.transpose(0, 2, 1, 3).reshape(B, S, D_MODEL).astype(x.dtype)
    return o @ w_out

def first_inputs(seed: int = 0) -> dict:
    key = jax.random.key(seed)
    ks = jax.random.split(key, 20)
    f32 = jnp.float32

    def nrm(k, shape, fan_in):
        return jax.random.normal(k, shape, f32) * (fan_in ** -0.5)

    def gain(k, shape):
        return 1.0 + 0.05 * jax.random.normal(k, shape, f32)

    f_bias = jnp.linspace(3.0, 6.0, MLSTM_HEADS, dtype=f32)
    b_gates = jnp.concatenate(
        [0.1 * jax.random.normal(ks[8], (N_A_LAYERS, MLSTM_HEADS), f32),
         f_bias[None, :] + 0.1 * jax.random.normal(ks[9], (N_A_LAYERS, MLSTM_HEADS), f32)], axis=-1)
    return {
        "x": jax.random.normal(ks[0], (BATCH, SEQ, D_MODEL), f32),
        "p": jax.random.normal(ks[1], (DEPTH, BATCH, SEQ, PLE_DIM), f32),
        "norm_g": gain(ks[2], (DEPTH, N_SUBNORMS, D_MODEL)),
        "w_ffn_in": nrm(ks[3], (DEPTH, 2, D_MODEL, 2 * D_FF), D_MODEL),
        "w_ffn_out": nrm(ks[4], (DEPTH, 2, D_FF, D_MODEL), D_FF),
        "w_ple_proj": nrm(ks[5], (DEPTH, PLE_DIM, D_MODEL), PLE_DIM),
        "w_ple_gate": nrm(ks[6], (DEPTH, D_MODEL, D_MODEL), D_MODEL),
        "mlstm_w_in": nrm(ks[7], (N_A_LAYERS, D_MODEL, MLSTM_IN), D_MODEL),
        "mlstm_b_gates": b_gates,
        "mlstm_head_norm": gain(ks[10], (N_A_LAYERS, MLSTM_HEADS, MLSTM_DV)),
        "mlstm_w_out": nrm(ks[11], (N_A_LAYERS, D_MODEL, D_MODEL), D_MODEL),
        "kv_norm": gain(ks[12], (D_MODEL,)),
        "w_kv": nrm(ks[13], (D_MODEL, 2 * D_MODEL), D_MODEL),
        "diff_w_q": nrm(ks[14], (N_B_LAYERS, D_MODEL, D_MODEL), D_MODEL),
        "diff_lambda": 0.1 * jax.random.normal(ks[15], (N_B_LAYERS, 4, DIFF_HEAD_DIM), f32),
        "diff_subln": gain(ks[16], (N_B_LAYERS, 2 * DIFF_HEAD_DIM)),
        "diff_w_out": nrm(ks[17], (N_B_LAYERS, D_MODEL, D_MODEL), D_MODEL),
    }

def first_block(x, p, norm_g, w_ffn_in, w_ffn_out, w_ple_proj, w_ple_gate,
              mlstm_w_in, mlstm_b_gates, mlstm_head_norm, mlstm_w_out,
              kv_norm, w_kv, diff_w_q, diff_lambda, diff_subln, diff_w_out):
    k_sh = None
    v_sh = None
    for layer in range(DEPTH):
        g = norm_g[layer]
        h = swiglu(rms_norm(x, g[0]), w_ffn_in[layer, 0], w_ffn_out[layer, 0])
        x = x + 0.5 * rms_norm(h, g[1])
        h = rms_norm(x, g[2])
        if layer < N_A_LAYERS:
            h = mlstm_mixer(h, mlstm_w_in[layer], mlstm_b_gates[layer],
                            mlstm_head_norm[layer], mlstm_w_out[layer])
        else:
            j = layer - N_A_LAYERS
            lam_init = 0.8 - 0.6 * math.exp(-0.3 * layer)
            h = diff_attention(h, k_sh, v_sh, diff_w_q[j], diff_lambda[j],
                               diff_subln[j], diff_w_out[j], lam_init)
        x = x + rms_norm(h, g[3])
        h = swiglu(rms_norm(x, g[4]), w_ffn_in[layer, 1], w_ffn_out[layer, 1])
        x = x + 0.5 * rms_norm(h, g[5])
        gate = jax.nn.sigmoid(rms_norm(x, g[6]) @ w_ple_gate[layer])
        e = p[layer].astype(x.dtype) @ w_ple_proj[layer]
        x = x + rms_norm(e * gate, g[7])
        if layer == N_A_LAYERS - 1:
            k_sh, v_sh = shared_kv(x, kv_norm, w_kv)
    return x


DEPTH_2 = 1

D_CONV = D_MODEL
CONV_WIDTH = 3
N_HEADS = 16
HEAD_DIM = 64
D_ATTN = N_HEADS * HEAD_DIM
ATTN_PATTERNS = ((128, 1), (512, 4), (2048, 16))
QB = 128
IN_COLS = 4 * D_CONV + 4 * D_ATTN + 2 * D_MODEL


def rms_norm_2(x, g):
    xf = x.astype(jnp.float32)
    y = xf * lax.rsqrt(jnp.mean(xf * xf, axis=-1, keepdims=True) + EPS)
    return (y * g.astype(jnp.float32)).astype(x.dtype)

def alibi_slopes(n_heads):
    return jnp.exp2(-8.0 * jnp.arange(1, n_heads + 1, dtype=jnp.float32) / n_heads)

def causal_depthwise_conv(u, w):
    return lax.conv_general_dilated(
        u, w.astype(u.dtype)[:, None, :], window_strides=(1,),
        padding=[(CONV_WIDTH - 1, 0)],
        dimension_numbers=("NWC", "WIO", "NWC"),
        feature_group_count=u.shape[-1])

def dilated_window_attention(q, k, v, window, dilation, slopes):
    B, S, H, Dh = q.shape
    d = dilation
    win = window // dilation
    assert win == QB
    L = S // d
    nb = -(-L // QB)
    Lp = nb * QB

    def to_sub(t):
        t = t.reshape(B, L, d, H, Dh)
        return jnp.pad(t, ((0, 0), (0, Lp - L), (0, 0), (0, 0), (0, 0)))

    qs = (to_sub(q) * (Dh ** -0.5)).reshape(B, nb, QB, d, H, Dh)

    def key_blocks(t):
        tp = jnp.pad(to_sub(t), ((0, 0), (QB, 0), (0, 0), (0, 0), (0, 0)))
        prev = tp[:, :Lp].reshape(B, nb, QB, d, H, Dh)
        cur = tp[:, QB:QB + Lp].reshape(B, nb, QB, d, H, Dh)
        return jnp.concatenate([prev, cur], axis=2)

    kb = key_blocks(k)
    vb = key_blocks(v)

    s = jnp.einsum("bnqrhe,bnkrhe->bnrhqk", qs, kb,
                   preferred_element_type=jnp.float32)
    q_loc = jnp.arange(QB)[:, None] + QB
    k_loc = jnp.arange(2 * QB)[None, :]
    delta = q_loc - k_loc
    key_sub = jnp.arange(nb)[:, None] * QB - QB + jnp.arange(2 * QB)[None, :]
    valid = ((delta >= 0) & (delta <= win))[None] & (key_sub >= 0)[:, None, :]
    bias = -slopes[:, None, None] * (d * delta).astype(jnp.float32)[None]
    s = jnp.where(valid[None, :, None, None], s + bias, -jnp.inf)

    m = jnp.max(s, axis=-1, keepdims=True)
    p = jnp.exp(s - m)
    den = jnp.sum(p, axis=-1)
    lse = m[..., 0] + jnp.log(den)
    o = jnp.einsum("bnrhqk,bnkrhe->bnqrhe", p, vb.astype(jnp.float32))
    o = o / jnp.transpose(den, (0, 1, 4, 2, 3))[..., None]
    o = o.reshape(B, Lp, d, H, Dh)[:, :L].reshape(B, S, H, Dh)
    lse = jnp.transpose(lse, (0, 1, 4, 2, 3)).reshape(B, Lp, d, H)[:, :L].reshape(B, S, H)
    return o, lse

def mixture_of_dilations(q, k, v, slopes):
    outs, lses = [], []
    for window, dilation in ATTN_PATTERNS:
        o, lse = dilated_window_attention(q, k, v, window, dilation, slopes)
        outs.append(o)
        lses.append(lse)
    alpha = jax.nn.softmax(jnp.stack(lses, axis=0), axis=0)
    o = jnp.sum(alpha[..., None] * jnp.stack(outs, axis=0), axis=0)
    return o.astype(q.dtype)

def hybrid_mixer(h, w_in, b_merge, conv_w, w_out_conv, w_out_attn, w_o):
    B, S, _ = h.shape
    proj = jnp.einsum("bsd,dc->bsc", h, w_in)
    splits = np.cumsum([D_CONV] * 4 + [D_ATTN] * 4 + [D_MODEL])
    xc, bg, cg, zc, q, k, v, za, g_conv, g_attn = jnp.split(proj, splits, axis=-1)

    c = causal_depthwise_conv(cg * xc, conv_w)
    y_conv = jnp.einsum("bsc,cd->bsd", jax.nn.silu(zc) * bg * c, w_out_conv)

    shp = (B, S, N_HEADS, HEAD_DIM)
    o = mixture_of_dilations(q.reshape(shp), k.reshape(shp), v.reshape(shp),
                             alibi_slopes(N_HEADS)).reshape(B, S, D_ATTN)
    y_attn = jnp.einsum("bsc,cd->bsd", jax.nn.silu(za) * o, w_out_attn)

    g_conv = jax.nn.sigmoid(g_conv + b_merge[:D_MODEL])
    g_attn = jax.nn.sigmoid(g_attn + b_merge[D_MODEL:])
    merged = g_conv * y_conv + g_attn * y_attn
    return jnp.einsum("bsd,de->bse", merged, w_o)

def second_inputs(seed: int = 0) -> dict:
    key = jax.random.key(seed)
    ks = jax.random.split(key, 10)
    f32 = jnp.float32
    x = jax.random.normal(ks[0], (BATCH, SEQ, D_MODEL), f32)
    norm_g = 1.0 + 0.02 * jax.random.normal(ks[1], (DEPTH_2, D_MODEL), f32)
    w_in = jax.random.normal(ks[2], (DEPTH_2, D_MODEL, IN_COLS), f32) * D_MODEL ** -0.5
    b_merge = 0.01 * jax.random.normal(ks[3], (DEPTH_2, 2 * D_MODEL), f32)
    conv_w = jax.random.normal(ks[4], (DEPTH_2, CONV_WIDTH, D_CONV), f32) * CONV_WIDTH ** -0.5
    w_out_conv = jax.random.normal(ks[5], (DEPTH_2, D_CONV, D_MODEL), f32) * D_CONV ** -0.5
    w_out_attn = jax.random.normal(ks[6], (DEPTH_2, D_ATTN, D_MODEL), f32) * D_ATTN ** -0.5
    w_o = jax.random.normal(ks[7], (DEPTH_2, D_MODEL, D_MODEL), f32) * D_MODEL ** -0.5
    final_g = 1.0 + 0.02 * jax.random.normal(ks[8], (D_MODEL,), f32)
    return {"x": x, "norm_g": norm_g, "w_in": w_in, "b_merge": b_merge,
            "conv_w": conv_w, "w_out_conv": w_out_conv, "w_out_attn": w_out_attn,
            "w_o": w_o, "final_g": final_g}

def second_block(x, norm_g, w_in, b_merge, conv_w, w_out_conv, w_out_attn, w_o, final_g):
    h = x
    for layer in range(DEPTH_2):
        u = rms_norm_2(h, norm_g[layer])
        h = h + hybrid_mixer(u, w_in[layer], b_merge[layer], conv_w[layer],
                             w_out_conv[layer], w_out_attn[layer], w_o[layer])
    return rms_norm_2(h, final_g)


def setup_inputs(seed=0):
    out = dict(first_inputs(seed))
    for name, value in second_inputs(seed + 1).items():
        if name != "x":
            out[name + "_2"] = value
    return out


def reference(
    x, p, norm_g, w_ffn_in, w_ffn_out, w_ple_proj, w_ple_gate, mlstm_w_in, mlstm_b_gates,
    mlstm_head_norm, mlstm_w_out, kv_norm, w_kv, diff_w_q, diff_lambda, diff_subln, diff_w_out,
    norm_g_2, w_in_2, b_merge_2, conv_w_2, w_out_conv_2, w_out_attn_2, w_o_2, final_g_2,
):
    x = first_block(
        x, p, norm_g, w_ffn_in, w_ffn_out, w_ple_proj, w_ple_gate, mlstm_w_in, mlstm_b_gates,
        mlstm_head_norm, mlstm_w_out, kv_norm, w_kv, diff_w_q, diff_lambda, diff_subln,
        diff_w_out,
    )
    return second_block(
        x, norm_g_2, w_in_2, b_merge_2, conv_w_2, w_out_conv_2, w_out_attn_2, w_o_2, final_g_2,
    )


_drawn_inputs = setup_inputs


def setup_inputs(seed=0):
    import zlib

    import numpy as np

    out = dict(_drawn_inputs(seed))
    spreads = {}
    factors = {'norm_g_2': 8.0, 'b_merge_2': 42.401, 'final_g_2': 7.35, 'w_out_attn_2': 3.569}
    for name, (base, spread) in spreads.items():
        noise = np.random.default_rng([zlib.crc32(name.encode()), seed]).standard_normal(out[name].shape)
        drawn = base * np.exp(spread * noise) if base else spread * noise
        out[name] = jnp.asarray(drawn.astype(out[name].dtype))
    for name, factor in factors.items():
        out[name] = (out[name] * factor).astype(out[name].dtype)
    return out
```

```python
import math
from contextlib import ExitStack

import numpy as np

import concourse.bass as bass
from concourse import mybir

F32 = mybir.dt.float32
F32R = mybir.dt.float32r
BF16 = mybir.dt.bfloat16
I32 = mybir.dt.int32
ALU = mybir.AluOpType
ACT = mybir.ActivationFunctionType
AX = mybir.AxisListType.X

P = 128
TILES = 2
D = 1024
KT = D // P
FF = 2816
CH = 256
NIT = FF // CH
EPS = 1e-6
SLOT = 2048
NRAW = 3
NSPL = 6
AHEAD = 4
FAR = -1.0e30
MAGIC = 1597463007.0
ZS = -1.0 / 8192.0
MH, MDK, MDV = 4, 128, 256
DH = 8
LAM0 = 0.8 - 0.6 * math.exp(-0.3)
AH, AD = 16, 64
LCOLS = 3 * P

FFN_SLOTS = 3 * NIT
_N = dict(F0=FFN_SLOTS, MI=12, MO=4, F1=FFN_SLOTS, P0=5, KV=8, F2=FFN_SLOTS, DQ=4, DO=4,
          F3=FFN_SLOTS, P1=5, HI=40, HC=4, HA=4, HO=4)
S = {}
_at = 0
for _k, _v in _N.items():
    S[_k] = _at
    _at += _v
TOTAL = _at

T = {k: i for i, k in enumerate(("F0", "MI", "MO", "F1", "P0", "KV", "F2", "DQ", "DO", "F3", "P1",
                                 "HI", "HC", "HA", "HO"))}
PRE = dict(F0=0, MI=1, F1=2, P0=3, KV=4, F2=4, DQ=5, F3=6, P1=7, HI=8)
POST = dict(F0=0, MO=1, F1=2, P0=3, F2=4, DO=5, F3=6, P1=7)
FINAL_SUM = 17
FFN_NO = dict(F0=0, F1=1, F2=2, F3=3)
GAIN = dict(F0=0, MI=16, F1=32, P0=48, F2=64, DQ=80, F3=96, P1=112, KV=128, HI=136)
CONVW = 144
H_ORDER = [8, 9, 10, 11, 12, 13, 0, 4, 1, 5, 6, 2, 7, 3, 14, 15, 16, 17, 18, 19]

H_UNIT_NO = {0: 0, 1: 2, 2: 4, 3: 6, 7: 8, 9: 10, 11: 12, 13: 14}
H_PLACE = {0: 0, 1: 1, 2: 0, 3: 1, 6: 0, 7: 0, 8: 1, 9: 1, 10: 0, 11: 0, 12: 1, 13: 1, 14: 0, 15: 1}
H_S_FREE = {2: 1, 3: 3, 6: 5, 8: 7, 10: 9, 12: 11, 14: 13, 15: 15}
H_EVAC = {**{c: 2 * c + 2 for c in range(10)}, 11: 22, 13: 24}
H_SILU = {10: 2, 12: 4, 14: 6, 15: 8}


class At:

    def __init__(self, s, turn=None):
        self.s, self.turn = s, turn
        self.raw, self.spl = s % NRAW, s % NSPL

    def plus(self, n):
        return At(self.s + n, self.turn)

    def count(self, n=0):
        return self.s + 1 + n if self.turn is None else self.turn * NSPL + (self.s + 1 + n)

    def raw_count(self):
        base = 32 * (self.s // NRAW + 1)
        return base if self.turn is None else self.turn * (32 * NSPL // NRAW) + base


def psum_units(u):
    return u + 1 - (4 if u >= 4 * T["HC"] else 0)


def program(nc, A, out, stop=None):
    ctx = ExitStack()
    with ctx:
        def sb(name, shape, dt=F32):
            return ctx.enter_context(nc.sbuf_tensor(name, shape, dt))

        def sem(name):
            return ctx.enter_context(nc.semaphore(name))

        w_raw = sb("w_raw", [P, NRAW, SLOT])
        w_hi = sb("w_hi", [P, NSPL, SLOT], F32R)
        w_lo = sb("w_lo", [P, NSPL, SLOT], F32R)
        xT_hi = sb("xT_hi", [P, KT, TILES * P], F32R)
        xT_lo = sb("xT_lo", [P, KT, TILES * P], F32R)
        hT_hi = sb("hT_hi", [P, 2, TILES * P], F32R)
        hT_lo = sb("hT_lo", [P, 2, TILES * P], F32R)
        pT_hi = sb("pT_hi", [P, 2, TILES * P], F32R)
        pT_lo = sb("pT_lo", [P, 2, TILES * P], F32R)
        x = sb("x_res", [P, TILES, D])
        scaled = sb("scaled", [P, 2, 512])
        squares = sb("squares", [P, D], BF16)
        ident = sb("ident", [P, P])
        causal = sb("causal", [P, LCOLS])
        upto = sb("upto", [P, P])
        ones = sb("ones", [P, P])
        last_row = sb("last_row", [P, P])
        gcol = sb("gcol", [P, 168])
        ssq = sb("ssq", [P, 40])
        meansq = sb("meansq", [P, 40])
        zed = sb("zed", [P, 40])
        nt_ = sb("nt_", [P, 16])
        rstd = sb("rstd", [P, 20])
        wg_raw = sb("wg_raw", [P, KT, 8])
        wg_hi = sb("wg_hi", [P, KT, 8], F32R)
        wg_lo = sb("wg_lo", [P, KT, 8], F32R)
        rel = sb("rel", [P, LCOLS])
        times = sb("times", [P, LCOLS])
        ARENA = 13856
        arena = sb("arena", [P, ARENA])

        def area(at, *shape):
            n = int(np.prod(shape))
            assert at + n <= ARENA, (at, shape)
            v = arena[:, at:at + n]
            if len(shape) == 2:
                v = v.rearrange("p (a b) -> p a b", a=shape[0])
            if len(shape) == 3:
                v = v.rearrange("p (a b c) -> p a b c", a=shape[0], b=shape[1])
            return v

        gain_bc = area(0, D)
        ytmp = area(1024, TILES, 512)
        sg = area(2048, TILES, CH)
        hs = area(2560, TILES, CH)
        gate_sb = area(3072, TILES, D)
        hb = area(5120, TILES, D)
        p_nat = area(5120, TILES, 256)
        kT = area(11776, 8, 256)
        v_sh = area(9728, TILES, D)
        kn = area(3072, TILES, D)
        qn = area(2048, TILES, D)
        qT = area(4096, 8, 256)
        sc_ = area(6144, 2, 768)
        dif = area(7680, 2, LCOLS)
        difT = area(8448, 2, LCOLS)
        lamv = area(9216, 256)
        lamp = area(9472, 8)
        subln = area(9500, P)
        dstat = area(9632, 2, 16)
        hstat = area(9664, 64)
        m_qn = area(2048, TILES, 512)
        m_kn = area(3072, TILES, 512)
        m_qT = area(4096, MH, 256)
        m_kT = area(5120, MH, 256)
        m_v = area(6144, TILES, D)
        m_sig = area(8192, TILES, D)
        m_h = area(10240, TILES, D)
        m_am = area(12288, TILES, 512)
        m_P = area(13312, 512)
        m_PT = area(3584, 512)
        m_C = area(2048, D)
        m_ksc = area(1280, 512)
        at = 1024
        m_g = area(at, TILES, 8)
        (m_e, m_l, m_lf, m_b, m_a, m_mx, m_negmx, m_last, m_lrow, m_exp0, m_exp1, m_den, m_rden, m_hssq, m_hmean,
         m_hz, m_prev, m_n, m_qn_den) = (area(at + 16 + 8 * i, 8 if i < 16 else 4) for i in range(19))
        m_diag = area(1280, 512)
        h_v = area(0, TILES, D)
        h_kT = area(2048, 8, 256)
        h_qT = area(4096, 8, 256)
        h_o = area(4096, 8, TILES, P)
        h_s = area(6144, 2, TILES, 512)
        h_uT = area(8192, 8, 256)
        h_zT = area(10240, 8, 256)
        h_sc = area(12288, 2, LCOLS)
        h_pT = area(13056, 2, LCOLS)
        h_mx = area(13824, 2, 4)
        h_den = area(13832, 4, 2)
        h_rden = area(13840, 4, 2)
        h_gc = area(0, TILES, D)
        h_ga = area(2048, TILES, D)
        h_bm = area(8192, 2 * D)
        h_m = area(6144, TILES, D)
        f_gain = area(8192, D)
        f_out = area(10240, TILES, D)
        H_UNITS = {0: h_qT[:, 0:4], 1: h_qT[:, 4:8], 2: h_kT[:, 0:4], 3: h_kT[:, 4:8], 7: h_uT[:, 0:4],
                   9: h_uT[:, 4:8], 11: None, 13: None}
        rows1 = area(8192, P)
        rows2 = area(8320, P)
        iota_i = arena[:, 8448:8448 + LCOLS].bitcast(I32)
        iand_i = arena[:, 8832:8832 + 2 * LCOLS].bitcast(I32)
        build = area(9600, 4, LCOLS)
        bg_bc = sb("bg_bc", [P, 8])

        acc = ctx.enter_context(nc.psum_tensor("acc", [P, TILES, D], F32))
        gu = ctx.enter_context(nc.psum_tensor("gu", [P, TILES, 512], F32))
        tb = ctx.enter_context(nc.psum_tensor("tb", [P, 2, 512], F32))

        raw_landed = [sem(f"raw_landed{i}") for i in range(NRAW)]
        hi_ready = sem("hi_ready")
        lo_ready = sem("lo_ready")
        tile0_used = sem("tile0_used")
        slot_used = sem("slot_used")
        t_in_psum = sem("t_in_psum")
        t_scaled = sem("t_scaled")
        t_hi_ready = sem("t_hi_ready")
        t_lo_ready = sem("t_lo_ready")
        sums_ready = sem("sums_ready")
        rstd_ready = sem("rstd_ready")
        x_ready = sem("x_ready")
        x_landed = sem("x_landed")
        dve_link = sem("dve_link")
        act_link = sem("act_link")
        silu_ready = sem("silu_ready")
        h_ready = sem("h_ready")
        ht_in_psum = sem("ht_in_psum")
        ht_hi_ready = sem("ht_hi_ready")
        ht_lo_ready = sem("ht_lo_ready")
        consts_ready = sem("consts_ready")
        tables_ready = sem("tables_ready")
        gain_landed = sem("gain_landed")
        rows_landed = sem("rows_landed")
        gcol_in_psum = sem("gcol_in_psum")
        gcol_ready = sem("gcol_ready")
        p_landed = sem("p_landed")
        pt_in_psum = sem("pt_in_psum")
        pt_hi_ready = sem("pt_hi_ready")
        pt_lo_ready = sem("pt_lo_ready")
        gate_ready = sem("gate_ready")
        hb_ready = sem("hb_ready")
        out_ready = sem("out_ready")
        out_landed = sem("out_landed")
        kv_copied = sem("kv_copied")
        kt_in_psum = sem("kt_in_psum")
        kt_ready = sem("kt_ready")

        def pair(c, t):
            return (gu[:, t, :], acc[:, t, 0:512], acc[:, t, 512:1024])[c % 3]

        def x_count(n, t, half):
            return 4 * n + 2 * t + half + 1

        def tok(t):
            return slice(t * P, (t + 1) * P)

        wg_split = sem("wg_split")
        m_gates_in_psum = sem("m_gates_in_psum")
        m_copied = sem("m_copied")
        m_o_gate = sem("m_o_gate")
        m_absf = sem("m_absf")
        m_softlog = sem("m_softlog")
        m_logf = sem("m_logf")
        m_cum = sem("m_cum")
        m_diag_ready = sem("m_diag_ready")
        m_spread = sem("m_spread")
        m_am_ready = sem("m_am_ready")
        m_last_rhs = sem("m_last_rhs")
        m_last_in_psum = sem("m_last_in_psum")
        m_exps = sem("m_exps")
        m_exped = sem("m_exped")
        m_w_ready = sem("m_w_ready")
        m_pl_in_psum = sem("m_pl_in_psum")
        m_pl_ready = sem("m_pl_ready")
        m_ksc_ready = sem("m_ksc_ready")
        m_state_in_psum = sem("m_state_in_psum")
        m_state_ready = sem("m_state_ready")
        m_inter_in_psum = sem("m_inter_in_psum")
        m_qn_den_ready = sem("m_qn_den_ready")
        m_scores_in_psum = sem("m_scores_in_psum")
        m_p_ready = sem("m_p_ready")
        m_pt_in_psum = sem("m_pt_in_psum")
        m_pt_ready = sem("m_pt_ready")
        m_num_in_psum = sem("m_num_in_psum")
        m_h_ready = sem("m_h_ready")
        m_hsums = sem("m_hsums")
        m_y_ready = sem("m_y_ready")
        d_landed = sem("d_landed")
        d_lam = sem("d_lam")
        d_lamexp = sem("d_lamexp")
        d_qn_ready = sem("d_qn_ready")
        d_pl_in_psum = sem("d_pl_in_psum")
        d_pl_ready = sem("d_pl_ready")
        d_scores = sem("d_scores")
        d_negmax = sem("d_negmax")
        d_exped = sem("d_exped")
        d_dif_ready = sem("d_dif_ready")
        d_dt_in_psum = sem("d_dt_in_psum")
        d_dt_ready = sem("d_dt_ready")
        d_o_in_psum = sem("d_o_in_psum")
        d_o_ready = sem("d_o_ready")
        d_y_ready = sem("d_y_ready")
        h_evac = sem("h_evac")
        h_pl_in_psum = sem("h_pl_in_psum")
        h_pl_ready = sem("h_pl_ready")
        h_scores = sem("h_scores")
        h_negmax = sem("h_negmax")
        h_exped = sem("h_exped")
        h_p_ready = sem("h_p_ready")
        h_pt_in_psum = sem("h_pt_in_psum")
        h_pt_ready = sem("h_pt_ready")
        h_pv_in_psum = sem("h_pv_in_psum")
        h_o_ready = sem("h_o_ready")
        h_silu = sem("h_silu")
        h_conv = sem("h_conv")
        h_z_ready = sem("h_z_ready")
        h_gated = sem("h_gated")
        h_bm_landed = sem("h_bm_landed")
        h_gpre = sem("h_gpre")
        h_sig = sem("h_sig")
        h_m_ready = sem("h_m_ready")
        f_gain_landed = sem("f_gain_landed")

        block = ctx.enter_context(nc.Block())

        @block.sync
        def _(sp):
            def load(slot, halves):
                if slot.turn is not None or slot.s >= NRAW:
                    sp.wait_ge(lo_ready, slot.count(-NRAW))
                for view, src in halves:
                    sp.dma_start(view, src).then_inc(raw_landed[slot.raw], 16)

            def ffn(name, w_in, w_out):
                up_src = w_in.rearrange("(k p) c -> p k c", p=P)
                down_src = w_out.rearrange("(f p) c -> p f c", p=P)

                def up(n, slot, half):
                    dst = w_raw[:, slot.raw, :].rearrange("p (k u c) -> p k u c", k=4, u=2)
                    load(slot, [(dst[:, :, u, :], up_src[:, 4 * half:4 * half + 4, bass.ds(n * CH + u * FF, CH)])
                                for u in range(2)])

                def down(n, slot):
                    dst = w_raw[:, slot.raw, :].rearrange("p (f c) -> p f c", f=2)
                    load(slot, [(dst[:, f:f + 1, :], down_src[:, bass.ds(n * 2 + f, 1), :]) for f in range(2)])

                s0 = S[name]
                up(0, At(s0), 0)
                up(0, At(s0 + 1), 1)
                for n in (1, 2):
                    up(n, At(s0 + 3 * n - 1), 0)
                    up(n, At(s0 + 3 * n), 1)
                    down(n - 1, At(s0 + 3 * n + 1))
                with sp.Fori(0, (NIT - 3) // 2) as i:
                    for d in (0, 1):
                        a = At(s0 + 8 + 3 * d, i)
                        up(i * 2 + (3 + d), a, 0)
                        up(i * 2 + (3 + d), a.plus(1), 1)
                        down(i * 2 + (2 + d), a.plus(2))
                down(NIT - 1, At(s0 + FFN_SLOTS - 1))

            def linear(s0, w, cols):
                src = w.rearrange("(k p) c -> p k c", p=P)
                for c, col in enumerate(cols):
                    for j in range(2):
                        slot = At(s0 + 2 * c + j)
                        dst = w_raw[:, slot.raw, :].rearrange("p (k c) -> p k c", k=4)
                        load(slot, [(dst[:, 2 * k:2 * k + 2, :],
                                     src[:, 4 * j + 2 * k:4 * j + 2 * k + 2, col:col + 512]) for k in range(2)])

            def ple(name, w_proj, w_gate):
                slot = At(S[name])
                dst = w_raw[:, slot.raw, :].rearrange("p (f c) -> p f c", f=2)
                src = w_proj.rearrange("(f p) c -> p f c", p=P)
                load(slot, [(dst[:, f, :], src[:, f, :]) for f in range(2)])
                linear(S[name] + 1, w_gate, (0, 512))

            both = (0, 512)
            ffn("F0", A["w_ffn_in"][0, 0], A["w_ffn_out"][0, 0])
            linear(S["MI"], A["mlstm_w_in"][0], [512 * c for c in range(6)])
            linear(S["MO"], A["mlstm_w_out"][0], both)
            ffn("F1", A["w_ffn_in"][0, 1], A["w_ffn_out"][0, 1])
            ple("P0", A["w_ple_proj"][0], A["w_ple_gate"][0])
            linear(S["KV"], A["w_kv"], [512 * c for c in range(4)])
            ffn("F2", A["w_ffn_in"][1, 0], A["w_ffn_out"][1, 0])
            linear(S["DQ"], A["diff_w_q"][0], both)
            linear(S["DO"], A["diff_w_out"][0], both)
            ffn("F3", A["w_ffn_in"][1, 1], A["w_ffn_out"][1, 1])
            ple("P1", A["w_ple_proj"][1], A["w_ple_gate"][1])
            linear(S["HI"], A["w_in_2"][0], [512 * c for c in H_ORDER])
            linear(S["HC"], A["w_out_conv_2"][0], both)
            linear(S["HA"], A["w_out_attn_2"][0], both)
            linear(S["HO"], A["w_o_2"][0], both)
            for t in range(TILES):
                sp.wait_ge(out_ready, t + 1)
                sp.dma_start(out[0, tok(t), :], f_out[:, t, :]).then_inc(out_landed, 16)
            sp.wait_ge(out_landed, 16 * TILES)

        @block.gpsimd
        def _(pool):
            pool.memset(ident[:], 0.0).then_inc(consts_ready, 1)
            pool.memset(causal[:], 0.0).then_inc(consts_ready, 1)
            pool.memset(upto[:], 1.0).then_inc(consts_ready, 1)
            pool.memset(ones[:], 1.0).then_inc(consts_ready, 1)
            pool.memset(last_row[:], 0.0).then_inc(consts_ready, 1)
            pool.iota(iota_i[:, 0:P], pattern=[[-1, P]], base=256, channel_multiplier=1).then_inc(consts_ready, 1)
            pool.iota(iota_i[:, P:LCOLS], pattern=[[-1, 2 * P]], base=256 + P,
                      channel_multiplier=1).then_inc(consts_ready, 1)
            pool.wait_ge(consts_ready, 7)
            pool.affine_select(out=ident[:], in_=ident[:], compare_op=ALU.not_equal, fill=1.0, base=0,
                               pattern=[[-1, P]], channel_multiplier=1).then_inc(consts_ready, 1)
            pool.affine_select(out=causal[:, 0:P], in_=causal[:, 0:P], compare_op=ALU.is_ge, fill=FAR, base=0,
                               pattern=[[-1, P]], channel_multiplier=1).then_inc(consts_ready, 1)
            pool.affine_select(out=causal[:, P:LCOLS], in_=causal[:, P:LCOLS], compare_op=ALU.is_ge, fill=FAR,
                               base=P, pattern=[[-1, 2 * P]], channel_multiplier=1).then_inc(consts_ready, 1)
            pool.affine_select(out=upto[:], in_=upto[:], compare_op=ALU.is_ge, fill=0.0, base=0,
                               pattern=[[1, P]], channel_multiplier=-1).then_inc(consts_ready, 1)
            pool.affine_select(out=last_row[:], in_=last_row[:], compare_op=ALU.not_equal, fill=1.0,
                               base=-(P - 1), pattern=[[0, P]], channel_multiplier=1).then_inc(consts_ready, 1)

            def subtract(slot):
                pool.wait_ge(hi_ready, slot.count())
                pool.tensor_tensor(w_lo[:, slot.spl, :], w_raw[:, slot.raw, :],
                                   w_hi[:, slot.spl, :].bitcast(F32), ALU.subtract).then_inc(lo_ready, 1)

            with pool.Fori(0, TOTAL // NSPL) as i:
                for j in range(NSPL):
                    subtract(At(j, i))
            for s in range(TOTAL - TOTAL % NSPL, TOTAL):
                subtract(At(s))

        @block.scalar
        def _(act):
            linked = [0]

            def link(ins):
                linked[0] += 1
                ins.then_inc(act_link, 1)
                act.wait_ge(act_link, linked[0])

            def round_hi(slot):
                act.wait_ge(raw_landed[slot.raw], slot.raw_count())
                if slot.turn is not None or slot.s >= NSPL:
                    act.wait_ge(slot_used, slot.count(-NSPL))
                nc.scalar.copy(w_hi[:, slot.spl, :], w_raw[:, slot.raw, :]).then_inc(hi_ready, 1)

            def ahead(slot):
                if slot.turn is not None or slot.s + AHEAD < TOTAL:
                    round_hi(slot.plus(AHEAD))

            def load_gain(row):
                act.dma_start(gain_bc, row.rearrange("(o d) -> o d", o=1).broadcast_to([P, D])
                              ).then_inc(gain_landed, 16)

            def sum_of(j, t, src):
                if 2 * j + t:
                    act.wait_ge(sums_ready, 2 * j + t)
                nc.scalar.activation(squares[:], src, ACT.Square,
                                     accum_out=ssq[:, 2 * j + t:2 * j + t + 1]).then_inc(sums_ready, 1)

            def pre_sums(name):
                m = PRE[name]
                for t in range(TILES):
                    if m == 0:
                        act.wait_ge(x_landed, 16)
                    else:
                        act.wait_ge(x_ready, x_count(m - 1, t, 1))
                    sum_of(2 * m, t, x[:, t, :])

            def t_hi(q):
                for u in range(4 * T[q], 4 * T[q] + 4):
                    t, half = u // 2 % 2, u % 2
                    act.wait_ge(t_scaled, psum_units(u))
                    nc.scalar.copy(xT_hi[:, 4 * half:4 * half + 4, tok(t)],
                                   scaled[:, u % 2, :].rearrange("p (k c) -> p k c", k=4)
                                   ).then_inc(t_hi_ready, 1)

            def pre(name):
                t_hi(name)
                if name not in ("F0", "F2"):
                    pre_sums(name)

            def post_sums(name, last_slot):
                n = POST[name]
                for t in range(TILES):
                    act.wait_ge((tile0_used, slot_used)[t], last_slot + 1)
                    sum_of(2 * n + 1, t, acc[:, t, :])

            def warm(func):
                link(nc.scalar.activation(squares[:, 0:1], ones[:, 0:1], func))

            def ffn(name):
                f, m, s0 = FFN_NO[name], PRE[name], S[name]
                pre(name)
                act.wait_ge(sums_ready, 4 * m + 2)
                warm(ACT.Silu)

                def iteration(n, turn, a, has_down):
                    b = a.plus(1)

                    def turns(per, v):
                        return v if turn is None else turn * per + v

                    ahead(a)
                    ahead(b)
                    for t in range(TILES):
                        act.wait_ge((tile0_used, slot_used)[t], b.count())
                        if n:
                            act.wait_ge(h_ready, turns(4, 2 * NIT * f + 2 * (n - 1) + t + 1))
                        elif t == 0:
                            act.wait_ge(rstd_ready, 2 * m + 2)
                        nc.scalar.activation(sg[:, t, :], gu[:, t, 0:CH], ACT.Silu,
                                             scale=rstd[:, 2 * m + t:2 * m + t + 1]).then_inc(silu_ready, 1)
                    if has_down:
                        ahead(a.plus(2))
                    act.wait_ge(ht_in_psum, turns(2, NIT * f + n + 1))
                    nc.scalar.copy(hT_hi[:], tb[:, 0, :].rearrange("p (k c) -> p k c", k=2)
                                   ).then_inc(ht_hi_ready, 1)

                iteration(0, None, At(s0), False)
                for n in (1, 2):
                    iteration(n, None, At(s0 + 3 * n - 1), True)
                with act.Fori(0, (NIT - 3) // 2) as i:
                    for d in (0, 1):
                        iteration(3 + d, i, At(s0 + 8 + 3 * d, i), True)
                ahead(At(s0 + FFN_SLOTS - 1))
                post_sums(name, s0 + FFN_SLOTS - 1)

            def p_hi(layer):
                act.wait_ge(pt_in_psum, layer + 1)
                nc.scalar.copy(pT_hi[:], (gu[:, 0, :], tb[:, 1, :])[layer].rearrange("p (k c) -> p k c", k=2)
                               ).then_inc(pt_hi_ready, 1)

            def ple(name, layer):
                m, s0 = PRE[name], S[name]
                pre(name)
                for j in range(5):
                    ahead(At(s0 + j))
                act.wait_ge(rstd_ready, 2 * m + 2)
                for c in range(2):
                    for t in range(TILES):
                        act.wait_ge((tile0_used, slot_used)[t], s0 + 1 + 2 * c + 2)
                        nc.scalar.activation(gate_sb[:, t, 512 * c:512 * c + 512], (gu, tb)[c][:, t, :],
                                             ACT.Sigmoid, scale=rstd[:, 2 * m + t:2 * m + t + 1]
                                             ).then_inc(gate_ready, 1)
                for t in range(TILES):
                    act.wait_ge(hb_ready, 2 * layer + t + 1)
                    sum_of(2 * POST[name] + 1, t, hb[:, t, :])

            def mlstm():
                m, s0 = PRE["MI"], S["MI"]
                pre("MI")
                act.wait_ge(sums_ready, 4 * m + 2)
                ahead(At(s0))
                ahead(At(s0 + 1))
                ahead(At(s0 + 2))
                act.wait_ge(m_absf, 1)
                link(nc.scalar.activation(m_e, m_e, ACT.Exp, scale=-1.0))
                nc.scalar.activation(m_l, m_e, ACT.Ln, bias=1.0).then_inc(m_softlog, 1)
                for j in range(3, 8):
                    ahead(At(s0 + j))
                act.wait_ge(m_am_ready, 1)
                for h in range(MH):
                    ins = nc.scalar.activation(m_am[:, 0, tok(h)], m_am[:, 0, tok(h)], ACT.Exp,
                                               bias=m_negmx[:, h:h + 1])
                ins.then_inc(m_w_ready, 1)
                act.wait_ge(m_exps, 1)
                nc.scalar.activation(m_exp0, m_exp0, ACT.Exp).then_inc(m_exped, 1)
                ahead(At(s0 + 8))
                ahead(At(s0 + 9))
                act.wait_ge(m_am_ready, 2)
                for h in range(MH):
                    ins = nc.scalar.activation(m_am[:, 1, tok(h)], m_am[:, 1, tok(h)], ACT.Exp,
                                               bias=m_negmx[:, 4 + h:5 + h])
                ins.then_inc(m_w_ready, 1)
                act.wait_ge(m_exps, 2)
                nc.scalar.activation(m_exp1, m_exp1, ACT.Exp).then_inc(m_exped, 1)
                for w in range(4):
                    act.wait_ge(m_pl_in_psum, w + 1)
                    dst = (m_qT, m_kT)[w // 2][:, :, tok(w % 2)]
                    nc.scalar.copy(dst, tb[:, 0, :].rearrange("p (h c) -> p h c", h=MH)).then_inc(m_pl_ready, 1)
                ahead(At(s0 + 10))
                ahead(At(s0 + 11))
                for c in (4, 5):
                    for t in range(TILES):
                        act.wait_ge((tile0_used, slot_used)[t], s0 + 2 * c + 2)
                        nc.scalar.activation(m_sig[:, t, 512 * (c - 4):512 * (c - 4) + 512], pair(c, t),
                                             ACT.Sigmoid, scale=rstd[:, 2 * m + t:2 * m + t + 1]
                                             ).then_inc(m_o_gate, 1)
                act.wait_ge(m_state_in_psum, 1)
                nc.scalar.copy(m_C.rearrange("p (a b) -> p a b", a=2), gu[:]).then_inc(m_state_ready, 1)
                for t in range(TILES):
                    act.wait_ge(m_pt_in_psum, t + 1)
                    if t:
                        act.wait_ge(m_num_in_psum, t)
                    nc.scalar.copy(m_PT, tb[:, t, :]).then_inc(m_pt_ready, 1)
                for t in range(TILES):
                    act.wait_ge(m_h_ready, t + 1)
                    for h in range(MH):
                        ins = nc.scalar.activation(squares[:, MDV * h:MDV * h + MDV],
                                                   m_h[:, t, MDV * h:MDV * h + MDV], ACT.Square,
                                                   accum_out=m_hssq[:, 4 * t + h:4 * t + h + 1])
                    ins.then_inc(m_hsums, 1)
                    act.wait_ge(m_hsums, t + 1)
                t_hi("MO")
                for j in range(4):
                    ahead(At(S["MO"] + j))
                act.wait_ge(m_y_ready, 2)
                load_gain(A["norm_g"][0, 3])
                post_sums("MO", S["MO"] + 3)

            def diff():
                s0 = S["DQ"]
                pre("DQ")
                act.wait_ge(sums_ready, 4 * PRE["DQ"] + 2)
                for j in range(4):
                    ahead(At(s0 + j))
                act.wait_ge(d_lam, 1)
                nc.scalar.activation(lamp[:, 2:4], lamp[:, 0:2], ACT.Exp).then_inc(d_lamexp, 1)
                for w in range(4):
                    act.wait_ge(d_pl_in_psum, w + 1)
                    nc.scalar.copy(qT[:, 4 * (w % 2):4 * (w % 2) + 4, tok(w // 2)],
                                   tb[:, w % 2, :].rearrange("p (k c) -> p k c", k=4)).then_inc(d_pl_ready, 1)
                for step in range(DH + 2):
                    h = step
                    if h < DH:
                        act.wait_ge(d_negmax, h + 1)
                        for t in range(TILES):
                            for a in range(2):
                                e = sc_[:, h % 2, LCOLS * a + P * t:LCOLS * a + P * t + P * (t + 1)]
                                i = 2 * t + a
                                ins = nc.scalar.activation(e, e, ACT.Exp, bias=dstat[:, h % 2, 4 + i:5 + i],
                                                           accum_out=dstat[:, h % 2, 8 + i:9 + i])
                        ins.then_inc(d_exped, 1)
                    h = step - 1
                    if 0 <= h < DH:
                        act.wait_ge(d_dt_in_psum, h + 1)
                        if h >= 2:
                            act.wait_ge(d_o_in_psum, h - 1)
                        nc.scalar.copy(difT[:, h % 2, :], acc[:, 0, 512 * (h % 2):512 * (h % 2) + LCOLS]
                                       ).then_inc(d_dt_ready, 1)
                    h = step - 2
                    if 0 <= h < DH:
                        act.wait_ge(d_o_in_psum, h + 1)
                        src = acc[:, 1, 512 * (h % 2):512 * (h % 2) + 2 * P].rearrange("p (t c) -> p t c", t=2)
                        nc.scalar.copy(qn[:, :, tok(h)], src)
                        if h:
                            act.wait_ge(d_o_ready, h)
                        for t in range(TILES):
                            ins = nc.scalar.activation(squares[:, tok(t)], src[:, t, :], ACT.Square,
                                                       accum_out=hstat[:, DH * t + h:DH * t + h + 1])
                        ins.then_inc(d_o_ready, 1)
                act.wait_ge(d_o_ready, DH)
                t_hi("DO")
                for j in range(4):
                    ahead(At(S["DO"] + j))
                post_sums("DO", S["DO"] + 3)

            def hybrid():
                m, s0 = PRE["HI"], S["HI"]
                pre("HI")
                act.wait_ge(rstd_ready, 2 * m + 2)

                def r(t):
                    return rstd[:, 2 * m + t:2 * m + t + 1]

                def step(k):
                    h = k
                    if h < AH:
                        act.wait_ge(h_negmax, h + 1)
                        at = 0
                        for t in range(TILES):
                            e = h_sc[:, h % 2, at:at + P * (t + 1)]
                            ins = nc.scalar.activation(e, e, ACT.Exp, bias=h_mx[:, h % 2, 2 + t:3 + t])
                            at += P * (t + 1)
                        ins.then_inc(h_exped, 1)
                    h = k - 2
                    if 0 <= h < AH:
                        act.wait_ge(h_pt_in_psum, h + 1)
                        if h >= 2:
                            act.wait_ge(h_pv_in_psum, h - 1)
                        nc.scalar.copy(h_pT[:, h % 2, :], tb[:, 0, 0:LCOLS]).then_inc(h_pt_ready, 1)

                def units(c):
                    dst = H_UNITS[c]
                    for t in range(TILES):
                        w = H_UNIT_NO[c] + t
                        act.wait_ge(h_pl_in_psum, w + 1)
                        nc.scalar.copy(dst[:, :, tok(t)], tb[:, 1, :].rearrange("p (k c) -> p k c", k=4)
                                       ).then_inc(h_pl_ready, 1)

                steps = 0
                for c in range(20):
                    for j in range(2):
                        ahead(At(s0 + 2 * c + j))
                        if c - 1 in H_UNITS and H_UNITS[c - 1] is not None and j == 0:
                            units(c - 1)
                        if c >= 5 and steps < AH + 3:
                            step(steps)
                            steps += 1
                    if c in (10, 12, 14, 15):
                        for t in range(TILES):
                            act.wait_ge((tile0_used, slot_used)[t], s0 + 2 * c + 2)
                            act.wait_ge(h_pl_in_psum, H_S_FREE[c] + t)
                            nc.scalar.activation(h_s[:, H_PLACE[c], t, :], acc[:, t, 512 * (c % 2):512 * (c % 2) + 512],
                                                 ACT.Silu, scale=r(t)).then_inc(h_silu, 1)
                    if c == 15:
                        act.wait_ge(h_conv, 1)
                        act.dma_start(h_bm, A["b_merge_2"].broadcast_to([P, 2 * D])).then_inc(h_bm_landed, 16)
                    if c in (17, 19):
                        for cc in (c - 1, c):
                            for t in range(TILES):
                                g = (h_gc, h_ga)[cc // 18][:, t, 512 * (cc % 2):512 * (cc % 2) + 512]
                                act.wait_ge(h_gpre, 2 * (cc - 16) + t + 1)
                                nc.scalar.activation(g, g, ACT.Sigmoid).then_inc(h_sig, 1)
                act.wait_ge(slot_used, S["HC"])
                act.wait_ge(h_z_ready, 4)
                for u in range(4):
                    t, half = u // 2, u % 2
                    nc.scalar.copy(xT_hi[:, 4 * half:4 * half + 4, tok(t)], h_zT[:, 4 * half:4 * half + 4, tok(t)]
                                   ).then_inc(t_hi_ready, 1)
                act.wait_ge(h_gpre, 8)
                act.dma_start(f_gain, A["final_g_2"].rearrange("(o d) -> o d", o=1).broadcast_to([P, D])
                              ).then_inc(f_gain_landed, 16)
                for j in range(4):
                    ahead(At(S["HC"] + j))
                t_hi("HA")
                for j in range(4):
                    ahead(At(S["HA"] + j))
                t_hi("HO")
                for t in range(TILES):
                    act.wait_ge(x_ready, x_count(8, t, 1))
                    sum_of(FINAL_SUM, t, x[:, t, :])

            act.dma_start(x[:], A["x"][0].rearrange("(t p) d -> p t d", p=P)).then_inc(x_landed, 16)
            act.dma_start(rows1, A["norm_g"].rearrange("l n (k c) -> (l n k) c", c=P)).then_inc(rows_landed, 16)
            act.dma_start(rows2[0:8], A["kv_norm"].rearrange("(k c) -> k c", c=P)).then_inc(rows_landed, 16)
            act.dma_start(rows2[8:16], A["norm_g_2"][0].rearrange("(k c) -> k c", c=P)).then_inc(rows_landed, 16)
            act.dma_start(rows2[16:40], A["conv_w_2"][0].rearrange("w (k c) -> (w k) c", c=P)
                          ).then_inc(rows_landed, 16)
            act.dma_start(p_nat, A["p"][0, 0].rearrange("(t p) c -> p t c", p=P)).then_inc(p_landed, 16)
            act.dma_start(wg_raw[:], A["mlstm_w_in"][0].rearrange("(k p) c -> p k c", p=P)[:, :, 3072:3080]
                          ).then_inc(rows_landed, 16)
            act.dma_start(bg_bc[:], A["mlstm_b_gates"].broadcast_to([P, 8])).then_inc(rows_landed, 16)
            load_gain(A["norm_g"][0, 1])
            act.wait_ge(consts_ready, 12)
            warm(ACT.Silu)
            pre_sums("F0")
            for s in range(AHEAD):
                round_hi(At(s))
            p_hi(0)
            act.wait_ge(rows_landed, 16 * 6)
            nc.scalar.copy(wg_hi[:], wg_raw[:]).then_inc(wg_split, 1)
            ffn("F0")
            act.wait_ge(x_ready, x_count(0, 1, 1))
            load_gain(A["mlstm_head_norm"][0].rearrange("h d -> (h d)"))
            mlstm()
            act.wait_ge(x_ready, x_count(1, 1, 1))
            load_gain(A["norm_g"][0, 5])
            ffn("F1")
            act.wait_ge(x_ready, x_count(2, 1, 1))
            load_gain(A["norm_g"][0, 7])
            ple("P0", 0)
            act.wait_ge(x_ready, x_count(3, 1, 1))
            load_gain(A["norm_g"][1, 1])
            act.dma_start(p_nat, A["p"][1, 0].rearrange("(t p) c -> p t c", p=P)).then_inc(p_landed, 16)
            pre("KV")
            for j in range(8):
                ahead(At(S["KV"] + j))
            p_hi(1)
            for w in range(4):
                act.wait_ge(kt_in_psum, w + 1)
                nc.scalar.copy(kT[:, 4 * (w % 2):4 * (w % 2) + 4, tok(w // 2)],
                               acc[:, w // 2, 512 * (w % 2):512 * (w % 2) + 512].rearrange("p (k c) -> p k c", k=4)
                               ).then_inc(kt_ready, 1)
            ffn("F2")
            act.wait_ge(x_ready, x_count(4, 1, 1))
            load_gain(A["norm_g"][1, 3])
            act.dma_start(lamv, A["diff_lambda"][0].rearrange("(o a) d -> o (a d)", o=1).broadcast_to([P, 256])
                          ).then_inc(d_landed, 16)
            act.dma_start(subln, A["diff_subln"].broadcast_to([P, P])).then_inc(d_landed, 16)
            diff()
            act.wait_ge(x_ready, x_count(5, 1, 1))
            load_gain(A["norm_g"][1, 5])
            ffn("F3")
            act.wait_ge(x_ready, x_count(6, 1, 1))
            load_gain(A["norm_g"][1, 7])
            ple("P1", 1)
            hybrid()

        @block.vector
        def _(dve):
            linked = [0]

            def link(ins):
                linked[0] += 1
                ins.then_inc(dve_link, 1)
                dve.wait_ge(dve_link, linked[0])

            v = nc.vector

            def rsqrt_steps(sums, mean, z, tmp, inv_n):
                link(v.tensor_scalar(mean, sums, inv_n, EPS, ALU.mult, ALU.add))
                link(v.tensor_scalar(z.bitcast(I32), mean.bitcast(I32), -0.5, MAGIC, ALU.mult, ALU.add))
                for c in (3.0, 12.0, 768.0):
                    if z.shape[1] == 1:
                        link(v.scalar_tensor_tensor(tmp, z, mean, z, ALU.mult, ALU.mult))
                    else:
                        link(v.tensor_tensor(tmp, z, mean, ALU.mult))
                        link(v.tensor_tensor(tmp, tmp, z, ALU.mult))
                    link(v.scalar_tensor_tensor(z, tmp, c, z, ALU.subtract, ALU.mult))

            def norm_steps(j, t):
                i = 2 * j + t
                dve.wait_ge(sums_ready, i + 1)
                rsqrt_steps(ssq[:, i:i + 1], meansq[:, i:i + 1], zed[:, i:i + 1], nt_[:, 0:1], 1.0 / D)

            def gain_of(q, half):
                g = GAIN[q] + 4 * half
                return gcol[:, g:g + 4].unsqueeze(2).broadcast_to([P, 4, P])

            def t_units(q):
                def scale(u):
                    dve.wait_ge(t_in_psum, psum_units(u))
                    if u >= 2:
                        dve.wait_ge(t_lo_ready, u - 1)
                    dst = scaled[:, u % 2, :]
                    if q in GAIN:
                        v.tensor_tensor(dst.rearrange("p (k c) -> p k c", k=4),
                                        tb[:, u % 2, :].rearrange("p (k c) -> p k c", k=4),
                                        gain_of(q, u % 2), ALU.mult).then_inc(t_scaled, 1)
                    else:
                        v.tensor_copy(dst, tb[:, u % 2, :]).then_inc(t_scaled, 1)

                def low(u):
                    t, half = u // 2 % 2, u % 2
                    dve.wait_ge(t_hi_ready, u + 1)
                    to = (slice(4 * half, 4 * half + 4), tok(t))
                    v.tensor_tensor(xT_lo[:, to[0], to[1]], scaled[:, u % 2, :].rearrange("p (k c) -> p k c", k=4),
                                    xT_hi[:, to[0], to[1]].bitcast(F32), ALU.subtract).then_inc(t_lo_ready, 1)

                u0 = 4 * T[q]
                scale(u0)
                for u in range(u0, u0 + 3):
                    scale(u + 1)
                    low(u)
                low(u0 + 3)

            def pre(name):
                t_units(name)
                if name == "F2":
                    return
                m = PRE[name]
                for t in range(TILES):
                    norm_steps(2 * m, t)
                    i = 4 * m + t
                    v.tensor_scalar(rstd[:, 2 * m + t:2 * m + t + 1], zed[:, i:i + 1], ZS, None, ALU.mult
                                    ).then_inc(rstd_ready, 1)

            def post(name, gain_no, weight, src):
                n = POST[name]
                dve.wait_ge(gain_landed, 16 * gain_no)
                for t in range(TILES):
                    norm_steps(2 * n + 1, t)
                    i = 2 * (2 * n + 1) + t
                    for half in range(2):
                        cols = slice(512 * half, 512 * half + 512)
                        ins = v.scalar_tensor_tensor(ytmp[:, half, :], src[:, t, cols], zed[:, i:i + 1],
                                                     gain_bc[:, cols], ALU.mult, ALU.mult)
                    link(ins)
                    for half in range(2):
                        cols = slice(512 * half, 512 * half + 512)
                        v.scalar_tensor_tensor(x[:, t, cols], ytmp[:, half, :], weight * ZS, x[:, t, cols],
                                               ALU.mult, ALU.add).then_inc(x_ready, 1)

            def ffn(name, gain_no):
                f, m, s0 = FFN_NO[name], PRE[name], S[name]
                if name != "F0":
                    pre(name)
                if name != "F2":
                    dve.wait_ge(rstd_ready, 2 * m + 2)

                def iteration(n, turn):
                    def turns(per, c):
                        return c if turn is None else turn * per + c

                    for t in range(TILES):
                        dve.wait_ge(silu_ready, turns(4, 2 * NIT * f + 2 * n + t + 1))
                        if n and t == 0:
                            dve.wait_ge(ht_in_psum, turns(2, NIT * f + n))
                        v.scalar_tensor_tensor(hs[:, t, :], gu[:, t, CH:2 * CH], rstd[:, 2 * m + t:2 * m + t + 1],
                                               sg[:, t, :], ALU.mult, ALU.mult).then_inc(h_ready, 1)
                    dve.wait_ge(ht_hi_ready, turns(2, NIT * f + n + 1))
                    v.tensor_tensor(hT_lo[:], tb[:, 0, :].rearrange("p (k c) -> p k c", k=2),
                                    hT_hi[:].bitcast(F32), ALU.subtract).then_inc(ht_lo_ready, 1)

                for n in range(3):
                    iteration(n, None)
                with dve.Fori(0, (NIT - 3) // 2) as i:
                    for d in (0, 1):
                        iteration(3 + d, i)
                post(name, gain_no, 0.5, acc)

            def p_lo(layer):
                dve.wait_ge(pt_hi_ready, layer + 1)
                v.tensor_tensor(pT_lo[:], (gu[:, 0, :], tb[:, 1, :])[layer].rearrange("p (k c) -> p k c", k=2),
                                pT_hi[:].bitcast(F32), ALU.subtract).then_inc(pt_lo_ready, 1)

            def ple(name, layer, gain_no):
                pre(name)
                for t in range(TILES):
                    dve.wait_ge(gate_ready, 4 * layer + 2 + t + 1)
                    v.tensor_tensor(hb[:, t, :], acc[:, t, :], gate_sb[:, t, :], ALU.mult).then_inc(hb_ready, 1)
                post(name, gain_no, 1.0, hb)

            def mlstm():
                m, s0 = PRE["MI"], S["MI"]
                pre("MI")
                dve.wait_ge(rstd_ready, 2 * m + 2)

                def r(t):
                    return rstd[:, 2 * m + t:2 * m + t + 1]

                def take(c):
                    for t in range(TILES):
                        dve.wait_ge((tile0_used, slot_used)[t], s0 + 2 * c + 2)
                        dst = (m_qn[:, t, :], m_kn[:, t, :], m_v[:, t, 0:512], m_v[:, t, 512:1024])[c]
                        if c == 1:
                            v.tensor_scalar(dst, pair(c, t), r(t), float(MDK) ** -0.5, ALU.mult, ALU.mult
                                            ).then_inc(m_copied, 1)
                        else:
                            v.tensor_scalar(dst, pair(c, t), r(t), None, ALU.mult).then_inc(m_copied, 1)

                take(0)
                dve.wait_ge(m_gates_in_psum, 1)
                for t in range(TILES):
                    ins = v.scalar_tensor_tensor(m_g[:, t, :], tb[:, 1, 8 * t:8 * t + 8], r(t), bg_bc[:],
                                                 ALU.mult, ALU.add)
                link(ins)
                li, f = m_g[:, :, 0:MH], m_g[:, :, MH:2 * MH]
                v.scalar_tensor_tensor(m_e.rearrange("p (t h) -> p t h", t=2), f, -1.0, f, ALU.mult, ALU.max).then_inc(m_absf, 1)
                take(1)
                dve.wait_ge(m_softlog, 1)
                v.scalar_tensor_tensor(m_lf.rearrange("p (t h) -> p t h", t=2), f, 0.0,
                                       m_l.rearrange("p (t h) -> p t h", t=2), ALU.min, ALU.subtract
                                       ).then_inc(m_logf, 1)
                dve.wait_ge(m_cum, 1)
                link(v.tensor_copy(m_b, tb[:, 1, 16:24]))
                link(v.tensor_tensor(m_a.rearrange("p (t h) -> p t h", t=2), li,
                                     m_b.rearrange("p (t h) -> p t h", t=2), ALU.subtract))

                def diag(t):
                    v.tensor_tensor(m_diag.rearrange("p (h c) -> p h c", h=MH),
                                    ident[:].unsqueeze(1).broadcast_to([P, MH, P]),
                                    m_a[:, 4 * t:4 * t + 4].unsqueeze(2).broadcast_to([P, MH, P]),
                                    ALU.mult).then_inc(m_diag_ready, 1)

                def causal_max(t):
                    dve.wait_ge(m_spread, t + 1)
                    link(v.tensor_tensor(m_am[:, t, :].rearrange("p (h c) -> p h c", h=MH),
                                         tb[:, 0, :].rearrange("p (h c) -> p h c", h=MH),
                                         causal[:, 0:P].unsqueeze(1).broadcast_to([P, MH, P]), ALU.add))
                    link(v.tensor_reduce(m_mx[:, 4 * t:4 * t + 4],
                                         m_am[:, t, :].rearrange("p (h c) -> p h c", h=MH), AX, ALU.max))

                diag(0)
                take(2)
                causal_max(0)
                v.tensor_scalar(m_negmx[:, 0:4], m_mx[:, 0:4], -1.0, None, ALU.mult).then_inc(m_am_ready, 1)
                link(v.tensor_copy(m_last[:, 0:4], m_b[:, 0:4]))
                v.tensor_copy(m_last[:, 4:8], m_mx[:, 0:4]).then_inc(m_last_rhs, 1)
                diag(1)
                take(3)
                dve.wait_ge(m_last_in_psum, 1)
                link(v.tensor_copy(m_lrow, tb[:, 1, 24:32]))
                link(v.tensor_tensor(m_prev, m_lrow[:, 0:4], m_lrow[:, 4:8], ALU.add))
                link(v.scalar_tensor_tensor(m_exp0[:, 0:4], m_b[:, 0:4], -1.0, m_mx[:, 0:4], ALU.mult, ALU.subtract))
                v.tensor_tensor(m_exp0[:, 4:8], m_a[:, 0:4], m_lrow[:, 4:8], ALU.subtract).then_inc(m_exps, 1)
                causal_max(1)
                link(v.tensor_tensor(m_mx[:, 4:8], m_mx[:, 4:8], m_prev, ALU.max))
                v.tensor_scalar(m_negmx[:, 4:8], m_mx[:, 4:8], -1.0, None, ALU.mult).then_inc(m_am_ready, 1)
                link(v.scalar_tensor_tensor(m_exp1[:, 0:4], m_b[:, 4:8], -1.0, m_mx[:, 4:8], ALU.mult, ALU.subtract))
                v.tensor_tensor(m_exp1[:, 4:8], m_prev, m_mx[:, 4:8], ALU.subtract).then_inc(m_exps, 1)
                dve.wait_ge(m_exped, 2)
                v.tensor_tensor(m_ksc.rearrange("p (h c) -> p h c", h=MH),
                                m_kn[:, 0, :].rearrange("p (h c) -> p h c", h=MH),
                                m_exp0[:, 4:8].unsqueeze(2).broadcast_to([P, MH, P]), ALU.mult
                                ).then_inc(m_ksc_ready, 1)
                dve.wait_ge(m_state_in_psum, 2)
                v.tensor_copy(m_n, tb[:, 1, 32:36]).then_inc(m_state_ready, 1)
                dve.wait_ge(m_inter_in_psum, 1)
                v.tensor_tensor(m_qn_den, tb[:, 1, 36:40], m_exp1[:, 4:8], ALU.mult).then_inc(m_qn_den_ready, 1)
                for t in range(TILES):
                    dve.wait_ge(m_scores_in_psum, t + 1)
                    dve.wait_ge(m_w_ready, t + 1)
                    if t:
                        dve.wait_ge(m_pt_in_psum, t)
                    link(v.tensor_tensor(m_P, tb[:, t, :], m_am[:, t, :], ALU.mult))
                    v.tensor_reduce(m_den[:, 4 * t:4 * t + 4], m_P.rearrange("p (h c) -> p h c", h=MH), AX, ALU.add
                                    ).then_inc(m_p_ready, 1)
                dve.wait_ge(m_p_ready, 2)
                link(v.tensor_tensor(m_den[:, 4:8], m_den[:, 4:8], m_qn_den, ALU.add))
                link(v.scalar_tensor_tensor(m_den, m_den, -1.0, m_den, ALU.mult, ALU.max))
                link(v.tensor_tensor(m_den[:, 0:4], m_den[:, 0:4], m_exp0[:, 0:4], ALU.max))
                link(v.tensor_tensor(m_den[:, 4:8], m_den[:, 4:8], m_exp1[:, 0:4], ALU.max))
                link(v.reciprocal(m_rden, m_den))

                def heads(ap):
                    return ap.rearrange("p (h c) -> p h c", h=MH)

                def per_head(ap):
                    return ap.unsqueeze(2).broadcast_to([P, MH, MDV])

                dve.wait_ge(m_inter_in_psum, 2)
                link(v.tensor_tensor(heads(m_h[:, 1, :]), gu[:].rearrange("p a (b c) -> p (a b) c", b=2),
                                     per_head(m_exp1[:, 4:8]), ALU.mult))
                dve.wait_ge(m_num_in_psum, 1)
                v.tensor_tensor(heads(m_h[:, 0, :]), heads(acc[:, 0, :]), per_head(m_rden[:, 0:4]), ALU.mult
                                ).then_inc(m_h_ready, 1)
                dve.wait_ge(m_num_in_psum, 2)
                link(v.tensor_tensor(m_h[:, 1, :], acc[:, 1, :], m_h[:, 1, :], ALU.add))
                v.tensor_tensor(heads(m_h[:, 1, :]), heads(m_h[:, 1, :]), per_head(m_rden[:, 4:8]), ALU.mult
                                ).then_inc(m_h_ready, 1)
                dve.wait_ge(gain_landed, 16 * 2)
                dve.wait_ge(m_o_gate, 4)
                for t in range(TILES):
                    dve.wait_ge(m_hsums, t + 1)
                    c = slice(4 * t, 4 * t + 4)
                    rsqrt_steps(m_hssq[:, c], m_hmean[:, c], m_hz[:, c], nt_[:, 0:4], 1.0 / MDV)
                    link(v.tensor_scalar(m_hz[:, c], m_hz[:, c], ZS, None, ALU.mult))
                    for h in range(MH):
                        cols = slice(MDV * h, MDV * h + MDV)
                        ins = v.scalar_tensor_tensor(m_h[:, t, cols], m_h[:, t, cols],
                                                     m_hz[:, 4 * t + h:4 * t + h + 1], gain_bc[:, cols],
                                                     ALU.mult, ALU.mult)
                    link(ins)
                    v.tensor_tensor(m_h[:, t, :], m_h[:, t, :], m_sig[:, t, :], ALU.mult).then_inc(m_y_ready, 1)
                t_units("MO")
                post("MO", 3, 1.0, acc)

            def diff():
                m, s0 = PRE["DQ"], S["DQ"]
                pre("DQ")
                dve.wait_ge(d_landed, 32)
                for a in range(2):
                    link(v.tensor_tensor(lamv[:, 128 * a:128 * a + 64], lamv[:, 128 * a:128 * a + 64],
                                         lamv[:, 128 * a + 64:128 * a + 128], ALU.mult))
                v.tensor_reduce(lamp[:, 0:2], lamv.rearrange("p (a d) -> p a d", a=2)[:, :, 0:64], AX, ALU.add
                                ).then_inc(d_lam, 1)
                dve.wait_ge(d_lamexp, 1)
                link(v.tensor_tensor(lamp[:, 4:5], lamp[:, 3:4], lamp[:, 2:3], ALU.subtract))
                link(v.tensor_scalar(lamp[:, 5:6], lamp[:, 4:5], -LAM0, None, ALU.add))
                dve.wait_ge(rstd_ready, 2 * m + 2)
                for t in range(TILES):
                    dve.wait_ge((tile0_used, slot_used)[t], s0 + 4)
                    v.tensor_scalar(qn[:, t, :], acc[:, t, :], rstd[:, 2 * m + t:2 * m + t + 1], 0.125,
                                    ALU.mult, ALU.mult).then_inc(d_qn_ready, 1)
                for step in range(DH + 1):
                    h = step
                    if h < DH:
                        dve.wait_ge(d_scores, h + 1)
                        s, st = sc_[:, h % 2, :], dstat[:, h % 2, :]
                        for a in range(2):
                            ins = v.tensor_tensor(s[:, LCOLS * a:LCOLS * a + LCOLS], (tb, gu)[a][:, h % 2, 0:LCOLS],
                                                  causal[:], ALU.add)
                        link(ins)
                        maps = s.rearrange("p (a c) -> p a c", a=2)
                        v.tensor_reduce(st[:, 0:2], maps[:, :, 0:P], AX, ALU.max)
                        link(v.tensor_reduce(st[:, 2:4], maps[:, :, P:LCOLS], AX, ALU.max))
                        v.tensor_scalar(st[:, 4:8], st[:, 0:4], -1.0, None, ALU.mult).then_inc(d_negmax, 1)
                    h = step - 1
                    if h >= 0:
                        dve.wait_ge(d_exped, h + 1)
                        s, st = sc_[:, h % 2, :], dstat[:, h % 2, :]
                        link(v.reciprocal(st[:, 12:16], st[:, 8:12]))
                        rr = st[:, 12:16].rearrange("p (t a) -> p t a", t=2)
                        link(v.tensor_scalar(rr[:, :, 1:2], rr[:, :, 1:2], lamp[:, 5:6], None, ALU.mult))
                        if h >= 2:
                            dve.wait_ge(d_dt_in_psum, h - 1)
                        d = dif[:, h % 2, :]
                        v.tensor_scalar(d[:, 0:P], s[:, 0:P], st[:, 12:13], None, ALU.mult)
                        link(v.tensor_scalar(d[:, P:LCOLS], s[:, P:LCOLS], st[:, 14:15], None, ALU.mult))
                        v.scalar_tensor_tensor(d[:, 0:P], s[:, LCOLS:LCOLS + P], st[:, 13:14], d[:, 0:P],
                                               ALU.mult, ALU.add)
                        v.scalar_tensor_tensor(d[:, P:LCOLS], s[:, LCOLS + P:2 * LCOLS], st[:, 15:16], d[:, P:LCOLS],
                                               ALU.mult, ALU.add).then_inc(d_dif_ready, 1)
                dve.wait_ge(d_o_ready, DH)
                rsqrt_steps(hstat[:, 0:16], hstat[:, 16:32], hstat[:, 32:48], hstat[:, 48:64], 1.0 / P)
                link(v.tensor_scalar(hstat[:, 32:48], hstat[:, 32:48], ZS * (1.0 - LAM0), None, ALU.mult))
                for t in range(TILES):
                    y = qn[:, t, :].rearrange("p (h c) -> p h c", h=DH)
                    link(v.tensor_tensor(y, y, hstat[:, 32 + DH * t:32 + DH * t + DH].unsqueeze(2)
                                         .broadcast_to([P, DH, P]), ALU.mult))
                    v.tensor_tensor(y, y, subln.unsqueeze(1).broadcast_to([P, DH, P]), ALU.mult
                                    ).then_inc(d_y_ready, 1)
                t_units("DO")
                post("DO", 7, 1.0, acc)

            def hybrid():
                m, s0 = PRE["HI"], S["HI"]
                pre("HI")
                dve.wait_ge(rstd_ready, 2 * m + 2)

                def r(t):
                    return rstd[:, 2 * m + t:2 * m + t + 1]

                def bank(c, t):
                    return acc[:, t, 512 * (c % 2):512 * (c % 2) + 512]

                def step(k):
                    h = k
                    if h < AH:
                        dve.wait_ge(h_scores, h + 1)
                        if h >= 2:
                            dve.wait_ge(h_pt_in_psum, h - 1)
                        s, st = h_sc[:, h % 2, :], h_mx[:, h % 2, :]
                        link(v.scalar_tensor_tensor(s, rel[:], 2.0 ** (-8.0 * (h + 1) / AH), gu[:, h % 2, 0:LCOLS],
                                                    ALU.mult, ALU.add))
                        v.tensor_reduce(st[:, 0:1], s[:, 0:P], AX, ALU.max)
                        link(v.tensor_reduce(st[:, 1:2], s[:, P:LCOLS], AX, ALU.max))
                        v.tensor_scalar(st[:, 2:4], st[:, 0:2], -1.0, None, ALU.mult).then_inc(h_negmax, 1)
                    h = k - 1
                    if 0 <= h < AH:
                        dve.wait_ge(h_exped, h + 1)
                        s = h_sc[:, h % 2, :]
                        v.tensor_tensor_reduce(s[:, 0:P], s[:, 0:P], times[:, 0:P], 1.0, 0.0, ALU.mult, ALU.add,
                                               h_den[:, h % 4, 0:1])
                        link(v.tensor_tensor_reduce(s[:, P:LCOLS], s[:, P:LCOLS], times[:, P:LCOLS], 1.0, 0.0,
                                                    ALU.mult, ALU.add, h_den[:, h % 4, 1:2]))
                        v.reciprocal(h_rden[:, h % 4, :], h_den[:, h % 4, :]).then_inc(h_p_ready, 1)
                    h = k - 3
                    if 0 <= h < AH:
                        dve.wait_ge(h_pv_in_psum, h + 1)
                        at = AD * (h % 2)
                        v.tensor_tensor(h_o[:, h // 2, :, at:at + AD],
                                        gu[:, h % 2, LCOLS:512].rearrange("p (t c) -> p t c", t=2),
                                        h_rden[:, h % 4, :].unsqueeze(2).broadcast_to([P, TILES, AD]), ALU.mult
                                        ).then_inc(h_o_ready, 1)

                def take(c):
                    for t in range(TILES):
                        dve.wait_ge((tile0_used, slot_used)[t], s0 + 2 * c + 2)
                        if c in H_S_FREE:
                            dve.wait_ge(h_pl_in_psum, H_S_FREE[c] + t)
                        s = h_s[:, H_PLACE[c], t, :] if c in H_PLACE else None
                        if c < 2:
                            ins = v.tensor_scalar(s, bank(c, t), r(t), float(AD) ** -0.5, ALU.mult, ALU.mult)
                        elif c < 4 or c in (6, 8):
                            ins = v.tensor_scalar(s, bank(c, t), r(t), None, ALU.mult)
                        elif c < 6:
                            ins = v.tensor_scalar(h_v[:, t, 512 * (c - 4):512 * (c - 4) + 512], bank(c, t), r(t),
                                                  None, ALU.mult)
                        elif c in (7, 9):
                            ins = v.scalar_tensor_tensor(s, bank(c, t), r(t), s, ALU.mult, ALU.mult)
                        else:
                            dve.wait_ge(h_silu, H_SILU[c - 1] - 1 + t)
                            ins = v.scalar_tensor_tensor(s, bank(c, t), r(t), s, ALU.mult, ALU.mult)
                        ins.then_inc(h_evac, 1)

                def convolve():
                    dve.wait_ge(h_pl_ready, 12)
                    for k in range(8):
                        z, u = h_zT[:, k, :], h_uT[:, k, :]
                        w = [gcol[:, CONVW + 8 * i + k:CONVW + 8 * i + k + 1] for i in range(3)]
                        link(v.tensor_scalar(z, u, w[2], None, ALU.mult))
                        link(v.scalar_tensor_tensor(z[:, 1:256], u[:, 0:255], w[1], z[:, 1:256], ALU.mult, ALU.add))
                        ins = v.scalar_tensor_tensor(z[:, 2:256], u[:, 0:254], w[0], z[:, 2:256], ALU.mult, ALU.add)
                        if k == 7:
                            ins.then_inc(h_conv, 1)
                        else:
                            link(ins)

                def z_units(c):
                    half = (c - 11) // 2
                    dve.wait_ge(h_conv, 1)
                    for t in range(TILES):
                        dve.wait_ge(h_pl_in_psum, H_UNIT_NO[c] + t + 1)
                        z = h_zT[:, 4 * half:4 * half + 4, tok(t)]
                        v.tensor_tensor(z, tb[:, 1, :].rearrange("p (k c) -> p k c", k=4), z, ALU.mult
                                        ).then_inc(h_z_ready, 1)

                steps = 0
                for c in range(20):
                    for j in range(2):
                        if c - 1 in (11, 13) and j == 0:
                            z_units(c - 1)
                        if c >= 5 and steps < AH + 3:
                            step(steps)
                            steps += 1
                        if c == 10 and j == 1:
                            convolve()
                    if c < 10 or c in (11, 13):
                        take(c)
                    elif c in (14, 15):
                        dve.wait_ge(h_o_ready, AH)
                        for t in range(TILES):
                            dve.wait_ge(h_silu, H_SILU[c] - 1 + t)
                            o = h_o[:, 4 * (c - 14):4 * (c - 14) + 4, t, :]
                            v.tensor_tensor(o, o, h_s[:, H_PLACE[c], t, :].rearrange("p (k c) -> p k c", k=4),
                                            ALU.mult).then_inc(h_gated, 1)
                    elif c >= 16:
                        dve.wait_ge(h_bm_landed, 16)
                        for t in range(TILES):
                            dve.wait_ge((tile0_used, slot_used)[t], s0 + 2 * c + 2)
                            g = (h_gc, h_ga)[c // 18][:, t, 512 * (c % 2):512 * (c % 2) + 512]
                            v.scalar_tensor_tensor(g, bank(c, t), r(t), h_bm[:, 512 * (c - 16):512 * (c - 16) + 512],
                                                   ALU.mult, ALU.add).then_inc(h_gpre, 1)
                for u in range(4):
                    t, half = u // 2, u % 2
                    dve.wait_ge(t_hi_ready, 4 * T["HC"] + u + 1)
                    at = (slice(4 * half, 4 * half + 4), tok(t))
                    v.tensor_tensor(xT_lo[:, at[0], at[1]], h_zT[:, at[0], at[1]],
                                    xT_hi[:, at[0], at[1]].bitcast(F32), ALU.subtract).then_inc(t_lo_ready, 1)
                dve.wait_ge(h_sig, 8)
                for t in range(TILES):
                    dve.wait_ge((tile0_used, slot_used)[t], S["HC"] + 4)
                    ins = v.tensor_tensor(h_m[:, t, :], acc[:, t, :], h_gc[:, t, :], ALU.mult)
                link(ins)
                t_units("HA")
                for t in range(TILES):
                    dve.wait_ge((tile0_used, slot_used)[t], S["HA"] + 4)
                    for half, src in enumerate((gu, tb)):
                        cols = slice(512 * half, 512 * half + 512)
                        ins = v.tensor_tensor(h_ga[:, t, cols], src[:, t, :], h_ga[:, t, cols], ALU.mult)
                    link(ins)
                    v.tensor_tensor(h_m[:, t, :], h_m[:, t, :], h_ga[:, t, :], ALU.add).then_inc(h_m_ready, 1)
                t_units("HO")
                for t in range(TILES):
                    dve.wait_ge((tile0_used, slot_used)[t], S["HO"] + 4)
                    for half in range(2):
                        cols = slice(512 * half, 512 * half + 512)
                        v.tensor_tensor(x[:, t, cols], acc[:, t, cols], x[:, t, cols], ALU.add
                                        ).then_inc(x_ready, 1)
                dve.wait_ge(f_gain_landed, 16)
                for t in range(TILES):
                    norm_steps(FINAL_SUM, t)
                    i = 2 * FINAL_SUM + t
                    link(v.tensor_scalar(zed[:, i:i + 1], zed[:, i:i + 1], ZS, None, ALU.mult))
                    v.scalar_tensor_tensor(f_out[:, t, :], x[:, t, :], zed[:, i:i + 1], f_gain, ALU.mult, ALU.mult
                                           ).then_inc(out_ready, 1)

            dve.wait_ge(gcol_in_psum, 1)
            v.tensor_copy(gcol[:], tb[:, 0, 0:168]).then_inc(gcol_ready, 1)
            dve.wait_ge(gcol_ready, 1)
            p_lo(0)
            dve.wait_ge(wg_split, 1)
            v.tensor_tensor(wg_lo[:], wg_raw[:], wg_hi[:].bitcast(F32), ALU.subtract).then_inc(wg_split, 1)
            pre("F0")
            dve.wait_ge(consts_ready, 12)
            fdist, m4, m16, fwin = (build[:, i, :] for i in range(4))
            v.tensor_scalar(iand_i[:, 0:LCOLS], iota_i, 3, None, ALU.bitwise_and)
            v.tensor_scalar(iand_i[:, LCOLS:2 * LCOLS], iota_i, 15, None, ALU.bitwise_and)
            link(v.tensor_scalar(fdist, iota_i, -256.0, None, ALU.add))
            v.tensor_scalar(m4, iand_i[:, 0:LCOLS], 0.0, None, ALU.is_equal)
            v.tensor_scalar(m16, iand_i[:, LCOLS:2 * LCOLS], 0.0, None, ALU.is_equal)
            link(v.tensor_scalar(fwin, fdist, float(P), None, ALU.is_le))
            link(v.tensor_tensor(m4, m4, m16, ALU.add))
            link(v.tensor_tensor(m4, m4, fwin, ALU.add))
            link(v.tensor_scalar(m16, fdist, 0.0, None, ALU.is_ge))
            link(v.tensor_tensor(times[:], m4, m16, ALU.mult))
            link(v.tensor_scalar(m4, times[:], 0.5, None, ALU.is_le))
            link(v.tensor_scalar(m4, m4, FAR, None, ALU.mult))
            v.tensor_tensor(rel[:], m4, fdist, ALU.subtract).then_inc(tables_ready, 1)
            dve.wait_ge(tables_ready, 1)
            ffn("F0", 1)
            mlstm()
            ffn("F1", 4)
            ple("P0", 0, 5)
            pre("KV")
            dve.wait_ge(rstd_ready, 2 * PRE["KV"] + 2)
            for c in range(4):
                for t in range(TILES):
                    dve.wait_ge((tile0_used, slot_used)[t], S["KV"] + 2 * c + 2)
                    i = 2 * PRE["KV"] + t
                    v.tensor_scalar((kn, v_sh)[c // 2][:, t, 512 * (c % 2):512 * (c % 2) + 512], pair(c, t),
                                    rstd[:, i:i + 1], None, ALU.mult).then_inc(kv_copied, 1)
            p_lo(1)
            ffn("F2", 6)
            diff()
            ffn("F3", 8)
            ple("P1", 1, 9)
            hybrid()

        @block.tensor
        def _(pe):
            mm = nc.tensor.matmul

            def has_t(q, t, half):
                pe.wait_ge(t_lo_ready, 4 * T[q] + 2 * t + half + 1)

            def across(slot, half, outs, q=None):
                pe.wait_ge(lo_ready, slot.count())
                for t in range(TILES):
                    if q:
                        has_t(q, t, half)
                    for k in range(4):
                        wh = w_hi[:, slot.spl, 512 * k:512 * k + 512]
                        wl = w_lo[:, slot.spl, 512 * k:512 * k + 512]
                        xh, xl = xT_hi[:, 4 * half + k, tok(t)], xT_lo[:, 4 * half + k, tok(t)]
                        mm(outs[t], xh, wh, start=(half == 0 and k == 0), stop=False)
                        mm(outs[t], xh, wl, start=False, stop=False)
                        last = mm(outs[t], xl, wh, start=False, stop=(half == 1 and k == 3))
                    last.then_inc((tile0_used, slot_used)[t], 1)

            def down(slot, a_hi, a_lo, first, final):
                pe.wait_ge(lo_ready, slot.count())
                for t in range(TILES):
                    for k in range(2):
                        def w(ring, half):
                            return ring[:, slot.spl, D * k + 512 * half:D * k + 512 * half + 512]
                        st, sp_ = first and k == 0, final and k == 1
                        for half in range(2):
                            mm(acc[:, t, 512 * half:512 * half + 512], a_hi[:, k, tok(t)], w(w_hi, half),
                               start=st, stop=False)
                        for half in range(2):
                            mm(acc[:, t, 512 * half:512 * half + 512], a_hi[:, k, tok(t)], w(w_lo, half),
                               start=False, stop=False)
                        for half in range(2):
                            last = mm(acc[:, t, 512 * half:512 * half + 512], a_lo[:, k, tok(t)], w(w_hi, half),
                                      start=False, stop=sp_)
                    last.then_inc((tile0_used, slot_used)[t], 1)

            def t_units(q, src, wait):
                for u in range(4 * T[q], 4 * T[q] + 4):
                    t, half = u // 2 % 2, u % 2
                    wait(t, half)
                    if psum_units(u) > 2:
                        pe.wait_ge(t_scaled, psum_units(u) - 2)
                    for k in range(4):
                        ins = nc.tensor.transpose(tb[:, u % 2, tok(k)], src(t, 4 * half + k), ident[:])
                    ins.then_inc(t_in_psum, 1)

            def pre(name):
                n = PRE[name]

                def wait(t, half):
                    if n:
                        pe.wait_ge(x_ready, x_count(n - 1, t, half))
                    elif t + half == 0:
                        pe.wait_ge(x_landed, 16)
                        pe.wait_ge(gcol_ready, 1)
                t_units(name, lambda t, k: x[:, t, tok(k)], wait)

            def ffn(name):
                f, s0 = FFN_NO[name], S[name]
                pre(name)

                def gate_up(n, turn, a):
                    if n:
                        pe.wait_ge(h_ready, 2 * NIT * f + 2 * n if turn is None else turn * 4 + 2 * NIT * f + 2 * n)
                    across(a, 0, [gu[:, t, :] for t in range(TILES)], None if n else name)
                    across(a.plus(1), 1, [gu[:, t, :] for t in range(TILES)], None if n else name)

                def down_n(n, turn, slot):
                    pe.wait_ge(ht_lo_ready, NIT * f + n + 1 if turn is None else turn * 2 + NIT * f + n + 1)
                    down(slot, hT_hi, hT_lo, n == 0, n == NIT - 1)

                def turn_h(n, turn):
                    pe.wait_ge(h_ready, 2 * NIT * f + 2 * n + 2 if turn is None
                               else turn * 4 + 2 * NIT * f + 2 * n + 2)
                    for k in range(2):
                        for t in range(TILES):
                            ins = nc.tensor.transpose(tb[:, 0, 256 * k + P * t:256 * k + P * t + P],
                                                      hs[:, t, tok(k)], ident[:])
                    ins.then_inc(ht_in_psum, 1)

                gate_up(0, None, At(s0))
                turn_h(0, None)
                for n in (1, 2):
                    gate_up(n, None, At(s0 + 3 * n - 1))
                    down_n(n - 1, None, At(s0 + 3 * n + 1))
                    turn_h(n, None)
                with pe.Fori(0, (NIT - 3) // 2) as i:
                    for d in (0, 1):
                        gate_up(3 + d, i, At(s0 + 8 + 3 * d, i))
                        down_n(2 + d, i, At(s0 + 10 + 3 * d, i))
                        turn_h(3 + d, i)
                down_n(NIT - 1, None, At(s0 + FFN_SLOTS - 1))

            def linear(s0, q, outs, before=None):
                for c in range(2):
                    if before:
                        before(c)
                    for j in range(2):
                        across(At(s0 + 2 * c + j), j, [outs(c, t) for t in range(TILES)], None if c else q)

            def acc_outs(c, t):
                return acc[:, t, 512 * c:512 * c + 512]

            def turn_p(layer):
                pe.wait_ge(p_landed, 16 * (layer + 1))
                dst = (gu[:, 0, :], tb[:, 1, :])[layer]
                for k in range(2):
                    for t in range(TILES):
                        ins = nc.tensor.transpose(dst[:, 256 * k + P * t:256 * k + P * t + P],
                                                  p_nat[:, t, tok(k)], ident[:])
                ins.then_inc(pt_in_psum, 1)

            def ple(name, layer):
                pre(name)
                pe.wait_ge(pt_lo_ready, layer + 1)
                down(At(S[name]), pT_hi, pT_lo, True, True)
                linear(S[name] + 1, name, lambda c, t: (gu, tb)[c][:, t, :])

            def mlstm():
                s0 = S["MI"]
                pre("MI")

                def chunk(c):
                    if c >= 3:
                        pe.wait_ge(m_copied, 2 * (c - 3) + 2)
                    for j in range(2):
                        across(At(s0 + 2 * c + j), j, [pair(c, t) for t in range(TILES)], None if c else "MI")

                chunk(0)
                pe.wait_ge(wg_split, 2)
                for t in range(TILES):
                    o = tb[:, 1, 8 * t:8 * t + 8]
                    for k in range(KT):
                        mm(o, xT_hi[:, k, tok(t)], wg_hi[:, k, :], start=(k == 0), stop=False)
                        mm(o, xT_hi[:, k, tok(t)], wg_lo[:, k, :], start=False, stop=False)
                        ins = mm(o, xT_lo[:, k, tok(t)], wg_hi[:, k, :], start=False, stop=(k == KT - 1))
                ins.then_inc(m_gates_in_psum, 1)
                chunk(1)
                pe.wait_ge(m_logf, 1)
                mm(tb[:, 1, 16:24], upto[:], m_lf, start=True, stop=True).then_inc(m_cum, 1)
                chunk(2)

                def spread(t):
                    pe.wait_ge(m_diag_ready, t + 1)
                    if t:
                        pe.wait_ge(m_am_ready, t)
                    mm(tb[:, 0, :], ones[:], m_diag, start=True, stop=True).then_inc(m_spread, 1)

                spread(0)
                chunk(3)
                pe.wait_ge(m_last_rhs, 1)
                mm(tb[:, 1, 24:32], last_row[:], m_last, start=True, stop=True).then_inc(m_last_in_psum, 1)
                spread(1)
                chunk(4)
                pe.wait_ge(m_am_ready, 2)
                for w in range(4):
                    if w:
                        pe.wait_ge(m_pl_ready, w)
                    for h in range(MH):
                        ins = nc.tensor.transpose(tb[:, 0, tok(h)], (m_qn, m_kn)[w // 2][:, w % 2, tok(h)], ident[:])
                    ins.then_inc(m_pl_in_psum, 1)
                chunk(5)
                pe.wait_ge(m_ksc_ready, 1)
                pe.wait_ge(m_copied, 8)
                cs = gu[:].rearrange("p a (b c) -> p (a b) c", b=2)
                for h in range(MH):
                    ins = mm(cs[:, h, :], m_ksc[:, tok(h)], m_v[:, 0, MDV * h:MDV * h + MDV], start=True, stop=True)
                ins.then_inc(m_state_in_psum, 1)
                for h in range(MH):
                    ins = mm(tb[:, 1, 32 + h:33 + h], m_ksc[:, tok(h)], ones[:, 0:1], start=True, stop=True)
                ins.then_inc(m_state_in_psum, 1)
                pe.wait_ge(m_pl_ready, 4)
                pe.wait_ge(m_state_ready, 2)
                for h in range(MH):
                    ins = mm(tb[:, 1, 36 + h:37 + h], m_qT[:, h, tok(1)], m_n[:, h:h + 1], start=True, stop=True)
                ins.then_inc(m_inter_in_psum, 1)
                for h in range(MH):
                    ins = mm(cs[:, h, :], m_qT[:, h, tok(1)], m_C[:, MDV * h:MDV * h + MDV], start=True, stop=True)
                ins.then_inc(m_inter_in_psum, 1)
                pe.wait_ge(m_o_gate, 4)
                for t in range(TILES):
                    if t:
                        pe.wait_ge(m_qn_den_ready, 1)
                    for h in range(MH):
                        ins = mm(tb[:, t, tok(h)], m_qT[:, h, tok(t)], m_kT[:, h, tok(t)], start=True, stop=True)
                    ins.then_inc(m_scores_in_psum, 1)
                for t in range(TILES):
                    pe.wait_ge(m_p_ready, t + 1)
                    for h in range(MH):
                        ins = nc.tensor.transpose(tb[:, t, tok(h)], m_P[:, tok(h)], ident[:])
                    ins.then_inc(m_pt_in_psum, 1)
                    pe.wait_ge(m_pt_ready, t + 1)
                    for h in range(MH):
                        ins = mm(acc[:, t, MDV * h:MDV * h + MDV], m_PT[:, tok(h)],
                                 m_v[:, t, MDV * h:MDV * h + MDV], start=True, stop=True)
                    ins.then_inc(m_num_in_psum, 1)
                t_units("MO", lambda t, k: m_h[:, t, tok(k)], lambda t, half: pe.wait_ge(m_y_ready, t + 1))
                linear(S["MO"], "MO", acc_outs)

            def diff():
                pre("DQ")
                linear(S["DQ"], "DQ", acc_outs)
                has_t("DQ", 1, 1)
                for w in range(4):
                    pe.wait_ge(d_qn_ready, w // 2 + 1)
                    if w >= 2:
                        pe.wait_ge(d_pl_ready, w - 1)
                    for k in range(4):
                        ins = nc.tensor.transpose(tb[:, w % 2, tok(k)], qn[:, w // 2, tok(4 * (w % 2) + k)], ident[:])
                    ins.then_inc(d_pl_in_psum, 1)
                pe.wait_ge(d_pl_ready, 4)
                for step in range(DH + 2):
                    h = step
                    if h < DH:
                        if h >= 2:
                            pe.wait_ge(d_negmax, h - 1)
                        for t in range(TILES):
                            for a in range(2):
                                b = slice(64 * a, 64 * a + 64)
                                o = (tb, gu)[a][:, h % 2, P * t:P * t + P * (t + 1)]
                                ins = mm(o, qT[b, h, tok(t)], kT[b, h, 0:P * (t + 1)], start=True, stop=True)
                        ins.then_inc(d_scores, 1)
                    h = step - 1
                    if 0 <= h < DH:
                        pe.wait_ge(d_dif_ready, h + 1)
                        if h >= 2:
                            pe.wait_ge(d_dt_ready, h - 1)
                        for i in range(3):
                            ins = nc.tensor.transpose(acc[:, 0, 512 * (h % 2) + P * i:512 * (h % 2) + P * i + P],
                                                      dif[:, h % 2, tok(i)], ident[:])
                        ins.then_inc(d_dt_in_psum, 1)
                    h = step - 2
                    if 0 <= h < DH:
                        pe.wait_ge(d_dt_ready, h + 1)
                        if h >= 2:
                            pe.wait_ge(d_o_ready, h - 1)
                        o = acc[:, 1, 512 * (h % 2):512 * (h % 2) + 2 * P]
                        mm(o[:, 0:P], difT[:, h % 2, 0:P], v_sh[:, 0, tok(h)], start=True, stop=True)
                        mm(o[:, P:2 * P], difT[:, h % 2, P:2 * P], v_sh[:, 0, tok(h)], start=True, stop=False)
                        mm(o[:, P:2 * P], difT[:, h % 2, 2 * P:3 * P], v_sh[:, 1, tok(h)], start=False, stop=True
                           ).then_inc(d_o_in_psum, 1)
                t_units("DO", lambda t, k: qn[:, t, tok(k)], lambda t, half: pe.wait_ge(d_y_ready, t + 1))
                linear(S["DO"], "DO", acc_outs)

            def hybrid():
                s0 = S["HI"]
                pre("HI")

                def step(k):
                    h = k
                    if h < AH:
                        if h == 0:
                            pe.wait_ge(h_pl_ready, 8)
                        if h >= 2:
                            pe.wait_ge(h_negmax, h - 1)
                        if h >= 4:
                            pe.wait_ge(h_o_ready, h - 3)
                        b = slice(AD * (h % 2), AD * (h % 2) + AD)
                        for t in range(TILES):
                            ins = mm(gu[:, h % 2, P * t:P * t + P * (t + 1)], h_qT[b, h // 2, tok(t)],
                                     h_kT[b, h // 2, 0:P * (t + 1)], start=True, stop=True)
                        ins.then_inc(h_scores, 1)
                    h = k - 2
                    if 0 <= h < AH:
                        pe.wait_ge(h_p_ready, h + 1)
                        if h >= 1:
                            pe.wait_ge(h_pt_ready, h)
                        for i in range(3):
                            ins = nc.tensor.transpose(tb[:, 0, tok(i)], h_sc[:, h % 2, tok(i)], ident[:])
                        ins.then_inc(h_pt_in_psum, 1)
                    h = k - 3
                    if 0 <= h < AH:
                        pe.wait_ge(h_pt_ready, h + 1)
                        if h + 2 < AH:
                            pe.wait_ge(h_negmax, h + 3)
                        if h >= AH - 2:
                            pe.wait_ge(h_o_ready, h - 1)
                        o = gu[:, h % 2, LCOLS:512]
                        pt = h_pT[:, h % 2, :]
                        vc = slice(AD * h, AD * h + AD)
                        mm(o[:, 0:AD], pt[:, 0:P], h_v[:, 0, vc], start=True, stop=True)
                        mm(o[:, AD:2 * AD], pt[:, P:2 * P], h_v[:, 0, vc], start=True, stop=False)
                        mm(o[:, AD:2 * AD], pt[:, 2 * P:3 * P], h_v[:, 1, vc], start=False, stop=True
                           ).then_inc(h_pv_in_psum, 1)

                def units(c):
                    pe.wait_ge(h_evac, H_EVAC[c])
                    for t in range(TILES):
                        w = H_UNIT_NO[c] + t
                        if 0 < w <= 12:
                            pe.wait_ge(h_pl_ready, w)
                        elif w > 12:
                            pe.wait_ge(h_z_ready, w - 12)
                        for k in range(4):
                            ins = nc.tensor.transpose(tb[:, 1, tok(k)], h_s[:, H_PLACE[c], t, tok(k)], ident[:])
                        ins.then_inc(h_pl_in_psum, 1)

                steps = 0
                for c in range(20):
                    if c - 2 in H_EVAC:
                        pe.wait_ge(h_evac, H_EVAC[c - 2])
                    elif c - 2 in H_SILU:
                        pe.wait_ge(h_silu, H_SILU[c - 2])
                    elif c >= 18:
                        pe.wait_ge(h_gpre, 2 * (c - 18) + 2)
                    for j in range(2):
                        across(At(s0 + 2 * c + j), j, [acc[:, t, 512 * (c % 2):512 * (c % 2) + 512]
                                                       for t in range(TILES)], None if c else "HI")
                        if c - 1 in H_UNITS and j == 0:
                            units(c - 1)
                        if c >= 5 and steps < AH + 3:
                            step(steps)
                            steps += 1
                pe.wait_ge(h_gpre, 8)
                linear(S["HC"], "HC", acc_outs)
                t_units("HA", lambda t, k: h_o[:, k, t, :],
                        lambda t, half: pe.wait_ge(h_gated, 4))
                has_t("HA", 1, 1)
                linear(S["HA"], "HA", lambda c, t: (gu, tb)[c][:, t, :])
                t_units("HO", lambda t, k: h_m[:, t, tok(k)], lambda t, half: pe.wait_ge(h_m_ready, 2))
                linear(S["HO"], "HO", acc_outs)

            pe.wait_ge(consts_ready, 12)
            pe.wait_ge(rows_landed, 16 * 6)
            nc.tensor.transpose(tb[:, 0, 0:P], rows1, ident[:])
            nc.tensor.transpose(tb[:, 0, P:168], rows2[0:40], ident[0:40, 0:40]).then_inc(gcol_in_psum, 1)
            turn_p(0)
            pe.wait_ge(pt_lo_ready, 1)
            ffn("F0")
            mlstm()
            ffn("F1")
            ple("P0", 0)
            pre("KV")
            for c in range(4):
                if c == 3:
                    pe.wait_ge(kv_copied, 2)
                if c == 0:
                    pe.wait_ge(hb_ready, 2)
                for j in range(2):
                    across(At(S["KV"] + 2 * c + j), j, [pair(c, t) for t in range(TILES)], None if c else "KV")
            turn_p(1)
            pe.wait_ge(kv_copied, 8)
            for w in range(4):
                for k in range(4):
                    ins = nc.tensor.transpose(acc[:, w // 2, 512 * (w % 2) + P * k:512 * (w % 2) + P * k + P],
                                              kn[:, w // 2, tok(4 * (w % 2) + k)], ident[:])
                ins.then_inc(kt_in_psum, 1)
            pe.wait_ge(pt_lo_ready, 2)
            pe.wait_ge(kt_ready, 4)
            ffn("F2")
            diff()
            ffn("F3")
            ple("P1", 1)
            hybrid()


_INS = ["x", "p", "norm_g", "w_ffn_in", "w_ffn_out", "w_ple_proj", "w_ple_gate", "mlstm_w_in", "mlstm_b_gates",
        "mlstm_head_norm", "mlstm_w_out", "kv_norm", "w_kv", "diff_w_q", "diff_lambda", "diff_subln", "diff_w_out",
        "norm_g_2", "w_in_2", "b_merge_2", "conv_w_2", "w_out_conv_2", "w_out_attn_2", "w_o_2", "final_g_2"]


def kernel(**inputs):
    import numpy as _np
    import concourse.bacc as _bacc
    from concourse import mybir as _mybir
    from concourse.bass_utils import run_bass_kernel_spmd as _run

    nc = _bacc.Bacc("TRN2", target_bir_lowering=False, num_devices=1, dynamic_dma_scratch_size=1024)
    arrays, aps = {}, {}
    for name in _INS:
        a = _np.ascontiguousarray(inputs[name])
        arrays[f"in_{name}"] = a
        aps[name] = nc.dram_tensor(f"in_{name}", a.shape, _mybir.dt.from_np(a.dtype), kind="ExternalInput").ap()
    out = nc.dram_tensor("out_x", (1, 256, 1024), F32, kind="ExternalOutput").ap()
    program(nc, aps, out)
    r = _run(nc, [arrays], core_ids=[0])
    return r.results[0]["out_x"]
```

```python
import math
from contextlib import ExitStack

import numpy as np

import concourse.bass as bass
from concourse import mybir

F32 = mybir.dt.float32
F32R = mybir.dt.float32r
BF16 = mybir.dt.bfloat16
I32 = mybir.dt.int32
ALU = mybir.AluOpType
ACT = mybir.ActivationFunctionType
AX = mybir.AxisListType.X

P = 128
TILES = 2
D = 1024
KT = D // P
FF = 2816
CH = 256
NIT = FF // CH
EPS = 1e-6
SLOT = 2048
NRAW = 3
NSPL = 6
AHEAD = 4
FAR = -1.0e30
MAGIC = 1597463007.0
ZS = -1.0 / 8192.0
MH, MDK, MDV = 4, 128, 256
DH = 8
LAM0 = 0.8 - 0.6 * math.exp(-0.3)
AH, AD = 16, 64
LCOLS = 3 * P

FFN_SLOTS = 3 * NIT
_N = dict(F0=FFN_SLOTS, MI=12, MO=4, F1=FFN_SLOTS, P0=5, KV=8, F2=FFN_SLOTS, DQ=4, DO=4,
          F3=FFN_SLOTS, P1=5, HI=40, HC=4, HA=4, HO=4)
S = {}
_at = 0
for _k, _v in _N.items():
    S[_k] = _at
    _at += _v
TOTAL = _at

T = {k: i for i, k in enumerate(("F0", "MI", "MO", "F1", "P0", "KV", "F2", "DQ", "DO", "F3", "P1",
                                 "HI", "HC", "HA", "HO"))}
PRE = dict(F0=0, MI=1, F1=2, P0=3, KV=4, F2=4, DQ=5, F3=6, P1=7, HI=8)
POST = dict(F0=0, MO=1, F1=2, P0=3, F2=4, DO=5, F3=6, P1=7)
FINAL_SUM = 17
FFN_NO = dict(F0=0, F1=1, F2=2, F3=3)
GAIN = dict(F0=0, MI=16, F1=32, P0=48, F2=64, DQ=80, F3=96, P1=112, KV=128, HI=136)
CONVW = 144
H_ORDER = [8, 9, 10, 11, 12, 13, 0, 4, 1, 5, 6, 2, 7, 3, 14, 15, 16, 17, 18, 19]

H_UNIT_NO = {0: 0, 1: 2, 2: 4, 3: 6, 7: 8, 9: 10, 11: 12, 13: 14}
H_PLACE = {0: 0, 1: 1, 2: 0, 3: 1, 6: 0, 7: 0, 8: 1, 9: 1, 10: 0, 11: 0, 12: 1, 13: 1, 14: 0, 15: 1}
H_S_FREE = {2: 1, 3: 3, 6: 5, 8: 7, 10: 9, 12: 11, 14: 13, 15: 15}
H_UNITS_AT = {(2, 0): 0, (2, 1): 1, (3, 0): 2, (4, 0): 3, (8, 0): 7, (10, 0): 9, (12, 0): 11, (14, 0): 13}
H_EVAC = {**{c: 2 * c + 2 for c in range(10)}, 11: 22, 13: 24}
H_SILU = {10: 2, 12: 4, 14: 6, 15: 8}


class At:

    def __init__(self, s, turn=None):
        self.s, self.turn = s, turn
        self.raw, self.spl = s % NRAW, s % NSPL

    def plus(self, n):
        return At(self.s + n, self.turn)

    def count(self, n=0):
        return self.s + 1 + n if self.turn is None else self.turn * NSPL + (self.s + 1 + n)

    def raw_count(self):
        base = 32 * (self.s // NRAW + 1)
        return base if self.turn is None else self.turn * (32 * NSPL // NRAW) + base


def psum_units(u):
    return u + 1 - (4 if u >= 4 * T["HC"] else 0)


def program(nc, A, out):
    ctx = ExitStack()
    with ctx:
        def sb(name, shape, dt=F32):
            return ctx.enter_context(nc.sbuf_tensor(name, shape, dt))

        def sem(name):
            return ctx.enter_context(nc.semaphore(name))

        w_raw = sb("w_raw", [P, NRAW, SLOT])
        w_hi = sb("w_hi", [P, NSPL, SLOT], F32R)
        w_lo = sb("w_lo", [P, NSPL, SLOT], F32R)
        xT_hi = sb("xT_hi", [P, KT, TILES * P], F32R)
        xT_lo = sb("xT_lo", [P, KT, TILES * P], F32R)
        hT_hi = sb("hT_hi", [P, 2, TILES * P], F32R)
        hT_lo = sb("hT_lo", [P, 2, TILES * P], F32R)
        pT_hi = sb("pT_hi", [P, 2, TILES * P], F32R)
        pT_lo = sb("pT_lo", [P, 2, TILES * P], F32R)
        x = sb("x_res", [P, TILES, D])
        scaled = sb("scaled", [P, 2, 512])
        squares = sb("squares", [P, D], BF16)
        ident = sb("ident", [P, P])
        causal = sb("causal", [P, LCOLS])
        upto = sb("upto", [P, P])
        ones = sb("ones", [P, P])
        last_row = sb("last_row", [P, P])
        gcol = sb("gcol", [P, 168])
        ssq = sb("ssq", [P, 40])
        meansq = sb("meansq", [P, 40])
        zed = sb("zed", [P, 40])
        nt_ = sb("nt_", [P, 16])
        rstd = sb("rstd", [P, 20])
        wg_raw = sb("wg_raw", [P, KT, 8])
        wg_hi = sb("wg_hi", [P, KT, 8], F32R)
        wg_lo = sb("wg_lo", [P, KT, 8], F32R)
        rel = sb("rel", [P, LCOLS])
        times = sb("times", [P, LCOLS])
        ARENA = 13856
        arena = sb("arena", [P, ARENA])

        def area(at, *shape):
            n = int(np.prod(shape))
            assert at + n <= ARENA, (at, shape)
            v = arena[:, at:at + n]
            if len(shape) == 2:
                v = v.rearrange("p (a b) -> p a b", a=shape[0])
            if len(shape) == 3:
                v = v.rearrange("p (a b c) -> p a b c", a=shape[0], b=shape[1])
            return v

        gain_bc = area(0, D)
        ytmp = area(1024, TILES, 512)
        sg = area(2048, TILES, CH)
        hs = area(2560, TILES, CH)
        gate_sb = area(3072, TILES, D)
        hb = area(5120, TILES, D)
        p_nat = area(5120, TILES, 256)
        kT = area(11776, 8, 256)
        v_sh = area(9728, TILES, D)
        kn = area(3072, TILES, D)
        qn = area(2048, TILES, D)
        qT = area(4096, 8, 256)
        sc_ = area(6144, 2, 768)
        dif = area(7680, 2, LCOLS)
        difT = area(8448, 2, LCOLS)
        lamv = area(9216, 256)
        lamp = area(9472, 8)
        subln = area(9500, P)
        dstat = area(9632, 2, 16)
        hstat = area(9664, 64)
        m_qn = area(2048, TILES, 512)
        m_kn = area(3072, TILES, 512)
        m_qT = area(4096, MH, 256)
        m_kT = area(5120, MH, 256)
        m_v = area(6144, TILES, D)
        m_sig = area(8192, TILES, D)
        m_h = area(10240, TILES, D)
        m_am = area(12288, TILES, 512)
        m_P = area(13312, 512)
        m_PT = area(3584, 512)
        m_C = area(2048, D)
        m_ksc = area(1280, 512)
        at = 1024
        m_g = area(at, TILES, 8)
        (m_e, m_l, m_lf, m_b, m_a, m_mx, m_negmx, m_last, m_lrow, m_exp0, m_exp1, m_den, m_rden, m_hssq, m_hmean,
         m_hz, m_prev, m_n, m_qn_den) = (area(at + 16 + 8 * i, 8 if i < 16 else 4) for i in range(19))
        m_diag = area(1280, 512)
        h_v = area(0, TILES, D)
        h_kT = area(2048, 8, 256)
        h_qT = area(4096, 8, 256)
        h_o = area(4096, 8, TILES, P)
        h_s = area(6144, 2, TILES, 512)
        h_uT = area(8192, 8, 256)
        h_zT = area(10240, 8, 256)
        h_sc = area(12288, 2, LCOLS)
        h_pT = area(13056, 2, LCOLS)
        h_mx = area(13824, 2, 4)
        h_den = area(13832, 4, 2)
        h_rden = area(13840, 4, 2)
        h_gc = area(0, TILES, D)
        h_ga = area(2048, TILES, D)
        h_bm = area(8192, 2 * D)
        h_m = area(6144, TILES, D)
        f_gain = area(8192, D)
        f_out = area(10240, TILES, D)
        H_UNITS = {0: h_qT[:, 0:4], 1: h_qT[:, 4:8], 2: h_kT[:, 0:4], 3: h_kT[:, 4:8], 7: h_uT[:, 0:4],
                   9: h_uT[:, 4:8], 11: None, 13: None}
        rows1 = area(8192, P)
        rows2 = area(8320, P)
        iota_i = arena[:, 8448:8448 + LCOLS].bitcast(I32)
        iand_i = arena[:, 8832:8832 + 2 * LCOLS].bitcast(I32)
        build = area(9600, 4, LCOLS)
        bg_bc = sb("bg_bc", [P, 8])

        acc = ctx.enter_context(nc.psum_tensor("acc", [P, TILES, D], F32))
        gu = ctx.enter_context(nc.psum_tensor("gu", [P, TILES, 512], F32))
        tb = ctx.enter_context(nc.psum_tensor("tb", [P, 2, 512], F32))

        raw_landed = [sem(f"raw_landed{i}") for i in range(NRAW)]
        hi_ready = sem("hi_ready")
        lo_ready = sem("lo_ready")
        tile0_used = sem("tile0_used")
        slot_used = sem("slot_used")
        t_in_psum = sem("t_in_psum")
        t_scaled = sem("t_scaled")
        t_hi_ready = sem("t_hi_ready")
        t_lo_ready = sem("t_lo_ready")
        sums_ready = sem("sums_ready")
        rstd_ready = sem("rstd_ready")
        x_ready = sem("x_ready")
        x_landed = sem("x_landed")
        dve_link = sem("dve_link")
        act_link = sem("act_link")
        silu_ready = sem("silu_ready")
        h_ready = sem("h_ready")
        ht_in_psum = sem("ht_in_psum")
        ht_hi_ready = sem("ht_hi_ready")
        ht_lo_ready = sem("ht_lo_ready")
        consts_ready = sem("consts_ready")
        tables_ready = sem("tables_ready")
        gain_landed = sem("gain_landed")
        rows_landed = sem("rows_landed")
        gcol_in_psum = sem("gcol_in_psum")
        gcol_ready = sem("gcol_ready")
        p_landed = sem("p_landed")
        pt_in_psum = sem("pt_in_psum")
        pt_hi_ready = sem("pt_hi_ready")
        pt_lo_ready = sem("pt_lo_ready")
        gate_ready = sem("gate_ready")
        hb_ready = sem("hb_ready")
        out_ready = sem("out_ready")
        out_landed = sem("out_landed")
        kv_copied = sem("kv_copied")
        kt_in_psum = sem("kt_in_psum")
        kt_ready = sem("kt_ready")

        def pair(c, t):
            return (gu[:, t, :], acc[:, t, 0:512], acc[:, t, 512:1024])[c % 3]

        def x_count(n, t, half):
            return 4 * n + 2 * t + half + 1

        def tok(t):
            return slice(t * P, (t + 1) * P)

        def t_bank(q, t, half):
            return acc[:, t, 512 * half:512 * half + 512] if q in ("HA", "HO") else tb[:, half, :]

        def ht_count(f, n, t=0):
            return (NIT + 1) * f + n + 1 + t

        wg_split = sem("wg_split")
        m_gates_in_psum = sem("m_gates_in_psum")
        m_copied = sem("m_copied")
        m_o_gate = sem("m_o_gate")
        m_absf = sem("m_absf")
        m_softlog = sem("m_softlog")
        m_logf = sem("m_logf")
        m_cum = sem("m_cum")
        m_diag_ready = sem("m_diag_ready")
        m_spread = sem("m_spread")
        m_am_ready = sem("m_am_ready")
        m_last_rhs = sem("m_last_rhs")
        m_last_in_psum = sem("m_last_in_psum")
        m_exps = sem("m_exps")
        m_exped = sem("m_exped")
        m_w_ready = sem("m_w_ready")
        m_pl_in_psum = sem("m_pl_in_psum")
        m_pl_ready = sem("m_pl_ready")
        m_ksc_ready = sem("m_ksc_ready")
        m_state_in_psum = sem("m_state_in_psum")
        m_state_ready = sem("m_state_ready")
        m_inter_in_psum = sem("m_inter_in_psum")
        m_qn_den_ready = sem("m_qn_den_ready")
        m_scores_in_psum = sem("m_scores_in_psum")
        m_p_ready = sem("m_p_ready")
        m_pt_in_psum = sem("m_pt_in_psum")
        m_pt_ready = sem("m_pt_ready")
        m_num_in_psum = sem("m_num_in_psum")
        m_h_ready = sem("m_h_ready")
        m_hsums = sem("m_hsums")
        m_y_ready = sem("m_y_ready")
        d_landed = sem("d_landed")
        d_lam = sem("d_lam")
        d_lamexp = sem("d_lamexp")
        d_qn_ready = sem("d_qn_ready")
        d_pl_in_psum = sem("d_pl_in_psum")
        d_pl_ready = sem("d_pl_ready")
        d_scores = sem("d_scores")
        d_negmax = sem("d_negmax")
        d_exped = sem("d_exped")
        d_dif_ready = sem("d_dif_ready")
        d_dt_in_psum = sem("d_dt_in_psum")
        d_dt_ready = sem("d_dt_ready")
        d_o_in_psum = sem("d_o_in_psum")
        d_o_ready = sem("d_o_ready")
        d_y_ready = sem("d_y_ready")
        h_evac = sem("h_evac")
        h_pl_in_psum = sem("h_pl_in_psum")
        h_pl_ready = sem("h_pl_ready")
        h_scores = sem("h_scores")
        h_negmax = sem("h_negmax")
        h_exped = sem("h_exped")
        h_p_ready = sem("h_p_ready")
        h_pt_in_psum = sem("h_pt_in_psum")
        h_pt_ready = sem("h_pt_ready")
        h_pv_in_psum = sem("h_pv_in_psum")
        h_o_ready = sem("h_o_ready")
        h_silu = sem("h_silu")
        h_conv = sem("h_conv")
        h_z_ready = sem("h_z_ready")
        h_gated = sem("h_gated")
        h_bm_landed = sem("h_bm_landed")
        h_gpre = sem("h_gpre")
        h_sig = sem("h_sig")
        h_m_ready = sem("h_m_ready")
        f_gain_landed = sem("f_gain_landed")

        block = ctx.enter_context(nc.Block())

        @block.sync
        def _(sp):
            def load(slot, halves):
                if slot.turn is not None or slot.s >= NRAW:
                    sp.wait_ge(lo_ready, slot.count(-NRAW))
                for view, src in halves:
                    sp.dma_start(view, src).then_inc(raw_landed[slot.raw], 16)

            def ffn(name, w_in, w_out):
                up_src = w_in.rearrange("(k p) c -> p k c", p=P)
                down_src = w_out.rearrange("(f p) c -> p f c", p=P)

                def up(n, slot, half):
                    dst = w_raw[:, slot.raw, :].rearrange("p (k u c) -> p k u c", k=4, u=2)
                    load(slot, [(dst[:, :, u, :], up_src[:, 4 * half:4 * half + 4, bass.ds(n * CH + u * FF, CH)])
                                for u in range(2)])

                def down(n, slot):
                    dst = w_raw[:, slot.raw, :].rearrange("p (f c) -> p f c", f=2)
                    load(slot, [(dst[:, f:f + 1, :], down_src[:, bass.ds(n * 2 + f, 1), :]) for f in range(2)])

                s0 = S[name]
                up(0, At(s0), 0)
                up(0, At(s0 + 1), 1)
                up(1, At(s0 + 2), 0)
                up(1, At(s0 + 3), 1)
                down(0, At(s0 + 4))
                with sp.Fori(0, (NIT - 3) // 2) as i:
                    for d in (0, 1):
                        a = At(s0 + 5 + 3 * d, i)
                        up(i * 2 + (2 + d), a, 0)
                        up(i * 2 + (2 + d), a.plus(1), 1)
                        down(i * 2 + (1 + d), a.plus(2))
                a = At(s0 + FFN_SLOTS - 4)
                up(NIT - 1, a, 0)
                up(NIT - 1, a.plus(1), 1)
                down(NIT - 2, a.plus(2))
                down(NIT - 1, a.plus(3))

            def linear(s0, w, cols):
                src = w.rearrange("(k p) c -> p k c", p=P)
                for c, col in enumerate(cols):
                    for j in range(2):
                        slot = At(s0 + 2 * c + j)
                        dst = w_raw[:, slot.raw, :].rearrange("p (k c) -> p k c", k=4)
                        load(slot, [(dst[:, 2 * k:2 * k + 2, :],
                                     src[:, 4 * j + 2 * k:4 * j + 2 * k + 2, col:col + 512]) for k in range(2)])

            def ple(name, w_proj, w_gate):
                slot = At(S[name])
                dst = w_raw[:, slot.raw, :].rearrange("p (f c) -> p f c", f=2)
                src = w_proj.rearrange("(f p) c -> p f c", p=P)
                load(slot, [(dst[:, f, :], src[:, f, :]) for f in range(2)])
                linear(S[name] + 1, w_gate, (0, 512))

            both = (0, 512)
            ffn("F0", A["w_ffn_in"][0, 0], A["w_ffn_out"][0, 0])
            linear(S["MI"], A["mlstm_w_in"][0], [512 * c for c in range(6)])
            linear(S["MO"], A["mlstm_w_out"][0], both)
            ffn("F1", A["w_ffn_in"][0, 1], A["w_ffn_out"][0, 1])
            ple("P0", A["w_ple_proj"][0], A["w_ple_gate"][0])
            linear(S["KV"], A["w_kv"], [512 * c for c in range(4)])
            ffn("F2", A["w_ffn_in"][1, 0], A["w_ffn_out"][1, 0])
            linear(S["DQ"], A["diff_w_q"][0], both)
            linear(S["DO"], A["diff_w_out"][0], both)
            ffn("F3", A["w_ffn_in"][1, 1], A["w_ffn_out"][1, 1])
            ple("P1", A["w_ple_proj"][1], A["w_ple_gate"][1])
            linear(S["HI"], A["w_in_2"][0], [512 * c for c in H_ORDER])
            linear(S["HC"], A["w_out_conv_2"][0], both)
            linear(S["HA"], A["w_out_attn_2"][0], both)
            linear(S["HO"], A["w_o_2"][0], both)
            for t in range(TILES):
                sp.wait_ge(out_ready, t + 1)
                sp.dma_start(out[0, tok(t), :], f_out[:, t, :]).then_inc(out_landed, 16)
            sp.wait_ge(out_landed, 16 * TILES)

        @block.gpsimd
        def _(pool):
            pool.memset(ident[:], 0.0).then_inc(consts_ready, 1)
            pool.memset(causal[:], 0.0).then_inc(consts_ready, 1)
            pool.memset(upto[:], 1.0).then_inc(consts_ready, 1)
            pool.memset(ones[:], 1.0).then_inc(consts_ready, 1)
            pool.memset(last_row[:], 0.0).then_inc(consts_ready, 1)
            pool.iota(iota_i[:, 0:P], pattern=[[-1, P]], base=256, channel_multiplier=1).then_inc(consts_ready, 1)
            pool.iota(iota_i[:, P:LCOLS], pattern=[[-1, 2 * P]], base=256 + P,
                      channel_multiplier=1).then_inc(consts_ready, 1)
            pool.wait_ge(consts_ready, 7)
            pool.affine_select(out=ident[:], in_=ident[:], compare_op=ALU.not_equal, fill=1.0, base=0,
                               pattern=[[-1, P]], channel_multiplier=1).then_inc(consts_ready, 1)
            pool.affine_select(out=causal[:, 0:P], in_=causal[:, 0:P], compare_op=ALU.is_ge, fill=FAR, base=0,
                               pattern=[[-1, P]], channel_multiplier=1).then_inc(consts_ready, 1)
            pool.affine_select(out=causal[:, P:LCOLS], in_=causal[:, P:LCOLS], compare_op=ALU.is_ge, fill=FAR,
                               base=P, pattern=[[-1, 2 * P]], channel_multiplier=1).then_inc(consts_ready, 1)
            pool.affine_select(out=upto[:], in_=upto[:], compare_op=ALU.is_ge, fill=0.0, base=0,
                               pattern=[[1, P]], channel_multiplier=-1).then_inc(consts_ready, 1)
            pool.affine_select(out=last_row[:], in_=last_row[:], compare_op=ALU.not_equal, fill=1.0,
                               base=-(P - 1), pattern=[[0, P]], channel_multiplier=1).then_inc(consts_ready, 1)

            def subtract(slot):
                pool.wait_ge(hi_ready, slot.count())
                pool.tensor_tensor(w_lo[:, slot.spl, :], w_raw[:, slot.raw, :],
                                   w_hi[:, slot.spl, :].bitcast(F32), ALU.subtract).then_inc(lo_ready, 1)

            with pool.Fori(0, TOTAL // NSPL) as i:
                for j in range(NSPL):
                    subtract(At(j, i))
            for s in range(TOTAL - TOTAL % NSPL, TOTAL):
                subtract(At(s))

        @block.scalar
        def _(act):
            linked = [0]

            def link(ins):
                linked[0] += 1
                ins.then_inc(act_link, 1)
                act.wait_ge(act_link, linked[0])

            def round_hi(slot):
                act.wait_ge(raw_landed[slot.raw], slot.raw_count())
                if slot.turn is not None or slot.s >= NSPL:
                    act.wait_ge(slot_used, slot.count(-NSPL))
                nc.scalar.copy(w_hi[:, slot.spl, :], w_raw[:, slot.raw, :]).then_inc(hi_ready, 1)

            def ahead(slot):
                if slot.turn is not None or slot.s + AHEAD < TOTAL:
                    round_hi(slot.plus(AHEAD))

            def load_gain(row):
                act.dma_start(gain_bc, row.rearrange("(o d) -> o d", o=1).broadcast_to([P, D])
                              ).then_inc(gain_landed, 16)

            def sum_of(j, t, src):
                if 2 * j + t:
                    act.wait_ge(sums_ready, 2 * j + t)
                nc.scalar.activation(squares[:], src, ACT.Square,
                                     accum_out=ssq[:, 2 * j + t:2 * j + t + 1]).then_inc(sums_ready, 1)

            def pre_sum(name, t):
                m = PRE[name]
                if m == 0:
                    act.wait_ge(x_landed, 16)
                else:
                    act.wait_ge(x_ready, x_count(m - 1, t, 1))
                sum_of(2 * m, t, x[:, t, :])

            def t_hi(q, t):
                for half in range(2):
                    u = 4 * T[q] + 2 * t + half
                    act.wait_ge(t_scaled, psum_units(u))
                    nc.scalar.copy(xT_hi[:, 4 * half:4 * half + 4, tok(t)],
                                   scaled[:, u % 2, :].rearrange("p (k c) -> p k c", k=4)
                                   ).then_inc(t_hi_ready, 1)

            def boundary(following, post_sum, between=lambda: None, late=lambda: None):
                post_sum(0)
                between()
                t_hi(following, 0)
                late()
                post_sum(1)
                pre_sum(following, 0)
                ahead(At(S[following]))
                t_hi(following, 1)
                pre_sum(following, 1)
                act.wait_ge(sums_ready, 4 * PRE[following] + 2)

            def acc_sum(name, last_slot):
                def post_sum(t):
                    act.wait_ge((tile0_used, slot_used)[t], last_slot + 1)
                    sum_of(2 * POST[name] + 1, t, acc[:, t, :])
                return post_sum

            def warm(func):
                link(nc.scalar.activation(squares[:, 0:1], ones[:, 0:1], func))

            def ffn(name, following):
                f, m, s0 = FFN_NO[name], PRE[name], S[name]
                warm(ACT.Silu)

                def iteration(n, turn, a, has_down):
                    b = a.plus(1)

                    def turns(per, v):
                        return v if turn is None else turn * per + v

                    def silu(t):
                        act.wait_ge((tile0_used, slot_used)[t], b.count())
                        if n:
                            act.wait_ge(h_ready, turns(4, 2 * NIT * f + 2 * (n - 1) + t + 1))
                        else:
                            act.wait_ge(rstd_ready, 2 * m + t + 1)
                        nc.scalar.activation(sg[:, t, :], gu[:, t, 0:CH], ACT.Silu,
                                             scale=rstd[:, 2 * m + t:2 * m + t + 1]).then_inc(silu_ready, 1)

                    if n:
                        ahead(a)
                    ahead(b)
                    silu(0)
                    if n < NIT - 1:
                        silu(1)
                        if has_down:
                            ahead(a.plus(2))
                        act.wait_ge(ht_in_psum, turns(2, ht_count(f, n)))
                        nc.scalar.copy(hT_hi[:], tb[:, 0, :].rearrange("p (k c) -> p k c", k=2)
                                       ).then_inc(ht_hi_ready, 1)
                        return

                    def hidden_hi(t):
                        act.wait_ge(ht_in_psum, ht_count(f, n, t))
                        nc.scalar.copy(hT_hi[:, :, tok(t)], tb[:, t, 0:2 * P].rearrange("p (k c) -> p k c", k=2)
                                       ).then_inc(ht_hi_ready, 1)

                    def second_tile():
                        hidden_hi(1)
                        ahead(a.plus(3))

                    hidden_hi(0)
                    silu(1)
                    ahead(a.plus(2))
                    boundary(following, acc_sum(name, s0 + FFN_SLOTS - 1), second_tile)

                iteration(0, None, At(s0), False)
                iteration(1, None, At(s0 + 2), True)
                with act.Fori(0, (NIT - 3) // 2) as i:
                    for d in (0, 1):
                        iteration(2 + d, i, At(s0 + 5 + 3 * d, i), True)
                iteration(NIT - 1, None, At(s0 + FFN_SLOTS - 4), True)

            def p_hi(layer):
                act.wait_ge(pt_in_psum, layer + 1)
                nc.scalar.copy(pT_hi[:], (gu[:, 0, :], tb[:, 1, :])[layer].rearrange("p (k c) -> p k c", k=2)
                               ).then_inc(pt_hi_ready, 1)

            def ple(name, layer, following):
                m, s0 = PRE[name], S[name]
                ahead(At(s0 + 1))

                def gate(t):
                    act.wait_ge(rstd_ready, 2 * m + t + 1)
                    for c in range(2):
                        act.wait_ge((tile0_used, slot_used)[t], s0 + 1 + 2 * c + 2)
                        nc.scalar.activation(gate_sb[:, t, 512 * c:512 * c + 512], (gu, tb)[c][:, t, :],
                                             ACT.Sigmoid, scale=rstd[:, 2 * m + t:2 * m + t + 1]
                                             ).then_inc(gate_ready, 1)

                def post_sum(t):
                    if t:
                        ahead(At(s0 + 4))
                    gate(t)
                    act.wait_ge(hb_ready, 2 * layer + t + 1)
                    sum_of(2 * POST[name] + 1, t, hb[:, t, :])

                def second_tile():
                    ahead(At(s0 + 2))
                    ahead(At(s0 + 3))

                boundary(following, post_sum, second_tile)

            def out_linear(name, following):
                s0 = S[name]

                ahead(At(s0))
                ahead(At(s0 + 1))
                boundary(following, acc_sum(name, s0 + 3), lambda: ahead(At(s0 + 2)), lambda: ahead(At(s0 + 3)))

            def mlstm():
                m, s0 = PRE["MI"], S["MI"]
                for j in range(1, 4):
                    ahead(At(s0 + j))
                act.wait_ge(m_absf, 1)
                link(nc.scalar.activation(m_e, m_e, ACT.Exp, scale=-1.0))
                nc.scalar.activation(m_l, m_e, ACT.Ln, bias=1.0).then_inc(m_softlog, 1)
                for j in range(4, 8):
                    ahead(At(s0 + j))
                act.wait_ge(m_am_ready, 1)
                for h in range(MH):
                    ins = nc.scalar.activation(m_am[:, 0, tok(h)], m_am[:, 0, tok(h)], ACT.Exp,
                                               bias=m_negmx[:, h:h + 1])
                ins.then_inc(m_w_ready, 1)
                act.wait_ge(m_exps, 1)
                nc.scalar.activation(m_exp0, m_exp0, ACT.Exp).then_inc(m_exped, 1)
                ahead(At(s0 + 8))
                ahead(At(s0 + 9))
                act.wait_ge(m_am_ready, 2)
                for h in range(MH):
                    ins = nc.scalar.activation(m_am[:, 1, tok(h)], m_am[:, 1, tok(h)], ACT.Exp,
                                               bias=m_negmx[:, 4 + h:5 + h])
                ins.then_inc(m_w_ready, 1)
                act.wait_ge(m_exps, 2)
                nc.scalar.activation(m_exp1, m_exp1, ACT.Exp).then_inc(m_exped, 1)
                for w in range(4):
                    act.wait_ge(m_pl_in_psum, w + 1)
                    dst = (m_qT, m_kT)[w // 2][:, :, tok(w % 2)]
                    nc.scalar.copy(dst, tb[:, 0, :].rearrange("p (h c) -> p h c", h=MH)).then_inc(m_pl_ready, 1)
                ahead(At(s0 + 10))
                ahead(At(s0 + 11))
                for c in (4, 5):
                    for t in range(TILES):
                        act.wait_ge((tile0_used, slot_used)[t], s0 + 2 * c + 2)
                        nc.scalar.activation(m_sig[:, t, 512 * (c - 4):512 * (c - 4) + 512], pair(c, t),
                                             ACT.Sigmoid, scale=rstd[:, 2 * m + t:2 * m + t + 1]
                                             ).then_inc(m_o_gate, 1)
                act.wait_ge(m_state_in_psum, 1)
                nc.scalar.copy(m_C.rearrange("p (a b) -> p a b", a=2), gu[:]).then_inc(m_state_ready, 1)
                for t in range(TILES):
                    act.wait_ge(m_pt_in_psum, t + 1)
                    if t:
                        act.wait_ge(m_num_in_psum, t)
                    nc.scalar.copy(m_PT, tb[:, t, :]).then_inc(m_pt_ready, 1)
                for t in range(TILES):
                    act.wait_ge(m_h_ready, t + 1)
                    for h in range(MH):
                        ins = nc.scalar.activation(squares[:, MDV * h:MDV * h + MDV],
                                                   m_h[:, t, MDV * h:MDV * h + MDV], ACT.Square,
                                                   accum_out=m_hssq[:, 4 * t + h:4 * t + h + 1])
                    ins.then_inc(m_hsums, 1)
                    act.wait_ge(m_hsums, t + 1)
                t_hi("MO", 0)
                t_hi("MO", 1)
                load_gain(A["norm_g"][0, 3])
                out_linear("MO", "F1")

            def diff():
                s0 = S["DQ"]
                ahead(At(s0 + 1))
                act.wait_ge(d_lam, 1)
                nc.scalar.activation(lamp[:, 2:4], lamp[:, 0:2], ACT.Exp).then_inc(d_lamexp, 1)
                ahead(At(s0 + 2))
                for w in range(4):
                    if w == 2:
                        ahead(At(s0 + 3))
                    act.wait_ge(d_pl_in_psum, w + 1)
                    nc.scalar.copy(qT[:, 4 * (w % 2):4 * (w % 2) + 4, tok(w // 2)],
                                   tb[:, w % 2, :].rearrange("p (k c) -> p k c", k=4)).then_inc(d_pl_ready, 1)
                for step in range(DH + 3):
                    h = step
                    if h < DH:
                        act.wait_ge(d_negmax, 4 * h + 4)
                        for t in range(TILES):
                            for a in range(2):
                                e = sc_[:, h % 2, LCOLS * a + P * t:LCOLS * a + P * t + P * (t + 1)]
                                i = 2 * t + a
                                ins = nc.scalar.activation(e, e, ACT.Exp, scale=-1.0, bias=dstat[:, h % 2, 4 + i:5 + i],
                                                           accum_out=dstat[:, h % 2, 8 + i:9 + i])
                        ins.then_inc(d_exped, 1)
                    h = step - 2
                    if 0 <= h < DH:
                        act.wait_ge(d_dt_in_psum, h + 1)
                        if h >= 2:
                            act.wait_ge(d_o_in_psum, h - 1)
                        nc.scalar.copy(difT[:, h % 2, :], acc[:, 0, 512 * (h % 2):512 * (h % 2) + LCOLS]
                                       ).then_inc(d_dt_ready, 1)
                    h = step - 3
                    if 0 <= h < DH:
                        act.wait_ge(d_o_in_psum, h + 1)
                        src = acc[:, 1, 512 * (h % 2):512 * (h % 2) + 2 * P].rearrange("p (t c) -> p t c", t=2)
                        nc.scalar.copy(qn[:, :, tok(h)], src)
                        if h:
                            act.wait_ge(d_o_ready, h)
                        for t in range(TILES):
                            ins = nc.scalar.activation(squares[:, tok(t)], src[:, t, :], ACT.Square,
                                                       accum_out=hstat[:, DH * t + h:DH * t + h + 1])
                        ins.then_inc(d_o_ready, 1)
                act.wait_ge(d_o_ready, DH)
                t_hi("DO", 0)
                t_hi("DO", 1)
                out_linear("DO", "F3")

            def hybrid():
                m, s0 = PRE["HI"], S["HI"]
                act.wait_ge(rstd_ready, 2 * m + 2)

                def r(t):
                    return rstd[:, 2 * m + t:2 * m + t + 1]

                def step(k):
                    h = k
                    if h < AH:
                        act.wait_ge(h_negmax, h + 1)
                        at = 0
                        for t in range(TILES):
                            e = h_sc[:, h % 2, at:at + P * (t + 1)]
                            ins = nc.scalar.activation(e, e, ACT.Exp, bias=h_mx[:, h % 2, 2 + t:3 + t])
                            at += P * (t + 1)
                        ins.then_inc(h_exped, 1)
                    h = k - 2
                    if 0 <= h < AH:
                        act.wait_ge(h_pt_in_psum, h + 1)
                        if h >= 2:
                            act.wait_ge(h_pv_in_psum, h - 1)
                        nc.scalar.copy(h_pT[:, h % 2, :], tb[:, 0, 0:LCOLS]).then_inc(h_pt_ready, 1)

                def units(c):
                    dst = H_UNITS[c]
                    for t in range(TILES):
                        w = H_UNIT_NO[c] + t
                        act.wait_ge(h_pl_in_psum, w + 1)
                        nc.scalar.copy(dst[:, :, tok(t)], tb[:, 1, :].rearrange("p (k c) -> p k c", k=4)
                                       ).then_inc(h_pl_ready, 1)

                steps = 0
                for c in range(20):
                    for j in range(2):
                        if c + j and c < 18:
                            ahead(At(s0 + 2 * c + j))
                        if H_UNITS.get(H_UNITS_AT.get((c, j))) is not None:
                            units(H_UNITS_AT[c, j])
                        if c >= 5 and steps < AH + 3:
                            step(steps)
                            steps += 1
                    if c in (10, 12, 14, 15):
                        for t in range(TILES):
                            act.wait_ge((tile0_used, slot_used)[t], s0 + 2 * c + 2)
                            act.wait_ge(h_pl_in_psum, H_S_FREE[c] + t)
                            nc.scalar.activation(h_s[:, H_PLACE[c], t, :], acc[:, t, 512 * (c % 2):512 * (c % 2) + 512],
                                                 ACT.Silu, scale=r(t)).then_inc(h_silu, 1)
                    if c == 15:
                        act.wait_ge(h_conv, 1)
                        act.dma_start(h_bm, A["b_merge_2"].broadcast_to([P, 2 * D])).then_inc(h_bm_landed, 16)
                    if c == 17:
                        for cc in (16, 17):
                            for t in range(TILES):
                                g = h_gc[:, t, 512 * (cc % 2):512 * (cc % 2) + 512]
                                act.wait_ge(h_gpre, 2 * (cc - 16) + t + 1)
                                nc.scalar.activation(g, g, ACT.Sigmoid).then_inc(h_sig, 1)
                ahead(At(s0 + 36))
                ahead(At(s0 + 37))
                for t in range(TILES):
                    act.wait_ge((tile0_used, slot_used)[t], S["HC"])
                    act.wait_ge(h_z_ready, 4)
                    for half in range(2):
                        nc.scalar.copy(xT_hi[:, 4 * half:4 * half + 4, tok(t)],
                                       h_zT[:, 4 * half:4 * half + 4, tok(t)]).then_inc(t_hi_ready, 1)
                    if t == 0:
                        ahead(At(s0 + 38))
                        ahead(At(s0 + 39))
                    act.wait_ge(h_gpre, 4 + 2 * t + 2)
                    nc.scalar.activation(h_ga[:, t, :], h_ga[:, t, :], ACT.Sigmoid).then_inc(h_sig, 1)
                act.dma_start(f_gain, A["final_g_2"].rearrange("(o d) -> o d", o=1).broadcast_to([P, D])
                              ).then_inc(f_gain_landed, 16)
                ahead(At(S["HC"]))
                ahead(At(S["HC"] + 1))
                ahead(At(S["HC"] + 2))
                t_hi("HA", 0)
                ahead(At(S["HC"] + 3))
                t_hi("HA", 1)
                for j in range(3):
                    ahead(At(S["HA"] + j))
                t_hi("HO", 0)
                ahead(At(S["HA"] + 3))
                t_hi("HO", 1)
                for t in range(TILES):
                    act.wait_ge(x_ready, x_count(8, t, 1))
                    sum_of(FINAL_SUM, t, x[:, t, :])

            act.dma_start(x[:], A["x"][0].rearrange("(t p) d -> p t d", p=P)).then_inc(x_landed, 16)
            act.dma_start(rows1, A["norm_g"].rearrange("l n (k c) -> (l n k) c", c=P)).then_inc(rows_landed, 16)
            act.dma_start(rows2[0:8], A["kv_norm"].rearrange("(k c) -> k c", c=P)).then_inc(rows_landed, 16)
            act.dma_start(rows2[8:16], A["norm_g_2"][0].rearrange("(k c) -> k c", c=P)).then_inc(rows_landed, 16)
            act.dma_start(rows2[16:40], A["conv_w_2"][0].rearrange("w (k c) -> (w k) c", c=P)
                          ).then_inc(rows_landed, 16)
            act.dma_start(p_nat, A["p"][0, 0].rearrange("(t p) c -> p t c", p=P)).then_inc(p_landed, 16)
            act.dma_start(wg_raw[:], A["mlstm_w_in"][0].rearrange("(k p) c -> p k c", p=P)[:, :, 3072:3080]
                          ).then_inc(rows_landed, 16)
            act.dma_start(bg_bc[:], A["mlstm_b_gates"].broadcast_to([P, 8])).then_inc(rows_landed, 16)
            load_gain(A["norm_g"][0, 1])
            act.wait_ge(consts_ready, 12)
            warm(ACT.Silu)
            pre_sum("F0", 0)
            pre_sum("F0", 1)
            for s in range(AHEAD):
                round_hi(At(s))
            p_hi(0)
            act.wait_ge(rows_landed, 16 * 6)
            nc.scalar.copy(wg_hi[:], wg_raw[:]).then_inc(wg_split, 1)
            t_hi("F0", 0)
            t_hi("F0", 1)
            act.wait_ge(sums_ready, 2)
            ahead(At(0))
            ffn("F0", "MI")
            act.wait_ge(x_ready, x_count(0, 1, 1))
            load_gain(A["mlstm_head_norm"][0].rearrange("h d -> (h d)"))
            mlstm()
            act.wait_ge(x_ready, x_count(1, 1, 1))
            load_gain(A["norm_g"][0, 5])
            ffn("F1", "P0")
            act.wait_ge(x_ready, x_count(2, 1, 1))
            load_gain(A["norm_g"][0, 7])
            ple("P0", 0, "KV")
            act.wait_ge(x_ready, x_count(3, 1, 1))
            load_gain(A["norm_g"][1, 1])
            act.dma_start(p_nat, A["p"][1, 0].rearrange("(t p) c -> p t c", p=P)).then_inc(p_landed, 16)
            for j in range(1, 6):
                ahead(At(S["KV"] + j))
            for w in range(4):
                act.wait_ge(kt_in_psum, w + 1)
                nc.scalar.copy(kT[:, 4 * (w % 2):4 * (w % 2) + 4, tok(w // 2)],
                               acc[:, w % 2, 0:512].rearrange("p (k c) -> p k c", k=4)
                               ).then_inc(kt_ready, 1)
                if w == 1:
                    p_hi(1)
            ahead(At(S["KV"] + 6))
            t_hi("F2", 0)
            ahead(At(S["KV"] + 7))
            t_hi("F2", 1)
            ahead(At(S["F2"]))
            ffn("F2", "DQ")
            act.wait_ge(x_ready, x_count(4, 1, 1))
            load_gain(A["norm_g"][1, 3])
            act.dma_start(lamv, A["diff_lambda"][0].rearrange("(o a) d -> o (a d)", o=1).broadcast_to([P, 256])
                          ).then_inc(d_landed, 16)
            act.dma_start(subln, A["diff_subln"].broadcast_to([P, P])).then_inc(d_landed, 16)
            diff()
            act.wait_ge(x_ready, x_count(5, 1, 1))
            load_gain(A["norm_g"][1, 5])
            ffn("F3", "P1")
            act.wait_ge(x_ready, x_count(6, 1, 1))
            load_gain(A["norm_g"][1, 7])
            ple("P1", 1, "HI")
            hybrid()

        @block.vector
        def _(dve):
            linked = [0]

            def link(ins):
                linked[0] += 1
                ins.then_inc(dve_link, 1)
                dve.wait_ge(dve_link, linked[0])

            v = nc.vector

            def rsqrt_steps(sums, mean, z, tmp, inv_n):
                link(v.tensor_scalar(mean, sums, inv_n, EPS, ALU.mult, ALU.add))
                link(v.tensor_scalar(z.bitcast(I32), mean.bitcast(I32), -0.5, MAGIC, ALU.mult, ALU.add))
                for c in (3.0, 12.0, 768.0):
                    if z.shape[1] == 1:
                        link(v.scalar_tensor_tensor(tmp, z, mean, z, ALU.mult, ALU.mult))
                    else:
                        link(v.tensor_tensor(tmp, z, mean, ALU.mult))
                        link(v.tensor_tensor(tmp, tmp, z, ALU.mult))
                    link(v.scalar_tensor_tensor(z, tmp, c, z, ALU.subtract, ALU.mult))

            def norm_steps(j, t):
                i = 2 * j + t
                dve.wait_ge(sums_ready, i + 1)
                rsqrt_steps(ssq[:, i:i + 1], meansq[:, i:i + 1], zed[:, i:i + 1], nt_[:, 0:1], 1.0 / D)

            def gain_of(q, half):
                g = GAIN[q] + 4 * half
                return gcol[:, g:g + 4].unsqueeze(2).broadcast_to([P, 4, P])

            def t_units(q, t):
                def scale(u):
                    dve.wait_ge(t_in_psum, psum_units(u))
                    if u >= 2:
                        dve.wait_ge(t_lo_ready, u - 1)
                    dst, src = scaled[:, u % 2, :], t_bank(q, t, u % 2)
                    if q in GAIN:
                        v.tensor_tensor(dst.rearrange("p (k c) -> p k c", k=4),
                                        src.rearrange("p (k c) -> p k c", k=4),
                                        gain_of(q, u % 2), ALU.mult).then_inc(t_scaled, 1)
                    else:
                        v.tensor_copy(dst, src).then_inc(t_scaled, 1)

                def low(u):
                    half = u % 2
                    dve.wait_ge(t_hi_ready, u + 1)
                    to = (slice(4 * half, 4 * half + 4), tok(t))
                    v.tensor_tensor(xT_lo[:, to[0], to[1]], scaled[:, u % 2, :].rearrange("p (k c) -> p k c", k=4),
                                    xT_hi[:, to[0], to[1]].bitcast(F32), ALU.subtract).then_inc(t_lo_ready, 1)

                u0 = 4 * T[q] + 2 * t
                scale(u0)
                scale(u0 + 1)
                low(u0)
                low(u0 + 1)

            def pre_norm(name, t):
                m = PRE[name]
                norm_steps(2 * m, t)
                i = 4 * m + t
                v.tensor_scalar(rstd[:, 2 * m + t:2 * m + t + 1], zed[:, i:i + 1], ZS, None, ALU.mult
                                ).then_inc(rstd_ready, 1)

            def boundary(name, gain_no, weight, src, last_slot, following, before=None, between=lambda: None):
                n = POST[name]
                dve.wait_ge(gain_landed, 16 * gain_no)
                for t in range(TILES):
                    if before:
                        before(t)
                    else:
                        dve.wait_ge((tile0_used, slot_used)[t], last_slot + 1)
                    norm_steps(2 * n + 1, t)
                    i = 2 * (2 * n + 1) + t
                    for half in range(2):
                        cols = slice(512 * half, 512 * half + 512)
                        if t or n:
                            dve.wait_ge(x_ready, x_count(n - (not t), not t, half))
                        link(v.scalar_tensor_tensor(ytmp[:, half, :], src[:, t, cols], zed[:, i:i + 1],
                                                    gain_bc[:, cols], ALU.mult, ALU.mult))
                        v.scalar_tensor_tensor(x[:, t, cols], ytmp[:, half, :], weight * ZS, x[:, t, cols],
                                               ALU.mult, ALU.add).then_inc(x_ready, 1)
                    if t:
                        pre_norm(following, 0)
                    else:
                        between()
                    t_units(following, t)
                pre_norm(following, 1)

            def ffn(name, gain_no, following):
                f, m, s0 = FFN_NO[name], PRE[name], S[name]
                if name != "F2":
                    dve.wait_ge(rstd_ready, 2 * m + 2)

                def iteration(n, turn):
                    def turns(per, c):
                        return c if turn is None else turn * per + c

                    def hidden(t):
                        dve.wait_ge(silu_ready, turns(4, 2 * NIT * f + 2 * n + t + 1))
                        if n and t == 0:
                            dve.wait_ge(ht_in_psum, turns(2, ht_count(f, n - 1)))
                        v.scalar_tensor_tensor(hs[:, t, :], gu[:, t, CH:2 * CH], rstd[:, 2 * m + t:2 * m + t + 1],
                                               sg[:, t, :], ALU.mult, ALU.mult).then_inc(h_ready, 1)

                    hidden(0)
                    if n < NIT - 1:
                        hidden(1)
                        dve.wait_ge(ht_hi_ready, turns(2, ht_count(f, n)))
                        v.tensor_tensor(hT_lo[:], tb[:, 0, :].rearrange("p (k c) -> p k c", k=2),
                                        hT_hi[:].bitcast(F32), ALU.subtract).then_inc(ht_lo_ready, 1)
                        return

                    def hidden_lo(t):
                        dve.wait_ge(ht_hi_ready, ht_count(f, n, t))
                        v.tensor_tensor(hT_lo[:, :, tok(t)], tb[:, t, 0:2 * P].rearrange("p (k c) -> p k c", k=2),
                                        hT_hi[:, :, tok(t)].bitcast(F32), ALU.subtract).then_inc(ht_lo_ready, 1)

                    hidden_lo(0)
                    hidden(1)
                    boundary(name, gain_no, 0.5, acc, s0 + FFN_SLOTS - 1, following,
                             between=lambda: hidden_lo(1))

                for n in range(2):
                    iteration(n, None)
                with dve.Fori(0, (NIT - 3) // 2) as i:
                    for d in (0, 1):
                        iteration(2 + d, i)
                iteration(NIT - 1, None)

            def p_lo(layer):
                dve.wait_ge(pt_hi_ready, layer + 1)
                v.tensor_tensor(pT_lo[:], (gu[:, 0, :], tb[:, 1, :])[layer].rearrange("p (k c) -> p k c", k=2),
                                pT_hi[:].bitcast(F32), ALU.subtract).then_inc(pt_lo_ready, 1)

            def ple(name, layer, gain_no, following):
                def gated(t):
                    dve.wait_ge(gate_ready, 4 * layer + 2 * t + 2)
                    v.tensor_tensor(hb[:, t, :], acc[:, t, :], gate_sb[:, t, :], ALU.mult).then_inc(hb_ready, 1)
                    dve.wait_ge(hb_ready, 2 * layer + t + 1)
                boundary(name, gain_no, 1.0, hb, None, following, before=gated)

            def mlstm():
                m, s0 = PRE["MI"], S["MI"]
                dve.wait_ge(rstd_ready, 2 * m + 2)

                def r(t):
                    return rstd[:, 2 * m + t:2 * m + t + 1]

                def take(c):
                    for t in range(TILES):
                        dve.wait_ge((tile0_used, slot_used)[t], s0 + 2 * c + 2)
                        dst = (m_qn[:, t, :], m_kn[:, t, :], m_v[:, t, 0:512], m_v[:, t, 512:1024])[c]
                        if c == 1:
                            v.tensor_scalar(dst, pair(c, t), r(t), float(MDK) ** -0.5, ALU.mult, ALU.mult
                                            ).then_inc(m_copied, 1)
                        else:
                            v.tensor_scalar(dst, pair(c, t), r(t), None, ALU.mult).then_inc(m_copied, 1)

                take(0)
                dve.wait_ge(m_gates_in_psum, 1)
                for t in range(TILES):
                    ins = v.scalar_tensor_tensor(m_g[:, t, :], tb[:, 1, 8 * t:8 * t + 8], r(t), bg_bc[:],
                                                 ALU.mult, ALU.add)
                link(ins)
                li, f = m_g[:, :, 0:MH], m_g[:, :, MH:2 * MH]
                v.scalar_tensor_tensor(m_e.rearrange("p (t h) -> p t h", t=2), f, -1.0, f, ALU.mult, ALU.max).then_inc(m_absf, 1)
                take(1)
                dve.wait_ge(m_softlog, 1)
                v.scalar_tensor_tensor(m_lf.rearrange("p (t h) -> p t h", t=2), f, 0.0,
                                       m_l.rearrange("p (t h) -> p t h", t=2), ALU.min, ALU.subtract
                                       ).then_inc(m_logf, 1)
                dve.wait_ge(m_cum, 1)
                link(v.tensor_copy(m_b, tb[:, 1, 16:24]))
                link(v.tensor_tensor(m_a.rearrange("p (t h) -> p t h", t=2), li,
                                     m_b.rearrange("p (t h) -> p t h", t=2), ALU.subtract))

                def diag(t):
                    v.tensor_tensor(m_diag.rearrange("p (h c) -> p h c", h=MH),
                                    ident[:].unsqueeze(1).broadcast_to([P, MH, P]),
                                    m_a[:, 4 * t:4 * t + 4].unsqueeze(2).broadcast_to([P, MH, P]),
                                    ALU.mult).then_inc(m_diag_ready, 1)

                def causal_max(t):
                    dve.wait_ge(m_spread, t + 1)
                    link(v.tensor_tensor(m_am[:, t, :].rearrange("p (h c) -> p h c", h=MH),
                                         tb[:, 0, :].rearrange("p (h c) -> p h c", h=MH),
                                         causal[:, 0:P].unsqueeze(1).broadcast_to([P, MH, P]), ALU.add))
                    link(v.tensor_reduce(m_mx[:, 4 * t:4 * t + 4],
                                         m_am[:, t, :].rearrange("p (h c) -> p h c", h=MH), AX, ALU.max))

                diag(0)
                take(2)
                causal_max(0)
                v.tensor_scalar(m_negmx[:, 0:4], m_mx[:, 0:4], -1.0, None, ALU.mult).then_inc(m_am_ready, 1)
                link(v.tensor_copy(m_last[:, 0:4], m_b[:, 0:4]))
                v.tensor_copy(m_last[:, 4:8], m_mx[:, 0:4]).then_inc(m_last_rhs, 1)
                diag(1)
                take(3)
                dve.wait_ge(m_last_in_psum, 1)
                link(v.tensor_copy(m_lrow, tb[:, 1, 24:32]))
                link(v.tensor_tensor(m_prev, m_lrow[:, 0:4], m_lrow[:, 4:8], ALU.add))
                link(v.scalar_tensor_tensor(m_exp0[:, 0:4], m_b[:, 0:4], -1.0, m_mx[:, 0:4], ALU.mult, ALU.subtract))
                v.tensor_tensor(m_exp0[:, 4:8], m_a[:, 0:4], m_lrow[:, 4:8], ALU.subtract).then_inc(m_exps, 1)
                causal_max(1)
                link(v.tensor_tensor(m_mx[:, 4:8], m_mx[:, 4:8], m_prev, ALU.max))
                v.tensor_scalar(m_negmx[:, 4:8], m_mx[:, 4:8], -1.0, None, ALU.mult).then_inc(m_am_ready, 1)
                link(v.scalar_tensor_tensor(m_exp1[:, 0:4], m_b[:, 4:8], -1.0, m_mx[:, 4:8], ALU.mult, ALU.subtract))
                v.tensor_tensor(m_exp1[:, 4:8], m_prev, m_mx[:, 4:8], ALU.subtract).then_inc(m_exps, 1)
                dve.wait_ge(m_exped, 2)
                v.tensor_tensor(m_ksc.rearrange("p (h c) -> p h c", h=MH),
                                m_kn[:, 0, :].rearrange("p (h c) -> p h c", h=MH),
                                m_exp0[:, 4:8].unsqueeze(2).broadcast_to([P, MH, P]), ALU.mult
                                ).then_inc(m_ksc_ready, 1)
                dve.wait_ge(m_state_in_psum, 2)
                v.tensor_copy(m_n, tb[:, 1, 32:36]).then_inc(m_state_ready, 1)
                dve.wait_ge(m_inter_in_psum, 1)
                v.tensor_tensor(m_qn_den, tb[:, 1, 36:40], m_exp1[:, 4:8], ALU.mult).then_inc(m_qn_den_ready, 1)
                for t in range(TILES):
                    dve.wait_ge(m_scores_in_psum, t + 1)
                    dve.wait_ge(m_w_ready, t + 1)
                    if t:
                        dve.wait_ge(m_pt_in_psum, t)
                    link(v.tensor_tensor(m_P, tb[:, t, :], m_am[:, t, :], ALU.mult))
                    v.tensor_reduce(m_den[:, 4 * t:4 * t + 4], m_P.rearrange("p (h c) -> p h c", h=MH), AX, ALU.add
                                    ).then_inc(m_p_ready, 1)
                dve.wait_ge(m_p_ready, 2)
                link(v.tensor_tensor(m_den[:, 4:8], m_den[:, 4:8], m_qn_den, ALU.add))
                link(v.scalar_tensor_tensor(m_den, m_den, -1.0, m_den, ALU.mult, ALU.max))
                link(v.tensor_tensor(m_den[:, 0:4], m_den[:, 0:4], m_exp0[:, 0:4], ALU.max))
                link(v.tensor_tensor(m_den[:, 4:8], m_den[:, 4:8], m_exp1[:, 0:4], ALU.max))
                link(v.reciprocal(m_rden, m_den))

                def heads(ap):
                    return ap.rearrange("p (h c) -> p h c", h=MH)

                def per_head(ap):
                    return ap.unsqueeze(2).broadcast_to([P, MH, MDV])

                dve.wait_ge(m_inter_in_psum, 2)
                link(v.tensor_tensor(heads(m_h[:, 1, :]), gu[:].rearrange("p a (b c) -> p (a b) c", b=2),
                                     per_head(m_exp1[:, 4:8]), ALU.mult))
                dve.wait_ge(m_num_in_psum, 1)
                v.tensor_tensor(heads(m_h[:, 0, :]), heads(acc[:, 0, :]), per_head(m_rden[:, 0:4]), ALU.mult
                                ).then_inc(m_h_ready, 1)
                dve.wait_ge(m_num_in_psum, 2)
                link(v.tensor_tensor(m_h[:, 1, :], acc[:, 1, :], m_h[:, 1, :], ALU.add))
                v.tensor_tensor(heads(m_h[:, 1, :]), heads(m_h[:, 1, :]), per_head(m_rden[:, 4:8]), ALU.mult
                                ).then_inc(m_h_ready, 1)
                dve.wait_ge(gain_landed, 16 * 2)
                dve.wait_ge(m_o_gate, 4)
                for t in range(TILES):
                    dve.wait_ge(m_hsums, t + 1)
                    c = slice(4 * t, 4 * t + 4)
                    rsqrt_steps(m_hssq[:, c], m_hmean[:, c], m_hz[:, c], nt_[:, 0:4], 1.0 / MDV)
                    link(v.tensor_scalar(m_hz[:, c], m_hz[:, c], ZS, None, ALU.mult))
                    for h in range(MH):
                        cols = slice(MDV * h, MDV * h + MDV)
                        ins = v.scalar_tensor_tensor(m_h[:, t, cols], m_h[:, t, cols],
                                                     m_hz[:, 4 * t + h:4 * t + h + 1], gain_bc[:, cols],
                                                     ALU.mult, ALU.mult)
                    link(ins)
                    v.tensor_tensor(m_h[:, t, :], m_h[:, t, :], m_sig[:, t, :], ALU.mult).then_inc(m_y_ready, 1)
                    t_units("MO", t)
                boundary("MO", 3, 1.0, acc, S["MO"] + 3, "F1")

            def diff():
                m, s0 = PRE["DQ"], S["DQ"]
                dve.wait_ge(d_landed, 32)
                for a in range(2):
                    link(v.tensor_tensor(lamv[:, 128 * a:128 * a + 64], lamv[:, 128 * a:128 * a + 64],
                                         lamv[:, 128 * a + 64:128 * a + 128], ALU.mult))
                v.tensor_reduce(lamp[:, 0:2], lamv.rearrange("p (a d) -> p a d", a=2)[:, :, 0:64], AX, ALU.add
                                ).then_inc(d_lam, 1)
                dve.wait_ge(d_lamexp, 1)
                link(v.tensor_tensor(lamp[:, 4:5], lamp[:, 3:4], lamp[:, 2:3], ALU.subtract))
                link(v.tensor_scalar(lamp[:, 5:6], lamp[:, 4:5], -LAM0, None, ALU.add))
                dve.wait_ge(rstd_ready, 2 * m + 2)
                for t in range(TILES):
                    dve.wait_ge((tile0_used, slot_used)[t], s0 + 4)
                    v.tensor_scalar(qn[:, t, :], acc[:, t, :], rstd[:, 2 * m + t:2 * m + t + 1], 0.125,
                                    ALU.mult, ALU.mult).then_inc(d_qn_ready, 1)
                for step in range(DH + 1):
                    h = step
                    if h < DH:
                        dve.wait_ge(d_scores, h + 1)
                        if h >= 2:
                            dve.wait_ge(d_dif_ready, h - 1)
                        s, st = sc_[:, h % 2, :], dstat[:, h % 2, :]
                        for t in range(TILES):
                            for a in range(2):
                                cols = slice(P * t, P * t + P * (t + 1))
                                i = 4 + 2 * t + a
                                v.tensor_tensor_reduce(s[:, LCOLS * a + P * t:LCOLS * a + P * t + P * (t + 1)],
                                                       (tb, gu)[a][:, h % 2, cols], causal[:, cols], -1.0, 3.0e38,
                                                       ALU.add, ALU.min, st[:, i:i + 1]).then_inc(d_negmax, 1)
                    h = step - 1
                    if h >= 0:
                        dve.wait_ge(d_exped, h + 1)
                        s, st = sc_[:, h % 2, :], dstat[:, h % 2, :]
                        link(v.reciprocal(st[:, 12:16], st[:, 8:12]))
                        rr = st[:, 12:16].rearrange("p (t a) -> p t a", t=2)
                        link(v.tensor_scalar(rr[:, :, 1:2], rr[:, :, 1:2], lamp[:, 5:6], None, ALU.mult))
                        if h >= 2:
                            dve.wait_ge(d_dt_in_psum, h - 1)
                        d = dif[:, h % 2, :]
                        v.tensor_scalar(d[:, 0:P], s[:, 0:P], st[:, 12:13], None, ALU.mult)
                        link(v.tensor_scalar(d[:, P:LCOLS], s[:, P:LCOLS], st[:, 14:15], None, ALU.mult))
                        v.scalar_tensor_tensor(d[:, 0:P], s[:, LCOLS:LCOLS + P], st[:, 13:14], d[:, 0:P],
                                               ALU.mult, ALU.add)
                        v.scalar_tensor_tensor(d[:, P:LCOLS], s[:, LCOLS + P:2 * LCOLS], st[:, 15:16], d[:, P:LCOLS],
                                               ALU.mult, ALU.add).then_inc(d_dif_ready, 1)
                dve.wait_ge(d_o_ready, DH)
                rsqrt_steps(hstat[:, 0:16], hstat[:, 16:32], hstat[:, 32:48], hstat[:, 48:64], 1.0 / P)
                link(v.tensor_scalar(hstat[:, 32:48], hstat[:, 32:48], ZS * (1.0 - LAM0), None, ALU.mult))
                for t in range(TILES):
                    y = qn[:, t, :].rearrange("p (h c) -> p h c", h=DH)
                    link(v.tensor_tensor(y, y, hstat[:, 32 + DH * t:32 + DH * t + DH].unsqueeze(2)
                                         .broadcast_to([P, DH, P]), ALU.mult))
                    v.tensor_tensor(y, y, subln.unsqueeze(1).broadcast_to([P, DH, P]), ALU.mult
                                    ).then_inc(d_y_ready, 1)
                t_units("DO", 0)
                t_units("DO", 1)
                boundary("DO", 7, 1.0, acc, S["DO"] + 3, "F3")

            def hybrid():
                m, s0 = PRE["HI"], S["HI"]
                dve.wait_ge(rstd_ready, 2 * m + 2)

                def r(t):
                    return rstd[:, 2 * m + t:2 * m + t + 1]

                def bank(c, t):
                    return acc[:, t, 512 * (c % 2):512 * (c % 2) + 512]

                def step(k):
                    h = k
                    if h < AH:
                        dve.wait_ge(h_scores, h + 1)
                        if h >= 2:
                            dve.wait_ge(h_pt_in_psum, h - 1)
                        s, st = h_sc[:, h % 2, :], h_mx[:, h % 2, :]
                        link(v.scalar_tensor_tensor(s, rel[:], 2.0 ** (-8.0 * (h + 1) / AH), gu[:, h % 2, 0:LCOLS],
                                                    ALU.mult, ALU.add))
                        v.tensor_reduce(st[:, 0:1], s[:, 0:P], AX, ALU.max)
                        link(v.tensor_reduce(st[:, 1:2], s[:, P:LCOLS], AX, ALU.max))
                        v.tensor_scalar(st[:, 2:4], st[:, 0:2], -1.0, None, ALU.mult).then_inc(h_negmax, 1)
                    h = k - 1
                    if 0 <= h < AH:
                        dve.wait_ge(h_exped, h + 1)
                        s = h_sc[:, h % 2, :]
                        v.tensor_tensor_reduce(s[:, 0:P], s[:, 0:P], times[:, 0:P], 1.0, 0.0, ALU.mult, ALU.add,
                                               h_den[:, h % 4, 0:1])
                        link(v.tensor_tensor_reduce(s[:, P:LCOLS], s[:, P:LCOLS], times[:, P:LCOLS], 1.0, 0.0,
                                                    ALU.mult, ALU.add, h_den[:, h % 4, 1:2]))
                        v.reciprocal(h_rden[:, h % 4, :], h_den[:, h % 4, :]).then_inc(h_p_ready, 1)
                    h = k - 3
                    if 0 <= h < AH:
                        dve.wait_ge(h_pv_in_psum, h + 1)
                        at = AD * (h % 2)
                        v.tensor_tensor(h_o[:, h // 2, :, at:at + AD],
                                        gu[:, h % 2, LCOLS:512].rearrange("p (t c) -> p t c", t=2),
                                        h_rden[:, h % 4, :].unsqueeze(2).broadcast_to([P, TILES, AD]), ALU.mult
                                        ).then_inc(h_o_ready, 1)

                def take(c):
                    for t in range(TILES):
                        dve.wait_ge((tile0_used, slot_used)[t], s0 + 2 * c + 2)
                        if c in H_S_FREE:
                            dve.wait_ge(h_pl_in_psum, H_S_FREE[c] + t)
                        s = h_s[:, H_PLACE[c], t, :] if c in H_PLACE else None
                        if c < 2:
                            ins = v.tensor_scalar(s, bank(c, t), r(t), float(AD) ** -0.5, ALU.mult, ALU.mult)
                        elif c < 4 or c in (6, 8):
                            ins = v.tensor_scalar(s, bank(c, t), r(t), None, ALU.mult)
                        elif c < 6:
                            ins = v.tensor_scalar(h_v[:, t, 512 * (c - 4):512 * (c - 4) + 512], bank(c, t), r(t),
                                                  None, ALU.mult)
                        elif c in (7, 9):
                            ins = v.scalar_tensor_tensor(s, bank(c, t), r(t), s, ALU.mult, ALU.mult)
                        else:
                            dve.wait_ge(h_silu, H_SILU[c - 1] - 1 + t)
                            ins = v.scalar_tensor_tensor(s, bank(c, t), r(t), s, ALU.mult, ALU.mult)
                        ins.then_inc(h_evac, 1)

                def convolve():
                    dve.wait_ge(h_pl_ready, 12)
                    for k in range(8):
                        z, u = h_zT[:, k, :], h_uT[:, k, :]
                        w = [gcol[:, CONVW + 8 * i + k:CONVW + 8 * i + k + 1] for i in range(3)]
                        link(v.tensor_scalar(z, u, w[2], None, ALU.mult))
                        link(v.scalar_tensor_tensor(z[:, 1:256], u[:, 0:255], w[1], z[:, 1:256], ALU.mult, ALU.add))
                        ins = v.scalar_tensor_tensor(z[:, 2:256], u[:, 0:254], w[0], z[:, 2:256], ALU.mult, ALU.add)
                        if k == 7:
                            ins.then_inc(h_conv, 1)
                        else:
                            link(ins)

                def z_units(c):
                    half = (c - 11) // 2
                    dve.wait_ge(h_conv, 1)
                    for t in range(TILES):
                        dve.wait_ge(h_pl_in_psum, H_UNIT_NO[c] + t + 1)
                        z = h_zT[:, 4 * half:4 * half + 4, tok(t)]
                        v.tensor_tensor(z, tb[:, 1, :].rearrange("p (k c) -> p k c", k=4), z, ALU.mult
                                        ).then_inc(h_z_ready, 1)

                def gate_before_sigmoid(c, t):
                    dve.wait_ge(h_bm_landed, 16)
                    dve.wait_ge((tile0_used, slot_used)[t], s0 + 2 * c + 2)
                    g = (h_gc, h_ga)[c // 18][:, t, 512 * (c % 2):512 * (c % 2) + 512]
                    v.scalar_tensor_tensor(g, bank(c, t), r(t), h_bm[:, 512 * (c - 16):512 * (c - 16) + 512],
                                           ALU.mult, ALU.add).then_inc(h_gpre, 1)

                steps = 0
                for c in range(18):
                    for j in range(2):
                        if H_UNITS_AT.get((c, j)) in (11, 13):
                            z_units(c - 1)
                        if c >= 5 and steps < AH + 3:
                            step(steps)
                            steps += 1
                        if c == 10 and j == 1:
                            convolve()
                    if c < 10 or c in (11, 13):
                        take(c)
                    elif c in (14, 15):
                        dve.wait_ge(h_o_ready, AH)
                        for t in range(TILES):
                            dve.wait_ge(h_silu, H_SILU[c] - 1 + t)
                            o = h_o[:, 4 * (c - 14):4 * (c - 14) + 4, t, :]
                            v.tensor_tensor(o, o, h_s[:, H_PLACE[c], t, :].rearrange("p (k c) -> p k c", k=4),
                                            ALU.mult).then_inc(h_gated, 1)
                    elif c in (16, 17):
                        for t in range(TILES):
                            gate_before_sigmoid(c, t)
                for t in range(TILES):
                    gate_before_sigmoid(18, t)
                    gate_before_sigmoid(19, t)
                    for half in range(2):
                        dve.wait_ge(t_hi_ready, 4 * T["HC"] + 2 * t + half + 1)
                        at = (slice(4 * half, 4 * half + 4), tok(t))
                        v.tensor_tensor(xT_lo[:, at[0], at[1]], h_zT[:, at[0], at[1]],
                                        xT_hi[:, at[0], at[1]].bitcast(F32), ALU.subtract).then_inc(t_lo_ready, 1)
                dve.wait_ge(h_sig, 4)
                for t in range(TILES):
                    dve.wait_ge((tile0_used, slot_used)[t], S["HC"] + 4)
                    for half, src in enumerate((gu, tb)):
                        cols = slice(512 * half, 512 * half + 512)
                        ins = v.tensor_tensor(h_m[:, t, cols], src[:, t, :], h_gc[:, t, cols], ALU.mult)
                    link(ins)
                    t_units("HA", t)
                for t in range(TILES):
                    dve.wait_ge(h_sig, 4 + t + 1)
                    dve.wait_ge((tile0_used, slot_used)[t], S["HA"] + 4)
                    link(v.tensor_tensor(h_ga[:, t, :], acc[:, t, :], h_ga[:, t, :], ALU.mult))
                    v.tensor_tensor(h_m[:, t, :], h_m[:, t, :], h_ga[:, t, :], ALU.add).then_inc(h_m_ready, 1)
                    t_units("HO", t)
                dve.wait_ge(f_gain_landed, 16)
                for t in range(TILES):
                    dve.wait_ge((tile0_used, slot_used)[t], S["HO"] + 4)
                    for half, src in enumerate((gu, tb)):
                        cols = slice(512 * half, 512 * half + 512)
                        v.tensor_tensor(x[:, t, cols], src[:, t, :], x[:, t, cols], ALU.add
                                        ).then_inc(x_ready, 1)
                    norm_steps(FINAL_SUM, t)
                    i = 2 * FINAL_SUM + t
                    link(v.tensor_scalar(zed[:, i:i + 1], zed[:, i:i + 1], ZS, None, ALU.mult))
                    v.scalar_tensor_tensor(f_out[:, t, :], x[:, t, :], zed[:, i:i + 1], f_gain, ALU.mult, ALU.mult
                                           ).then_inc(out_ready, 1)

            dve.wait_ge(gcol_in_psum, 1)
            v.tensor_copy(gcol[:], tb[:, 0, 0:168]).then_inc(gcol_ready, 1)
            dve.wait_ge(gcol_ready, 1)
            p_lo(0)
            dve.wait_ge(wg_split, 1)
            v.tensor_tensor(wg_lo[:], wg_raw[:], wg_hi[:].bitcast(F32), ALU.subtract).then_inc(wg_split, 1)
            for t in range(TILES):
                t_units("F0", t)
                pre_norm("F0", t)
            dve.wait_ge(consts_ready, 12)
            fdist, m4, m16, fwin = (build[:, i, :] for i in range(4))
            v.tensor_scalar(iand_i[:, 0:LCOLS], iota_i, 3, None, ALU.bitwise_and)
            v.tensor_scalar(iand_i[:, LCOLS:2 * LCOLS], iota_i, 15, None, ALU.bitwise_and)
            link(v.tensor_scalar(fdist, iota_i, -256.0, None, ALU.add))
            v.tensor_scalar(m4, iand_i[:, 0:LCOLS], 0.0, None, ALU.is_equal)
            v.tensor_scalar(m16, iand_i[:, LCOLS:2 * LCOLS], 0.0, None, ALU.is_equal)
            link(v.tensor_scalar(fwin, fdist, float(P), None, ALU.is_le))
            link(v.tensor_tensor(m4, m4, m16, ALU.add))
            link(v.tensor_tensor(m4, m4, fwin, ALU.add))
            link(v.tensor_scalar(m16, fdist, 0.0, None, ALU.is_ge))
            link(v.tensor_tensor(times[:], m4, m16, ALU.mult))
            link(v.tensor_scalar(m4, times[:], 0.5, None, ALU.is_le))
            link(v.tensor_scalar(m4, m4, FAR, None, ALU.mult))
            v.tensor_tensor(rel[:], m4, fdist, ALU.subtract).then_inc(tables_ready, 1)
            dve.wait_ge(tables_ready, 1)
            ffn("F0", 1, "MI")
            mlstm()
            ffn("F1", 4, "P0")
            ple("P0", 0, 5, "KV")
            dve.wait_ge(rstd_ready, 2 * PRE["KV"] + 2)
            for g, dst in enumerate((kn, v_sh)):
                if g:
                    p_lo(1)
                for t in range(TILES):
                    for c in (2 * g, 2 * g + 1):
                        dve.wait_ge((tile0_used, slot_used)[t], S["KV"] + 2 * c + 2)
                        i = 2 * PRE["KV"] + t
                        v.tensor_scalar(dst[:, t, 512 * (c % 2):512 * (c % 2) + 512], pair(c, t),
                                        rstd[:, i:i + 1], None, ALU.mult).then_inc(kv_copied, 1)
                    if g:
                        t_units("F2", t)
            ffn("F2", 6, "DQ")
            diff()
            ffn("F3", 8, "P1")
            ple("P1", 1, 9, "HI")
            hybrid()

        @block.tensor
        def _(pe):
            mm = nc.tensor.matmul

            def has_t(q, t, half):
                pe.wait_ge(t_lo_ready, 4 * T[q] + 2 * t + half + 1)

            def across_tile(slot, half, t, out, q=None):
                pe.wait_ge(lo_ready, slot.count())
                if q:
                    has_t(q, t, half)
                for k in range(4):
                    wh = w_hi[:, slot.spl, 512 * k:512 * k + 512]
                    wl = w_lo[:, slot.spl, 512 * k:512 * k + 512]
                    xh, xl = xT_hi[:, 4 * half + k, tok(t)], xT_lo[:, 4 * half + k, tok(t)]
                    mm(out, xh, wh, start=(half == 0 and k == 0), stop=False)
                    mm(out, xh, wl, start=False, stop=False)
                    last = mm(out, xl, wh, start=False, stop=(half == 1 and k == 3))
                last.then_inc((tile0_used, slot_used)[t], 1)

            def across(slot, half, outs):
                for t in range(TILES):
                    across_tile(slot, half, t, outs[t])

            def by_tile(s0, count, q, outs, amid):
                for t in range(TILES):
                    for i in range(count):
                        across_tile(At(s0 + i), i % 2, t, outs(i // 2, t), q if i < 2 else None)
                        if i == 1 and amid[t]:
                            amid[t]()

            def down_tile(slot, a_hi, a_lo, t, first, final, amid=None):
                pe.wait_ge(lo_ready, slot.count())
                for k in range(2):
                    def w(ring, half):
                        return ring[:, slot.spl, D * k + 512 * half:D * k + 512 * half + 512]
                    st, sp_ = first and k == 0, final and k == 1
                    for half in range(2):
                        mm(acc[:, t, 512 * half:512 * half + 512], a_hi[:, k, tok(t)], w(w_hi, half),
                           start=st, stop=False)
                    for half in range(2):
                        mm(acc[:, t, 512 * half:512 * half + 512], a_hi[:, k, tok(t)], w(w_lo, half),
                           start=False, stop=False)
                    for half in range(2):
                        last = mm(acc[:, t, 512 * half:512 * half + 512], a_lo[:, k, tok(t)], w(w_hi, half),
                                  start=False, stop=sp_)
                    if k == 0 and amid:
                        amid()
                last.then_inc((tile0_used, slot_used)[t], 1)

            def t_units(q, t, src, wait):
                for half in range(2):
                    u = 4 * T[q] + 2 * t + half
                    wait(half)
                    if psum_units(u) > 2:
                        pe.wait_ge(t_scaled, psum_units(u) - 2)
                    for k in range(4):
                        ins = nc.tensor.transpose(t_bank(q, t, half)[:, tok(k)], src(4 * half + k), ident[:])
                    ins.then_inc(t_in_psum, 1)

            def t_of_x(name, t):
                n = PRE[name]

                def wait(half):
                    if n:
                        pe.wait_ge(x_ready, x_count(n - 1, t, half))
                    elif t + half == 0:
                        pe.wait_ge(x_landed, 16)
                        pe.wait_ge(gcol_ready, 1)
                t_units(name, t, lambda k: x[:, t, tok(k)], wait)

            def ffn(name, following):
                f, s0 = FFN_NO[name], S[name]

                def gate_up(n, turn, a):
                    if n:
                        pe.wait_ge(h_ready, 2 * NIT * f + 2 * n if turn is None else turn * 4 + 2 * NIT * f + 2 * n)
                    across(a, 0, [gu[:, t, :] for t in range(TILES)])
                    across(a.plus(1), 1, [gu[:, t, :] for t in range(TILES)])

                def down_n(n, turn, slot):
                    pe.wait_ge(ht_lo_ready, ht_count(f, n) if turn is None else turn * 2 + ht_count(f, n))
                    for t in range(TILES):
                        down_tile(slot, hT_hi, hT_lo, t, n == 0, False)

                def turn_h(n, turn):
                    pe.wait_ge(h_ready, 2 * NIT * f + 2 * n + 2 if turn is None
                               else turn * 4 + 2 * NIT * f + 2 * n + 2)
                    for k in range(2):
                        for t in range(TILES):
                            ins = nc.tensor.transpose(tb[:, 0, 256 * k + P * t:256 * k + P * t + P],
                                                      hs[:, t, tok(k)], ident[:])
                    ins.then_inc(ht_in_psum, 1)

                by_tile(s0, 2, name, lambda c, t: gu[:, t, :], (lambda: t_of_x(name, 1), None))
                turn_h(0, None)
                gate_up(1, None, At(s0 + 2))
                down_n(0, None, At(s0 + 4))
                turn_h(1, None)
                with pe.Fori(0, (NIT - 3) // 2) as i:
                    for d in (0, 1):
                        gate_up(2 + d, i, At(s0 + 5 + 3 * d, i))
                        down_n(1 + d, i, At(s0 + 7 + 3 * d, i))
                        turn_h(2 + d, i)

                n, a = NIT - 1, At(s0 + FFN_SLOTS - 4)

                def turn_tile(t):
                    pe.wait_ge(h_ready, 2 * NIT * f + 2 * n + t + 1)
                    for k in range(2):
                        ins = nc.tensor.transpose(tb[:, t, tok(k)], hs[:, t, tok(k)], ident[:])
                    ins.then_inc(ht_in_psum, 1)

                def gate_up_tile(t):
                    pe.wait_ge(h_ready, 2 * NIT * f + 2 * n)
                    across_tile(a, 0, t, gu[:, t, :])
                    across_tile(a.plus(1), 1, t, gu[:, t, :])

                gate_up_tile(0)
                pe.wait_ge(ht_lo_ready, ht_count(f, n - 1))
                down_tile(a.plus(2), hT_hi, hT_lo, 0, False, False)
                turn_tile(0)
                gate_up_tile(1)
                pe.wait_ge(ht_lo_ready, ht_count(f, n, 0))
                down_tile(a.plus(3), hT_hi, hT_lo, 0, False, True)
                down_tile(a.plus(2), hT_hi, hT_lo, 1, False, False)
                turn_tile(1)
                pe.wait_ge(ht_lo_ready, ht_count(f, n, 1))
                down_tile(a.plus(3), hT_hi, hT_lo, 1, False, True, amid=lambda: t_of_x(following, 0))

            def acc_outs(c, t):
                return acc[:, t, 512 * c:512 * c + 512]

            def turn_p(layer):
                pe.wait_ge(p_landed, 16 * (layer + 1))
                dst = (gu[:, 0, :], tb[:, 1, :])[layer]
                for k in range(2):
                    for t in range(TILES):
                        ins = nc.tensor.transpose(dst[:, 256 * k + P * t:256 * k + P * t + P],
                                                  p_nat[:, t, tok(k)], ident[:])
                ins.then_inc(pt_in_psum, 1)

            def ple(name, layer, following):
                s0 = S[name]
                pe.wait_ge(pt_lo_ready, layer + 1)
                for t in range(TILES):
                    pe.wait_ge(x_ready, x_count(PRE[name] - 1, t, 1))
                    down_tile(At(s0), pT_hi, pT_lo, t, True, True)
                    for i in range(4):
                        if i == 2 and t == 0:
                            t_of_x(name, 1)
                        if i == 2:
                            if t:
                                t_of_x(following, 0)
                            pe.wait_ge(t_scaled, psum_units(4 * T[following if t else name] + 3 - 2 * t))
                        across_tile(At(s0 + 1 + i), i % 2, t, (gu, tb)[i // 2][:, t, :], name if i < 2 else None)

            def mlstm():
                s0 = S["MI"]

                def chunk(c, amid=None):
                    if c >= 3:
                        pe.wait_ge(m_copied, 2 * (c - 3) + 2)
                    for j in range(2):
                        across(At(s0 + 2 * c + j), j, [pair(c, t) for t in range(TILES)])
                        if amid and j == 0:
                            amid()

                by_tile(s0, 4, "MI", pair, (lambda: t_of_x("MI", 1), None))
                pe.wait_ge(wg_split, 2)
                for t in range(TILES):
                    o = tb[:, 1, 8 * t:8 * t + 8]
                    for k in range(KT):
                        mm(o, xT_hi[:, k, tok(t)], wg_hi[:, k, :], start=(k == 0), stop=False)
                        mm(o, xT_hi[:, k, tok(t)], wg_lo[:, k, :], start=False, stop=False)
                        ins = mm(o, xT_lo[:, k, tok(t)], wg_hi[:, k, :], start=False, stop=(k == KT - 1))
                ins.then_inc(m_gates_in_psum, 1)

                def cumulate():
                    pe.wait_ge(m_logf, 1)
                    mm(tb[:, 1, 16:24], upto[:], m_lf, start=True, stop=True).then_inc(m_cum, 1)

                chunk(2, cumulate)

                def spread(t):
                    pe.wait_ge(m_diag_ready, t + 1)
                    if t:
                        pe.wait_ge(m_am_ready, t)
                    mm(tb[:, 0, :], ones[:], m_diag, start=True, stop=True).then_inc(m_spread, 1)

                spread(0)
                chunk(3)
                pe.wait_ge(m_last_rhs, 1)
                mm(tb[:, 1, 24:32], last_row[:], m_last, start=True, stop=True).then_inc(m_last_in_psum, 1)
                spread(1)
                chunk(4)
                pe.wait_ge(m_am_ready, 2)
                for w in range(4):
                    if w:
                        pe.wait_ge(m_pl_ready, w)
                    for h in range(MH):
                        ins = nc.tensor.transpose(tb[:, 0, tok(h)], (m_qn, m_kn)[w // 2][:, w % 2, tok(h)], ident[:])
                    ins.then_inc(m_pl_in_psum, 1)
                chunk(5)
                pe.wait_ge(m_ksc_ready, 1)
                pe.wait_ge(m_copied, 8)
                cs = gu[:].rearrange("p a (b c) -> p (a b) c", b=2)
                for h in range(MH):
                    ins = mm(cs[:, h, :], m_ksc[:, tok(h)], m_v[:, 0, MDV * h:MDV * h + MDV], start=True, stop=True)
                ins.then_inc(m_state_in_psum, 1)
                for h in range(MH):
                    ins = mm(tb[:, 1, 32 + h:33 + h], m_ksc[:, tok(h)], ones[:, 0:1], start=True, stop=True)
                ins.then_inc(m_state_in_psum, 1)
                pe.wait_ge(m_pl_ready, 4)
                pe.wait_ge(m_state_ready, 2)
                for h in range(MH):
                    ins = mm(tb[:, 1, 36 + h:37 + h], m_qT[:, h, tok(1)], m_n[:, h:h + 1], start=True, stop=True)
                ins.then_inc(m_inter_in_psum, 1)
                for h in range(MH):
                    ins = mm(cs[:, h, :], m_qT[:, h, tok(1)], m_C[:, MDV * h:MDV * h + MDV], start=True, stop=True)
                ins.then_inc(m_inter_in_psum, 1)
                pe.wait_ge(m_o_gate, 4)
                for t in range(TILES):
                    if t:
                        pe.wait_ge(m_qn_den_ready, 1)
                    for h in range(MH):
                        ins = mm(tb[:, t, tok(h)], m_qT[:, h, tok(t)], m_kT[:, h, tok(t)], start=True, stop=True)
                    ins.then_inc(m_scores_in_psum, 1)
                for t in range(TILES):
                    pe.wait_ge(m_p_ready, t + 1)
                    for h in range(MH):
                        ins = nc.tensor.transpose(tb[:, t, tok(h)], m_P[:, tok(h)], ident[:])
                    ins.then_inc(m_pt_in_psum, 1)
                    pe.wait_ge(m_pt_ready, t + 1)
                    for h in range(MH):
                        ins = mm(acc[:, t, MDV * h:MDV * h + MDV], m_PT[:, tok(h)],
                                 m_v[:, t, MDV * h:MDV * h + MDV], start=True, stop=True)
                    ins.then_inc(m_num_in_psum, 1)
                def t_of_h(t):
                    t_units("MO", t, lambda k: m_h[:, t, tok(k)], lambda half: pe.wait_ge(m_y_ready, t + 1))

                t_of_h(0)
                by_tile(S["MO"], 4, "MO", acc_outs, (lambda: t_of_h(1), lambda: t_of_x("F1", 0)))

            def diff():
                def turn_q(t):
                    pe.wait_ge(d_qn_ready, t + 1)
                    for w in (2 * t, 2 * t + 1):
                        if t:
                            pe.wait_ge(d_pl_ready, w - 1)
                        for k in range(4):
                            ins = nc.tensor.transpose(tb[:, w % 2, tok(k)], qn[:, t, tok(4 * (w % 2) + k)], ident[:])
                        ins.then_inc(d_pl_in_psum, 1)

                by_tile(S["DQ"], 4, "DQ", acc_outs, (lambda: t_of_x("DQ", 1), lambda: turn_q(0)))
                turn_q(1)
                pe.wait_ge(d_pl_ready, 4)
                for step in range(DH + 3):
                    h = step
                    if h < DH:
                        if h >= 2:
                            pe.wait_ge(d_negmax, 4 * (h - 1))
                        for t in range(TILES):
                            for a in range(2):
                                b = slice(64 * a, 64 * a + 64)
                                o = (tb, gu)[a][:, h % 2, P * t:P * t + P * (t + 1)]
                                ins = mm(o, qT[b, h, tok(t)], kT[b, h, 0:P * (t + 1)], start=True, stop=True)
                        ins.then_inc(d_scores, 1)
                    h = step - 2
                    if 0 <= h < DH:
                        pe.wait_ge(d_dif_ready, h + 1)
                        if h >= 2:
                            pe.wait_ge(d_dt_ready, h - 1)
                        for i in range(3):
                            ins = nc.tensor.transpose(acc[:, 0, 512 * (h % 2) + P * i:512 * (h % 2) + P * i + P],
                                                      dif[:, h % 2, tok(i)], ident[:])
                        ins.then_inc(d_dt_in_psum, 1)
                    h = step - 3
                    if 0 <= h < DH:
                        pe.wait_ge(d_dt_ready, h + 1)
                        if h >= 2:
                            pe.wait_ge(d_o_ready, h - 1)
                        o = acc[:, 1, 512 * (h % 2):512 * (h % 2) + 2 * P]
                        mm(o[:, 0:P], difT[:, h % 2, 0:P], v_sh[:, 0, tok(h)], start=True, stop=True)
                        mm(o[:, P:2 * P], difT[:, h % 2, P:2 * P], v_sh[:, 0, tok(h)], start=True, stop=False)
                        mm(o[:, P:2 * P], difT[:, h % 2, 2 * P:3 * P], v_sh[:, 1, tok(h)], start=False, stop=True
                           ).then_inc(d_o_in_psum, 1)
                def t_of_o(t):
                    t_units("DO", t, lambda k: qn[:, t, tok(k)], lambda half: pe.wait_ge(d_y_ready, t + 1))

                t_of_o(0)
                by_tile(S["DO"], 4, "DO", acc_outs, (lambda: t_of_o(1), lambda: t_of_x("F3", 0)))

            def hybrid():
                s0 = S["HI"]

                def step(k):
                    h = k
                    if h < AH:
                        if h == 0:
                            pe.wait_ge(h_pl_ready, 8)
                        if h >= 2:
                            pe.wait_ge(h_negmax, h - 1)
                        if h >= 4:
                            pe.wait_ge(h_o_ready, h - 3)
                        b = slice(AD * (h % 2), AD * (h % 2) + AD)
                        for t in range(TILES):
                            ins = mm(gu[:, h % 2, P * t:P * t + P * (t + 1)], h_qT[b, h // 2, tok(t)],
                                     h_kT[b, h // 2, 0:P * (t + 1)], start=True, stop=True)
                        ins.then_inc(h_scores, 1)
                    h = k - 2
                    if 0 <= h < AH:
                        pe.wait_ge(h_p_ready, h + 1)
                        if h >= 1:
                            pe.wait_ge(h_pt_ready, h)
                        for i in range(3):
                            ins = nc.tensor.transpose(tb[:, 0, tok(i)], h_sc[:, h % 2, tok(i)], ident[:])
                        ins.then_inc(h_pt_in_psum, 1)
                    h = k - 3
                    if 0 <= h < AH:
                        pe.wait_ge(h_pt_ready, h + 1)
                        if h + 2 < AH:
                            pe.wait_ge(h_negmax, h + 3)
                        if h >= AH - 2:
                            pe.wait_ge(h_o_ready, h - 1)
                        o = gu[:, h % 2, LCOLS:512]
                        pt = h_pT[:, h % 2, :]
                        vc = slice(AD * h, AD * h + AD)
                        mm(o[:, 0:AD], pt[:, 0:P], h_v[:, 0, vc], start=True, stop=True)
                        mm(o[:, AD:2 * AD], pt[:, P:2 * P], h_v[:, 0, vc], start=True, stop=False)
                        mm(o[:, AD:2 * AD], pt[:, 2 * P:3 * P], h_v[:, 1, vc], start=False, stop=True
                           ).then_inc(h_pv_in_psum, 1)

                def units(c):
                    pe.wait_ge(h_evac, H_EVAC[c])
                    for t in range(TILES):
                        w = H_UNIT_NO[c] + t
                        if 0 < w <= 12:
                            pe.wait_ge(h_pl_ready, w)
                        elif w > 12:
                            pe.wait_ge(h_z_ready, w - 12)
                        for k in range(4):
                            ins = nc.tensor.transpose(tb[:, 1, tok(k)], h_s[:, H_PLACE[c], t, tok(k)], ident[:])
                        ins.then_inc(h_pl_in_psum, 1)

                by_tile(s0, 4, "HI", acc_outs, (lambda: t_of_x("HI", 1), None))
                steps = 0
                for c in range(2, 18):
                    if c - 2 in H_EVAC:
                        pe.wait_ge(h_evac, H_EVAC[c - 2])
                    elif c - 2 in H_SILU:
                        pe.wait_ge(h_silu, H_SILU[c - 2])
                    for j in range(2):
                        across(At(s0 + 2 * c + j), j, [acc[:, t, 512 * (c % 2):512 * (c % 2) + 512]
                                                       for t in range(TILES)])
                        if (c, j) in H_UNITS_AT:
                            units(H_UNITS_AT[c, j])
                        if c >= 5 and steps < AH + 3:
                            step(steps)
                            steps += 1
                pe.wait_ge(h_gpre, 4)
                by_tile(s0 + 36, 4, None, acc_outs, (None, None))

                def t_of_a(t):
                    def wait(half):
                        pe.wait_ge(h_gated, 4)
                        pe.wait_ge(h_gpre, 4 + 2 * t + 2)
                    t_units("HA", t, lambda k: h_o[:, k, t, :], wait)

                def t_of_m(t):
                    t_units("HO", t, lambda k: h_m[:, t, tok(k)], lambda half: pe.wait_ge(h_m_ready, t + 1))

                def gu_tb(c, t):
                    return (gu, tb)[c][:, t, :]

                pe.wait_ge(h_o_ready, AH)
                pe.wait_ge(h_z_ready, 4)
                by_tile(S["HC"], 4, "HC", gu_tb, (None, lambda: t_of_a(0)))
                by_tile(S["HA"], 4, "HA", acc_outs, (lambda: t_of_a(1), lambda: t_of_m(0)))
                by_tile(S["HO"], 4, "HO", gu_tb, (lambda: t_of_m(1), None))

            pe.wait_ge(consts_ready, 12)
            pe.wait_ge(rows_landed, 16 * 6)
            nc.tensor.transpose(tb[:, 0, 0:P], rows1, ident[:])
            nc.tensor.transpose(tb[:, 0, P:168], rows2[0:40], ident[0:40, 0:40]).then_inc(gcol_in_psum, 1)
            turn_p(0)
            pe.wait_ge(pt_lo_ready, 1)
            t_of_x("F0", 0)
            ffn("F0", "MI")
            mlstm()
            ffn("F1", "P0")
            ple("P0", 0, "KV")

            def turn_keys(t):
                pe.wait_ge(kv_copied, 4)
                for w in (2 * t, 2 * t + 1):
                    if t:
                        pe.wait_ge(kt_ready, w - 1)
                    for k in range(4):
                        ins = nc.tensor.transpose(acc[:, w % 2, tok(k)], kn[:, t, tok(4 * (w % 2) + k)], ident[:])
                    ins.then_inc(kt_in_psum, 1)

            def turn_keys_and_p():
                turn_keys(0)
                turn_p(1)
                turn_keys(1)

            def t_of_x_again():
                pe.wait_ge(pt_lo_ready, 2)
                t_of_x("F2", 0)

            by_tile(S["KV"], 4, "KV", pair, (lambda: t_of_x("KV", 1), None))
            pe.wait_ge(kv_copied, 3)
            by_tile(S["KV"] + 4, 4, None, lambda c, t: pair(c + 2, t), (turn_keys_and_p, t_of_x_again))
            ffn("F2", "DQ")
            diff()
            ffn("F3", "P1")
            ple("P1", 1, "HI")
            hybrid()


_INS = ["x", "p", "norm_g", "w_ffn_in", "w_ffn_out", "w_ple_proj", "w_ple_gate", "mlstm_w_in", "mlstm_b_gates",
        "mlstm_head_norm", "mlstm_w_out", "kv_norm", "w_kv", "diff_w_q", "diff_lambda", "diff_subln", "diff_w_out",
        "norm_g_2", "w_in_2", "b_merge_2", "conv_w_2", "w_out_conv_2", "w_out_attn_2", "w_o_2", "final_g_2"]


def kernel(**inputs):
    import numpy as _np
    import concourse.bacc as _bacc
    from concourse import mybir as _mybir
    from concourse.bass_utils import run_bass_kernel_spmd as _run

    nc = _bacc.Bacc("TRN2", target_bir_lowering=False, num_devices=1, dynamic_dma_scratch_size=1024)
    arrays, aps = {}, {}
    for name in _INS:
        a = _np.ascontiguousarray(inputs[name])
        arrays[f"in_{name}"] = a
        aps[name] = nc.dram_tensor(f"in_{name}", a.shape, _mybir.dt.from_np(a.dtype), kind="ExternalInput").ap()
    out = nc.dram_tensor("out_x", (1, 256, 1024), F32, kind="ExternalOutput").ap()
    program(nc, aps, out)
    r = _run(nc, [arrays], core_ids=[0])
    return r.results[0]["out_x"]
```

```python
import math
from contextlib import ExitStack

import numpy as np

import concourse.bass as bass
from concourse import mybir

F32 = mybir.dt.float32
F32R = mybir.dt.float32r
BF16 = mybir.dt.bfloat16
I32 = mybir.dt.int32
ALU = mybir.AluOpType
ACT = mybir.ActivationFunctionType
AX = mybir.AxisListType.X

P = 128
TILES = 2
D = 1024
KT = D // P
FF = 2816
CH = 256
NIT = FF // CH
EPS = 1e-6
SLOT = 2048
NRAW = 3
NSPL = 6
AHEAD = 4
FAR = -1.0e30
MAGIC = 1597463007.0
ZS = -1.0 / 8192.0
MH, MDK, MDV = 4, 128, 256
DH = 8
LAM0 = 0.8 - 0.6 * math.exp(-0.3)
AH, AD = 16, 64
LCOLS = 3 * P

FFN_SLOTS = 3 * NIT
_N = dict(F0=FFN_SLOTS, MI=12, MO=4, F1=FFN_SLOTS, P0=5, KV=8, F2=FFN_SLOTS, DQ=4, DO=4,
          F3=FFN_SLOTS, P1=5, HI=40, HC=4, HA=4, HO=4)
S = {}
_at = 0
for _k, _v in _N.items():
    S[_k] = _at
    _at += _v
TOTAL = _at

T = {k: i for i, k in enumerate(("F0", "MI", "MO", "F1", "P0", "KV", "F2", "DQ", "DO", "F3", "P1",
                                 "HI", "HC", "HA", "HO"))}
PRE = dict(F0=0, MI=1, F1=2, P0=3, KV=4, F2=4, DQ=5, F3=6, P1=7, HI=8)
POST = dict(F0=0, MO=1, F1=2, P0=3, F2=4, DO=5, F3=6, P1=7)
FINAL_SUM = 17
FFN_NO = dict(F0=0, F1=1, F2=2, F3=3)
GAIN = dict(F0=0, MI=16, F1=32, P0=48, F2=64, DQ=80, F3=96, P1=112, KV=128, HI=136)
CONVW = 144
T_FACTOR = dict(MO=ZS, DO=ZS * (1.0 - LAM0), HA=1.0, HO=1.0)
H_ORDER = [8, 9, 10, 11, 12, 13, 0, 4, 1, 5, 6, 2, 7, 3, 14, 15, 16, 17, 18, 19]

H_UNIT_NO = {0: 0, 1: 2, 2: 4, 3: 6, 7: 8, 9: 10, 11: 12, 13: 14}
H_PLACE = {0: 0, 1: 1, 2: 0, 3: 1, 6: 0, 7: 0, 8: 1, 9: 1, 10: 0, 11: 0, 12: 1, 13: 1, 14: 0, 15: 1}
H_S_FREE = {2: 1, 3: 3, 6: 5, 8: 7, 10: 9, 12: 11, 14: 13, 15: 15}
H_CONVOLVE = {(9, 0): 0, (9, 1): 1, (10, 0): 2, (10, 1): 3, (11, 0): 4, (12, 0): 5, (12, 1): 6, (13, 0): 7}
H_UNITS_AT = {(2, 0): 0, (2, 1): 1, (3, 0): 2, (4, 0): 3, (8, 1): 7, (10, 1): 9, (12, 1): 11, (14, 1): 13}
H_EVAC = {**{c: 2 * c + 2 for c in range(10)}, 11: 22, 13: 24}
H_SILU = {10: 2, 12: 4, 14: 6, 15: 8}


class At:

    def __init__(self, s, turn=None):
        self.s, self.turn = s, turn
        self.raw, self.spl = s % NRAW, s % NSPL

    def plus(self, n):
        return At(self.s + n, self.turn)

    def count(self, n=0):
        return self.s + 1 + n if self.turn is None else self.turn * NSPL + (self.s + 1 + n)

    def raw_count(self):
        base = 32 * (self.s // NRAW + 1)
        return base if self.turn is None else self.turn * (32 * NSPL // NRAW) + base


def psum_units(u):
    return u + 1 - (4 if u >= 4 * T["HC"] else 0)


def program(nc, A, out):
    ctx = ExitStack()
    with ctx:
        def sb(name, shape, dt=F32):
            return ctx.enter_context(nc.sbuf_tensor(name, shape, dt))

        def sem(name):
            return ctx.enter_context(nc.semaphore(name))

        w_raw = sb("w_raw", [P, NRAW, SLOT])
        w_hi = sb("w_hi", [P, NSPL, SLOT], F32R)
        w_lo = sb("w_lo", [P, NSPL, SLOT], F32R)
        xT_hi = sb("xT_hi", [P, KT, TILES * P], F32R)
        xT_lo = sb("xT_lo", [P, KT, TILES * P], F32R)
        hT_hi = sb("hT_hi", [P, 2, TILES * P], F32R)
        hT_lo = sb("hT_lo", [P, 2, TILES * P], F32R)
        pT_hi = sb("pT_hi", [P, 2, TILES * P], F32R)
        pT_lo = sb("pT_lo", [P, 2, TILES * P], F32R)
        x = sb("x_res", [P, TILES, D])
        scaled = sb("scaled", [P, 2, 512])
        squares = sb("squares", [P, D], BF16)
        ident = sb("ident", [P, P])
        causal = sb("causal", [P, LCOLS])
        upto = sb("upto", [P, P])
        ones = sb("ones", [P, P])
        last_row = sb("last_row", [P, P])
        gcol = sb("gcol", [P, 168])
        ssq = sb("ssq", [P, 40])
        meansq = sb("meansq", [P, 40])
        zed = sb("zed", [P, 40])
        nt_ = sb("nt_", [P, 16])
        rstd = sb("rstd", [P, 20])
        wg_raw = sb("wg_raw", [P, KT, 8])
        wg_hi = sb("wg_hi", [P, KT, 8], F32R)
        wg_lo = sb("wg_lo", [P, KT, 8], F32R)
        rel = sb("rel", [P, LCOLS])
        times = sb("times", [P, LCOLS])
        ARENA = 13856
        arena = sb("arena", [P, ARENA])

        def area(at, *shape):
            n = int(np.prod(shape))
            assert at + n <= ARENA, (at, shape)
            v = arena[:, at:at + n]
            if len(shape) == 2:
                v = v.rearrange("p (a b) -> p a b", a=shape[0])
            if len(shape) == 3:
                v = v.rearrange("p (a b c) -> p a b c", a=shape[0], b=shape[1])
            return v

        gain_bc = area(0, D)
        ytmp = area(1024, TILES, 512)
        sg = area(2048, TILES, CH)
        hs = area(2560, TILES, CH)
        gate_sb = area(3072, TILES, D)
        hb = area(5120, TILES, D)
        p_nat = area(5120, TILES, 256)
        kT = area(11776, 8, 256)
        v_sh = area(9728, TILES, D)
        kn = area(3072, TILES, D)
        qn = area(2048, TILES, D)
        qT = area(4096, 8, 256)
        sc_ = area(6144, 2, 768)
        dif = area(7680, 2, LCOLS)
        difT = area(8448, 2, LCOLS)
        lamv = area(9216, 256)
        lamp = area(9472, 8)
        subln = area(9500, 1)
        dstat = area(9632, 2, 16)
        hstat = area(9664, 64)
        m_qn = area(2048, TILES, 512)
        m_kn = area(3072, TILES, 512)
        m_qT = area(4096, MH, 256)
        m_kT = area(5120, MH, 256)
        m_v = area(6144, TILES, D)
        m_sig = area(8192, TILES, D)
        m_h = area(10240, TILES, D)
        m_am = area(12288, TILES, 512)
        m_PT = (area(3584, 512), area(13312, 512))
        m_C = area(2048, D)
        m_ksc = area(1280, 512)
        at = 1024
        m_g = area(at, TILES, 8)
        (m_e, m_l, m_lf, m_b, m_a, m_mx, m_negmx, m_last, m_lrow, m_exp0, m_exp1, m_den, m_rden, m_hssq, m_hmean,
         m_hz, m_prev, m_n, m_qn_den) = (area(at + 16 + 8 * i, 8 if i < 16 else 4) for i in range(19))
        m_diag = area(1280, 512)
        m_gT = arena[0:8, 1280:1536]
        h_v = area(0, TILES, D)
        h_kT = area(2048, 8, 256)
        h_qT = area(4096, 8, 256)
        h_o = area(4096, 8, TILES, P)
        h_s = area(6144, 2, TILES, 512)
        h_uT = area(8192, 8, 256)
        h_zT = area(10240, 8, 256)
        h_sc = area(12288, 2, LCOLS)
        h_pT = area(13056, 2, LCOLS)
        h_mx = area(13824, 2, 4)
        h_den = area(13832, 4, 2)
        h_rden = area(13840, 4, 2)
        h_gc = area(0, TILES, D)
        h_ga = area(2048, TILES, D)
        h_bm = area(8192, 2 * D)
        h_m = area(6144, TILES, D)
        f_gain = area(8192, D)
        f_out = area(10240, TILES, D)
        H_UNITS = {0: h_qT[:, 0:4], 1: h_qT[:, 4:8], 2: h_kT[:, 0:4], 3: h_kT[:, 4:8], 7: h_uT[:, 0:4],
                   9: h_uT[:, 4:8], 11: None, 13: None}
        rows1 = area(8192, P)
        rows2 = area(8320, P)
        iota_i = arena[:, 8448:8448 + LCOLS].bitcast(I32)
        iand_i = arena[:, 8832:8832 + 2 * LCOLS].bitcast(I32)
        build = area(9600, 4, LCOLS)
        bg_bc = sb("bg_bc", [P, 8])

        acc = ctx.enter_context(nc.psum_tensor("acc", [P, TILES, D], F32))
        gu = ctx.enter_context(nc.psum_tensor("gu", [P, TILES, 512], F32))
        tb = ctx.enter_context(nc.psum_tensor("tb", [P, 2, 512], F32))

        raw_landed = [sem(f"raw_landed{i}") for i in range(NRAW)]
        hi_ready = sem("hi_ready")
        lo_half_ready = sem("lo_half_ready")
        lo_ready = sem("lo_ready")
        tile0_used = sem("tile0_used")
        slot_used = sem("slot_used")
        t_in_psum = sem("t_in_psum")
        t_scaled = sem("t_scaled")
        t_hi_ready = sem("t_hi_ready")
        t_lo_ready = sem("t_lo_ready")
        sums_ready = sem("sums_ready")
        rstd_ready = sem("rstd_ready")
        x_ready = sem("x_ready")
        x_landed = [sem(f"x_landed{t}") for t in range(TILES)]
        dve_link = sem("dve_link")
        act_link = sem("act_link")
        silu_ready = sem("silu_ready")
        h_ready = sem("h_ready")
        ht_in_psum = sem("ht_in_psum")
        ht_hi_ready = sem("ht_hi_ready")
        ht_lo_ready = sem("ht_lo_ready")
        consts_ready = sem("consts_ready")
        tables_ready = sem("tables_ready")
        gain_landed = sem("gain_landed")
        rows1_landed = sem("rows1_landed")
        rows2_landed = sem("rows2_landed")
        wg_landed = sem("wg_landed")
        gcol_in_psum = sem("gcol_in_psum")
        gcol_ready = sem("gcol_ready")
        p_landed = sem("p_landed")
        pt_in_psum = sem("pt_in_psum")
        pt_hi_ready = sem("pt_hi_ready")
        pt_lo_ready = sem("pt_lo_ready")
        gate_ready = sem("gate_ready")
        hb_ready = sem("hb_ready")
        out_ready = sem("out_ready")
        out_landed = sem("out_landed")
        kv_copied = sem("kv_copied")
        kt_in_psum = sem("kt_in_psum")
        kt_ready = sem("kt_ready")

        def pair(c, t):
            return (gu[:, t, :], acc[:, t, 0:512], acc[:, t, 512:1024])[c % 3]

        def x_count(n, t, half):
            return 4 * n + 2 * t + half + 1

        def tok(t):
            return slice(t * P, (t + 1) * P)

        def t_bank(q, t, half):
            return acc[:, t, 512 * half:512 * half + 512] if q in ("KV", "HI", "HA", "HO") else tb[:, half, :]

        def ht_count(f, n, t=0):
            return (NIT + 1) * f + n + 1 + t

        wg_split = sem("wg_split")
        m_gt_in_psum = sem("m_gt_in_psum")
        m_gt_ready = sem("m_gt_ready")
        m_gates_in_psum = sem("m_gates_in_psum")
        m_copied = sem("m_copied")
        m_o_gate = sem("m_o_gate")
        m_absf = sem("m_absf")
        m_softlog = sem("m_softlog")
        m_logf = sem("m_logf")
        m_cum = sem("m_cum")
        m_diag_ready = sem("m_diag_ready")
        m_spread = sem("m_spread")
        m_am_ready = sem("m_am_ready")
        m_last_rhs = sem("m_last_rhs")
        m_last_in_psum = sem("m_last_in_psum")
        m_exps = sem("m_exps")
        m_exped = sem("m_exped")
        m_w_ready = sem("m_w_ready")
        m_pl_in_psum = sem("m_pl_in_psum")
        m_pl_ready = sem("m_pl_ready")
        m_ksc_ready = sem("m_ksc_ready")
        m_state_in_psum = sem("m_state_in_psum")
        m_state_ready = sem("m_state_ready")
        m_inter_in_psum = sem("m_inter_in_psum")
        m_qn_den_ready = sem("m_qn_den_ready")
        m_scores_in_psum = sem("m_scores_in_psum")
        m_p_ready = sem("m_p_ready")
        m_pt_in_psum = sem("m_pt_in_psum")
        m_pt_ready = sem("m_pt_ready")
        m_num_in_psum = sem("m_num_in_psum")
        m_h_ready = sem("m_h_ready")
        m_hsums = sem("m_hsums")
        m_y_ready = sem("m_y_ready")
        d_landed = sem("d_landed")
        d_lam = sem("d_lam")
        d_lamexp = sem("d_lamexp")
        d_qn_ready = sem("d_qn_ready")
        d_pl_in_psum = sem("d_pl_in_psum")
        d_pl_ready = sem("d_pl_ready")
        d_scores = sem("d_scores")
        d_negmax = sem("d_negmax")
        d_exped = sem("d_exped")
        d_dif_ready = sem("d_dif_ready")
        d_dt_in_psum = sem("d_dt_in_psum")
        d_dt_ready = sem("d_dt_ready")
        d_o_in_psum = sem("d_o_in_psum")
        d_o_ready = sem("d_o_ready")
        d_y_ready = sem("d_y_ready")
        h_evac = sem("h_evac")
        h_pl_in_psum = sem("h_pl_in_psum")
        h_pl_ready = sem("h_pl_ready")
        h_scores = sem("h_scores")
        h_negmax = sem("h_negmax")
        h_exped = sem("h_exped")
        h_p_ready = sem("h_p_ready")
        h_pt_in_psum = sem("h_pt_in_psum")
        h_pt_ready = sem("h_pt_ready")
        h_pv_in_psum = sem("h_pv_in_psum")
        h_o_ready = sem("h_o_ready")
        h_silu = sem("h_silu")
        h_conv = sem("h_conv")
        h_z_ready = sem("h_z_ready")
        h_gated = sem("h_gated")
        h_bm_landed = sem("h_bm_landed")
        h_gpre = sem("h_gpre")
        h_sig = sem("h_sig")
        h_m_ready = sem("h_m_ready")
        f_gain_landed = sem("f_gain_landed")

        block = ctx.enter_context(nc.Block())

        @block.sync
        def _(sp):
            def small_loads():
                sp.dma_start(rows2[0:8], A["kv_norm"].rearrange("(k c) -> k c", c=P)).then_inc(rows2_landed, 16)
                sp.dma_start(rows2[8:16], A["norm_g_2"][0].rearrange("(k c) -> k c", c=P)
                             ).then_inc(rows2_landed, 16)
                sp.dma_start(rows2[16:40], A["conv_w_2"][0].rearrange("w (k c) -> (w k) c", c=P)
                             ).then_inc(rows2_landed, 16)
                sp.dma_start(p_nat, A["p"][0, 0].rearrange("(t p) c -> p t c", p=P)).then_inc(p_landed, 16)
                sp.dma_start(gain_bc, A["norm_g"][0, 1].rearrange("(o d) -> o d", o=1).broadcast_to([P, D])
                             ).then_inc(gain_landed, 16)
                sp.dma_start(bg_bc[:], A["mlstm_b_gates"].broadcast_to([P, 8])).then_inc(wg_landed, 16)
                sp.dma_start(wg_raw[:], A["mlstm_w_in"][0].rearrange("(k p) c -> p k c", p=P)[:, :, 3072:3080]
                             ).then_inc(wg_landed, 16)

            def load(slot, halves):
                if slot.turn is None and slot.s == NRAW:
                    small_loads()
                    sp.wait_ge(lo_half_ready, 1)
                if slot.turn is not None or slot.s >= NRAW:
                    sp.wait_ge(lo_ready, slot.count(-NRAW))
                for view, src in halves:
                    sp.dma_start(view, src).then_inc(raw_landed[slot.raw], 16)

            def ffn(name, w_in, w_out):
                up_src = w_in.rearrange("(k p) c -> p k c", p=P)
                down_src = w_out.rearrange("(f p) c -> p f c", p=P)

                def up(n, slot, half):
                    dst = w_raw[:, slot.raw, :].rearrange("p (k u c) -> p k u c", k=4, u=2)
                    load(slot, [(dst[:, :, u, :], up_src[:, 4 * half:4 * half + 4, bass.ds(n * CH + u * FF, CH)])
                                for u in range(2)])

                def down(n, slot):
                    dst = w_raw[:, slot.raw, :].rearrange("p (f c) -> p f c", f=2)
                    load(slot, [(dst[:, f:f + 1, :], down_src[:, bass.ds(n * 2 + f, 1), :]) for f in range(2)])

                s0 = S[name]
                up(0, At(s0), 0)
                up(0, At(s0 + 1), 1)
                up(1, At(s0 + 2), 0)
                up(1, At(s0 + 3), 1)
                down(0, At(s0 + 4))
                with sp.Fori(0, (NIT - 3) // 2) as i:
                    for d in (0, 1):
                        a = At(s0 + 5 + 3 * d, i)
                        up(i * 2 + (2 + d), a, 0)
                        up(i * 2 + (2 + d), a.plus(1), 1)
                        down(i * 2 + (1 + d), a.plus(2))
                a = At(s0 + FFN_SLOTS - 4)
                up(NIT - 1, a, 0)
                up(NIT - 1, a.plus(1), 1)
                down(NIT - 2, a.plus(2))
                down(NIT - 1, a.plus(3))

            def linear(s0, w, cols, halves_first=False):
                src = w.rearrange("(k p) c -> p k c", p=P)
                order = [(c, j) for c in cols for j in range(2)]
                if halves_first:
                    order = [(c, j) for j in range(2) for c in cols]
                for i, (col, j) in enumerate(order):
                    slot = At(s0 + i)
                    dst = w_raw[:, slot.raw, :].rearrange("p (k c) -> p k c", k=4)
                    load(slot, [(dst[:, 2 * k:2 * k + 2, :],
                                 src[:, 4 * j + 2 * k:4 * j + 2 * k + 2, col:col + 512]) for k in range(2)])

            def ple(name, w_proj, w_gate):
                slot = At(S[name])
                dst = w_raw[:, slot.raw, :].rearrange("p (f c) -> p f c", f=2)
                src = w_proj.rearrange("(f p) c -> p f c", p=P)
                load(slot, [(dst[:, f, :], src[:, f, :]) for f in range(2)])
                linear(S[name] + 1, w_gate, (0, 512))

            both = (0, 512)
            ffn("F0", A["w_ffn_in"][0, 0], A["w_ffn_out"][0, 0])
            linear(S["MI"], A["mlstm_w_in"][0], [512 * c for c in range(6)])
            linear(S["MO"], A["mlstm_w_out"][0], both)
            ffn("F1", A["w_ffn_in"][0, 1], A["w_ffn_out"][0, 1])
            ple("P0", A["w_ple_proj"][0], A["w_ple_gate"][0])
            linear(S["KV"], A["w_kv"], [512 * c for c in range(4)])
            ffn("F2", A["w_ffn_in"][1, 0], A["w_ffn_out"][1, 0])
            linear(S["DQ"], A["diff_w_q"][0], both)
            linear(S["DO"], A["diff_w_out"][0], both, halves_first=True)
            ffn("F3", A["w_ffn_in"][1, 1], A["w_ffn_out"][1, 1])
            ple("P1", A["w_ple_proj"][1], A["w_ple_gate"][1])
            linear(S["HI"], A["w_in_2"][0], [512 * c for c in H_ORDER])
            linear(S["HC"], A["w_out_conv_2"][0], both)
            linear(S["HA"], A["w_out_attn_2"][0], both)
            linear(S["HO"], A["w_o_2"][0], both)
            for t in range(TILES):
                sp.wait_ge(out_ready, t + 1)
                sp.dma_start(out[0, tok(t), :], f_out[:, t, :]).then_inc(out_landed, 16)
            sp.wait_ge(out_landed, 16 * TILES)

        @block.gpsimd
        def _(pool):
            pool.memset(ident[:], 0.0).then_inc(consts_ready, 1)
            pool.memset(causal[:], 0.0).then_inc(consts_ready, 1)
            pool.memset(upto[:], 1.0).then_inc(consts_ready, 1)
            pool.memset(ones[:], 1.0).then_inc(consts_ready, 1)
            pool.memset(last_row[:], 0.0).then_inc(consts_ready, 1)
            pool.iota(iota_i[:, 0:P], pattern=[[-1, P]], base=256, channel_multiplier=1).then_inc(consts_ready, 1)
            pool.iota(iota_i[:, P:LCOLS], pattern=[[-1, 2 * P]], base=256 + P,
                      channel_multiplier=1).then_inc(consts_ready, 1)
            pool.wait_ge(consts_ready, 7)
            pool.affine_select(out=ident[:], in_=ident[:], compare_op=ALU.not_equal, fill=1.0, base=0,
                               pattern=[[-1, P]], channel_multiplier=1).then_inc(consts_ready, 1)
            pool.affine_select(out=causal[:, 0:P], in_=causal[:, 0:P], compare_op=ALU.is_ge, fill=FAR, base=0,
                               pattern=[[-1, P]], channel_multiplier=1).then_inc(consts_ready, 1)
            pool.affine_select(out=causal[:, P:LCOLS], in_=causal[:, P:LCOLS], compare_op=ALU.is_ge, fill=FAR,
                               base=P, pattern=[[-1, 2 * P]], channel_multiplier=1).then_inc(consts_ready, 1)
            pool.affine_select(out=upto[:], in_=upto[:], compare_op=ALU.is_ge, fill=0.0, base=0,
                               pattern=[[1, P]], channel_multiplier=-1).then_inc(consts_ready, 1)
            pool.affine_select(out=last_row[:], in_=last_row[:], compare_op=ALU.not_equal, fill=1.0,
                               base=-(P - 1), pattern=[[0, P]], channel_multiplier=1).then_inc(consts_ready, 1)

            def subtract(slot):
                pool.wait_ge(hi_ready, slot.count())
                pool.tensor_tensor(w_lo[:, slot.spl, :], w_raw[:, slot.raw, :],
                                   w_hi[:, slot.spl, :].bitcast(F32), ALU.subtract).then_inc(lo_ready, 1)

            pool.wait_ge(hi_ready, 1)
            pool.tensor_tensor(w_lo[:, 0, 0:SLOT // 2], w_raw[:, 0, 0:SLOT // 2],
                               w_hi[:, 0, 0:SLOT // 2].bitcast(F32), ALU.subtract).then_inc(lo_ready, 1)
            pool.wait_ge(lo_ready, 2)
            for s in range(2, NSPL):
                subtract(At(s))
            with pool.Fori(0, TOTAL // NSPL - 1) as i:
                for j in range(NSPL):
                    subtract(At(NSPL + j, i))
            for s in range(TOTAL - TOTAL % NSPL, TOTAL):
                subtract(At(s))

        @block.scalar
        def _(act):
            linked = [0]

            def link(ins):
                linked[0] += 1
                ins.then_inc(act_link, 1)
                act.wait_ge(act_link, linked[0])

            def round_hi(slot):
                act.wait_ge(raw_landed[slot.raw], slot.raw_count())
                if slot.turn is not None or slot.s >= NSPL:
                    act.wait_ge(slot_used, slot.count(-NSPL))
                nc.scalar.copy(w_hi[:, slot.spl, :], w_raw[:, slot.raw, :]).then_inc(hi_ready, 1)

            def ahead(slot):
                if slot.turn is not None or slot.s + AHEAD < TOTAL:
                    round_hi(slot.plus(AHEAD))

            def load_gain(row):
                act.dma_start(gain_bc, row.rearrange("(o d) -> o d", o=1).broadcast_to([P, D])
                              ).then_inc(gain_landed, 16)

            def sum_of(j, t, src):
                if 2 * j + t:
                    act.wait_ge(sums_ready, 2 * j + t)
                nc.scalar.activation(squares[:], src, ACT.Square,
                                     accum_out=ssq[:, 2 * j + t:2 * j + t + 1]).then_inc(sums_ready, 1)

            def pre_sum(name, t):
                m = PRE[name]
                if m == 0:
                    act.wait_ge(x_landed[t], 16)
                else:
                    act.wait_ge(x_ready, x_count(m - 1, t, 1))
                sum_of(2 * m, t, x[:, t, :])

            def t_hi(q, t):
                for half in range(2):
                    u = 4 * T[q] + 2 * t + half
                    act.wait_ge(t_scaled, psum_units(u))
                    nc.scalar.copy(xT_hi[:, 4 * half:4 * half + 4, tok(t)],
                                   scaled[:, u % 2, :].rearrange("p (k c) -> p k c", k=4)
                                   ).then_inc(t_hi_ready, 1)

            def boundary(following, post_sum, between=lambda: None, late=lambda: None):
                post_sum(0)
                between()
                t_hi(following, 0)
                late()
                post_sum(1)
                pre_sum(following, 0)
                ahead(At(S[following]))
                t_hi(following, 1)
                pre_sum(following, 1)
                act.wait_ge(sums_ready, 4 * PRE[following] + 2)

            def acc_sum(name, last_slot):
                def post_sum(t):
                    act.wait_ge((tile0_used, slot_used)[t], last_slot + 1)
                    sum_of(2 * POST[name] + 1, t, acc[:, t, :])
                return post_sum

            def warm(func):
                link(nc.scalar.activation(squares[:, 0:1], ones[:, 0:1], func))

            def ffn(name, following):
                f, m, s0 = FFN_NO[name], PRE[name], S[name]
                warm(ACT.Silu)

                def iteration(n, turn, a, has_down):
                    b = a.plus(1)

                    def turns(per, v):
                        return v if turn is None else turn * per + v

                    def silu(t):
                        act.wait_ge((tile0_used, slot_used)[t], b.count())
                        if n:
                            act.wait_ge(h_ready, turns(4, 2 * NIT * f + 2 * (n - 1) + t + 1))
                        else:
                            act.wait_ge(rstd_ready, 2 * m + t + 1)
                        nc.scalar.activation(sg[:, t, :], gu[:, t, 0:CH], ACT.Silu,
                                             scale=rstd[:, 2 * m + t:2 * m + t + 1]).then_inc(silu_ready, 1)

                    if n:
                        ahead(a)
                        ahead(b)
                    silu(0)
                    if n == 0 and name != "F0":
                        ahead(b)
                    if n < NIT - 1:
                        silu(1)
                        if n == 0 and name == "F0":
                            ahead(b)
                        if has_down:
                            ahead(a.plus(2))
                        act.wait_ge(ht_in_psum, turns(2, ht_count(f, n)))
                        nc.scalar.copy(hT_hi[:], tb[:, 0, :].rearrange("p (k c) -> p k c", k=2)
                                       ).then_inc(ht_hi_ready, 1)
                        return

                    def hidden_hi(t):
                        act.wait_ge(ht_in_psum, ht_count(f, n, t))
                        nc.scalar.copy((hT_hi, xT_hi)[t][:, 0:2, tok(t)],
                                       tb[:, t, 0:2 * P].rearrange("p (k c) -> p k c", k=2)
                                       ).then_inc(ht_hi_ready, 1)

                    def second_tile():
                        silu(1)
                        ahead(a.plus(3))
                        hidden_hi(1)

                    hidden_hi(0)
                    ahead(a.plus(2))
                    boundary(following, acc_sum(name, s0 + FFN_SLOTS - 1), second_tile)

                iteration(0, None, At(s0), False)
                iteration(1, None, At(s0 + 2), True)
                with act.Fori(0, (NIT - 3) // 2) as i:
                    for d in (0, 1):
                        iteration(2 + d, i, At(s0 + 5 + 3 * d, i), True)
                iteration(NIT - 1, None, At(s0 + FFN_SLOTS - 4), True)

            def p_hi(layer):
                act.wait_ge(pt_in_psum, layer + 1)
                nc.scalar.copy(pT_hi[:], (acc[:, 1, 0:512], tb[:, 1, :])[layer].rearrange("p (k c) -> p k c", k=2)
                               ).then_inc(pt_hi_ready, 1)

            def ple(name, layer, following):
                m, s0 = PRE[name], S[name]
                ahead(At(s0 + 1))

                def gate(t):
                    act.wait_ge(rstd_ready, 2 * m + t + 1)
                    for c in range(2):
                        act.wait_ge((tile0_used, slot_used)[t], s0 + 1 + 2 * c + 2)
                        nc.scalar.activation(gate_sb[:, t, 512 * c:512 * c + 512], (gu, tb)[c][:, t, :],
                                             ACT.Sigmoid, scale=rstd[:, 2 * m + t:2 * m + t + 1]
                                             ).then_inc(gate_ready, 1)

                def post_sum(t):
                    if t:
                        ahead(At(s0 + 4))
                    gate(t)
                    act.wait_ge(hb_ready, 2 * layer + t + 1)
                    sum_of(2 * POST[name] + 1, t, hb[:, t, :])

                def second_tile():
                    ahead(At(s0 + 2))
                    ahead(At(s0 + 3))

                boundary(following, post_sum, second_tile)

            def out_linear(name, following):
                s0 = S[name]

                ahead(At(s0))
                ahead(At(s0 + 1))
                boundary(following, acc_sum(name, s0 + 3), lambda: ahead(At(s0 + 2)), lambda: ahead(At(s0 + 3)))

            def mlstm():
                m, s0 = PRE["MI"], S["MI"]
                for j in range(1, 4):
                    ahead(At(s0 + j))
                act.wait_ge(m_absf, 1)
                link(nc.scalar.activation(m_e, m_e, ACT.Exp, scale=-1.0))
                nc.scalar.activation(m_l, m_e, ACT.Ln, bias=1.0).then_inc(m_softlog, 1)
                for j in range(4, 8):
                    ahead(At(s0 + j))
                act.wait_ge(m_am_ready, 1)
                for h in range(MH):
                    ins = nc.scalar.activation(m_am[:, 0, tok(h)], m_am[:, 0, tok(h)], ACT.Exp,
                                               bias=m_negmx[:, h:h + 1])
                ins.then_inc(m_w_ready, 1)
                act.wait_ge(m_exps, 1)
                nc.scalar.activation(m_exp0, m_exp0, ACT.Exp).then_inc(m_exped, 1)
                ahead(At(s0 + 8))
                act.wait_ge(m_am_ready, 2)
                for h in range(MH):
                    ins = nc.scalar.activation(m_am[:, 1, tok(h)], m_am[:, 1, tok(h)], ACT.Exp,
                                               bias=m_negmx[:, 4 + h:5 + h])
                ins.then_inc(m_w_ready, 1)
                act.wait_ge(m_exps, 2)
                nc.scalar.activation(m_exp1, m_exp1, ACT.Exp).then_inc(m_exped, 1)
                for w in range(4):
                    act.wait_ge(m_pl_in_psum, w + 1)
                    dst = (m_qT, m_kT)[w // 2][:, :, tok(w % 2)]
                    nc.scalar.copy(dst, tb[:, w % 2, :].rearrange("p (h c) -> p h c", h=MH)
                                   ).then_inc(m_pl_ready, 1)
                    if w == 1:
                        ahead(At(s0 + 9))
                ahead(At(s0 + 10))
                act.wait_ge(m_state_in_psum, 1)
                nc.scalar.copy(m_C.rearrange("p (a b) -> p a b", a=2), gu[:]).then_inc(m_state_ready, 1)

                def output_gate(c, t):
                    act.wait_ge((tile0_used, slot_used)[t], s0 + 2 * c + 2)
                    nc.scalar.activation(m_sig[:, t, 512 * (c - 4):512 * (c - 4) + 512], pair(c, t),
                                         ACT.Sigmoid, scale=rstd[:, 2 * m + t:2 * m + t + 1]
                                         ).then_inc(m_o_gate, 1)

                def turned_p(t):
                    act.wait_ge(m_pt_in_psum, t + 1)
                    nc.scalar.copy(m_PT[t], tb[:, t, :]).then_inc(m_pt_ready, 1)

                def head_sums(t):
                    act.wait_ge(m_h_ready, t + 1)
                    for h in range(MH):
                        ins = nc.scalar.activation(squares[:, MDV * h:MDV * h + MDV],
                                                   m_h[:, t, MDV * h:MDV * h + MDV], ACT.Square,
                                                   accum_out=m_hssq[:, 4 * t + h:4 * t + h + 1])
                    ins.then_inc(m_hsums, 1)
                    act.wait_ge(m_hsums, t + 1)

                output_gate(4, 0)
                turned_p(0)
                output_gate(4, 1)
                turned_p(1)
                head_sums(0)
                ahead(At(s0 + 11))
                output_gate(5, 0)
                t_hi("MO", 0)
                head_sums(1)
                output_gate(5, 1)
                t_hi("MO", 1)
                load_gain(A["norm_g"][0, 3])
                out_linear("MO", "F1")

            def diff():
                s0 = S["DQ"]
                ahead(At(s0 + 1))
                act.wait_ge(d_lam, 1)
                nc.scalar.activation(lamp[:, 2:4], lamp[:, 0:2], ACT.Exp).then_inc(d_lamexp, 1)
                ahead(At(s0 + 2))
                for w in range(4):
                    if w == 2:
                        ahead(At(s0 + 3))
                    act.wait_ge(d_pl_in_psum, w + 1)
                    nc.scalar.copy(qT[:, 4 * (w % 2):4 * (w % 2) + 4, tok(w // 2)],
                                   tb[:, w % 2, :].rearrange("p (k c) -> p k c", k=4)).then_inc(d_pl_ready, 1)
                for step in range(DH + 3):
                    h = step
                    if h < DH:
                        act.wait_ge(d_negmax, 4 * h + 4)
                        for t in range(TILES):
                            for a in range(2):
                                e = sc_[:, h % 2, LCOLS * a + P * t:LCOLS * a + P * t + P * (t + 1)]
                                i = 2 * t + a
                                ins = nc.scalar.activation(e, e, ACT.Exp, scale=-1.0, bias=dstat[:, h % 2, 4 + i:5 + i],
                                                           accum_out=dstat[:, h % 2, 8 + i:9 + i])
                        ins.then_inc(d_exped, 1)
                    h = step - 2
                    if 0 <= h < DH:
                        act.wait_ge(d_dt_in_psum, h + 1)
                        if h >= 2:
                            act.wait_ge(d_o_in_psum, h - 1)
                        nc.scalar.copy(difT[:, h % 2, :], acc[:, 0, 512 * (h % 2):512 * (h % 2) + LCOLS]
                                       ).then_inc(d_dt_ready, 1)
                    h = step - 3
                    if 0 <= h < DH:
                        act.wait_ge(d_o_in_psum, h + 1)
                        src = acc[:, 1, 512 * (h % 2):512 * (h % 2) + 2 * P].rearrange("p (t c) -> p t c", t=2)
                        nc.scalar.copy(qn[:, :, tok(h)], src)
                        if h:
                            act.wait_ge(d_o_ready, h)
                        for t in range(TILES):
                            i = 8 * (h // 4) + 4 * t + h % 4
                            ins = nc.scalar.activation(squares[:, tok(t)], src[:, t, :], ACT.Square,
                                                       accum_out=hstat[:, i:i + 1])
                        ins.then_inc(d_o_ready, 1)
                act.wait_ge(d_o_ready, DH)
                t_hi("DO", 0)
                t_hi("DO", 1)
                out_linear("DO", "F3")

            def hybrid():
                m, s0 = PRE["HI"], S["HI"]
                act.wait_ge(rstd_ready, 2 * m + 2)

                def r(t):
                    return rstd[:, 2 * m + t:2 * m + t + 1]

                def step(k):
                    h = k
                    if h < AH:
                        act.wait_ge(h_negmax, h + 1)
                        at = 0
                        for t in range(TILES):
                            e = h_sc[:, h % 2, at:at + P * (t + 1)]
                            ins = nc.scalar.activation(e, e, ACT.Exp, bias=h_mx[:, h % 2, 2 + t:3 + t])
                            at += P * (t + 1)
                        ins.then_inc(h_exped, 1)
                    h = k - 2
                    if 0 <= h < AH:
                        act.wait_ge(h_pt_in_psum, h + 1)
                        if h >= 2:
                            act.wait_ge(h_pv_in_psum, h - 1)
                        nc.scalar.copy(h_pT[:, h % 2, :], tb[:, 0, 0:LCOLS]).then_inc(h_pt_ready, 1)

                def units(c):
                    dst = H_UNITS[c]
                    for t in range(TILES):
                        w = H_UNIT_NO[c] + t
                        act.wait_ge(h_pl_in_psum, w + 1)
                        nc.scalar.copy(dst[:, :, tok(t)], tb[:, 1, :].rearrange("p (k c) -> p k c", k=4)
                                       ).then_inc(h_pl_ready, 1)

                steps = 0
                for c in range(20):
                    for j in range(2):
                        if c + j and c < 18:
                            ahead(At(s0 + 2 * c + j))
                        if H_UNITS.get(H_UNITS_AT.get((c, j))) is not None:
                            units(H_UNITS_AT[c, j])
                        if c >= 5 and steps < AH + 3:
                            step(steps)
                            steps += 1
                    if c in (10, 12, 14, 15):
                        for t in range(TILES):
                            act.wait_ge((tile0_used, slot_used)[t], s0 + 2 * c + 2)
                            act.wait_ge(h_pl_in_psum, H_S_FREE[c] + t)
                            nc.scalar.activation(h_s[:, H_PLACE[c], t, :], acc[:, t, 512 * (c % 2):512 * (c % 2) + 512],
                                                 ACT.Silu, scale=r(t)).then_inc(h_silu, 1)
                    if c == 15:
                        act.wait_ge(h_conv, 8)
                        act.dma_start(h_bm, A["b_merge_2"].broadcast_to([P, 2 * D])).then_inc(h_bm_landed, 16)
                    if c == 17:
                        for cc in (16, 17):
                            for t in range(TILES):
                                g = h_gc[:, t, 512 * (cc % 2):512 * (cc % 2) + 512]
                                act.wait_ge(h_gpre, 2 * (cc - 16) + t + 1)
                                nc.scalar.activation(g, g, ACT.Sigmoid).then_inc(h_sig, 1)
                ahead(At(s0 + 36))
                ahead(At(s0 + 37))
                for t in range(TILES):
                    act.wait_ge((tile0_used, slot_used)[t], S["HC"])
                    act.wait_ge(h_z_ready, 4)
                    for half in range(2):
                        nc.scalar.copy(xT_hi[:, 4 * half:4 * half + 4, tok(t)],
                                       h_zT[:, 4 * half:4 * half + 4, tok(t)]).then_inc(t_hi_ready, 1)
                    if t == 0:
                        ahead(At(s0 + 38))
                        ahead(At(s0 + 39))
                    act.wait_ge(h_gpre, 4 + 2 * t + 2)
                    nc.scalar.activation(h_ga[:, t, :], h_ga[:, t, :], ACT.Sigmoid).then_inc(h_sig, 1)
                act.dma_start(f_gain, A["final_g_2"].rearrange("(o d) -> o d", o=1).broadcast_to([P, D])
                              ).then_inc(f_gain_landed, 16)
                ahead(At(S["HC"]))
                ahead(At(S["HC"] + 1))
                ahead(At(S["HC"] + 2))
                t_hi("HA", 0)
                ahead(At(S["HC"] + 3))
                t_hi("HA", 1)
                for j in range(3):
                    ahead(At(S["HA"] + j))
                t_hi("HO", 0)
                ahead(At(S["HA"] + 3))
                t_hi("HO", 1)
                for t in range(TILES):
                    act.wait_ge(x_ready, x_count(8, t, 1))
                    sum_of(FINAL_SUM, t, x[:, t, :])

            act.dma_start(x[:, 0, :], A["x"][0, tok(0), :]).then_inc(x_landed[0], 16)
            act.dma_start(rows1, A["norm_g"].rearrange("l n (k c) -> (l n k) c", c=P)).then_inc(rows1_landed, 16)
            act.dma_start(x[:, 1, :], A["x"][0, tok(1), :]).then_inc(x_landed[1], 16)
            act.wait_ge(consts_ready, 12)
            warm(ACT.Silu)
            round_hi(At(0))
            t_hi("F0", 0)
            round_hi(At(1))
            round_hi(At(2))
            t_hi("F0", 1)
            pre_sum("F0", 0)
            round_hi(At(3))
            pre_sum("F0", 1)
            p_hi(0)
            act.wait_ge(wg_landed, 32)
            nc.scalar.copy(wg_hi[:], wg_raw[:]).then_inc(wg_split, 1)
            act.wait_ge(sums_ready, 2)
            ahead(At(0))
            ffn("F0", "MI")
            act.wait_ge(x_ready, x_count(0, 1, 1))
            load_gain(A["mlstm_head_norm"][0].rearrange("h d -> (h d)"))
            mlstm()
            act.wait_ge(x_ready, x_count(1, 1, 1))
            load_gain(A["norm_g"][0, 5])
            ffn("F1", "P0")
            act.wait_ge(x_ready, x_count(2, 1, 1))
            load_gain(A["norm_g"][0, 7])
            ple("P0", 0, "KV")
            act.wait_ge(x_ready, x_count(3, 1, 1))
            load_gain(A["norm_g"][1, 1])
            act.dma_start(p_nat, A["p"][1, 0].rearrange("(t p) c -> p t c", p=P)).then_inc(p_landed, 16)
            for j in range(1, 6):
                ahead(At(S["KV"] + j))
            for w in range(4):
                act.wait_ge(kt_in_psum, w + 1)
                nc.scalar.copy(kT[:, 4 * (w % 2):4 * (w % 2) + 4, tok(w // 2)],
                               acc[:, w % 2, 0:512].rearrange("p (k c) -> p k c", k=4)
                               ).then_inc(kt_ready, 1)
                if w == 1:
                    p_hi(1)
            ahead(At(S["KV"] + 6))
            t_hi("F2", 0)
            ahead(At(S["KV"] + 7))
            t_hi("F2", 1)
            ahead(At(S["F2"]))
            ffn("F2", "DQ")
            act.wait_ge(x_ready, x_count(4, 1, 1))
            load_gain(A["norm_g"][1, 3])
            act.dma_start(lamv, A["diff_lambda"][0].rearrange("(o a) d -> o (a d)", o=1).broadcast_to([P, 256])
                          ).then_inc(d_landed, 16)
            act.dma_start(subln, A["diff_subln"].rearrange("o d -> d o")).then_inc(d_landed, 16)
            diff()
            act.wait_ge(x_ready, x_count(5, 1, 1))
            load_gain(A["norm_g"][1, 5])
            ffn("F3", "P1")
            act.wait_ge(x_ready, x_count(6, 1, 1))
            load_gain(A["norm_g"][1, 7])
            ple("P1", 1, "HI")
            hybrid()

        @block.vector
        def _(dve):
            linked = [0]

            def link(ins):
                linked[0] += 1
                ins.then_inc(dve_link, 1)
                dve.wait_ge(dve_link, linked[0])

            v = nc.vector

            def rsqrt_steps(sums, mean, z, tmp, inv_n):
                link(v.tensor_scalar(mean, sums, inv_n, EPS, ALU.mult, ALU.add))
                link(v.tensor_scalar(z.bitcast(I32), mean.bitcast(I32), -0.5, MAGIC, ALU.mult, ALU.add))
                for c in (3.0, 12.0, 768.0):
                    if z.shape[1] == 1:
                        link(v.scalar_tensor_tensor(tmp, z, mean, z, ALU.mult, ALU.mult))
                    else:
                        link(v.tensor_tensor(tmp, z, mean, ALU.mult))
                        link(v.tensor_tensor(tmp, tmp, z, ALU.mult))
                    link(v.scalar_tensor_tensor(z, tmp, c, z, ALU.subtract, ALU.mult))

            def norm_steps(j, t):
                i = 2 * j + t
                dve.wait_ge(sums_ready, i + 1)
                rsqrt_steps(ssq[:, i:i + 1], meansq[:, i:i + 1], zed[:, i:i + 1], nt_[:, 0:1], 1.0 / D)

            def gain_of(q, half):
                g = GAIN[q] + 4 * half
                return gcol[:, g:g + 4].unsqueeze(2).broadcast_to([P, 4, P])

            def t_units(q, t, halves=(0, 1)):
                def scale(u):
                    dve.wait_ge(t_in_psum, psum_units(u))
                    if u >= 2:
                        dve.wait_ge(t_lo_ready, u - 1)
                    dst, src = scaled[:, u % 2, :], t_bank(q, t, u % 2)
                    if q in GAIN:
                        v.tensor_tensor(dst.rearrange("p (k c) -> p k c", k=4),
                                        src.rearrange("p (k c) -> p k c", k=4),
                                        gain_of(q, u % 2), ALU.mult).then_inc(t_scaled, 1)
                    elif q == "DO":
                        v.tensor_scalar(dst, src, subln, T_FACTOR[q], ALU.mult, ALU.mult).then_inc(t_scaled, 1)
                    else:
                        v.tensor_scalar(dst, src, T_FACTOR[q], None, ALU.mult).then_inc(t_scaled, 1)

                def low(u):
                    half = u % 2
                    dve.wait_ge(t_hi_ready, u + 1)
                    to = (slice(4 * half, 4 * half + 4), tok(t))
                    v.tensor_tensor(xT_lo[:, to[0], to[1]], scaled[:, u % 2, :].rearrange("p (k c) -> p k c", k=4),
                                    xT_hi[:, to[0], to[1]].bitcast(F32), ALU.subtract).then_inc(t_lo_ready, 1)

                for half in halves:
                    scale(4 * T[q] + 2 * t + half)
                for half in halves:
                    low(4 * T[q] + 2 * t + half)

            def pre_norm(name, t):
                m = PRE[name]
                norm_steps(2 * m, t)
                i = 4 * m + t
                v.tensor_scalar(rstd[:, 2 * m + t:2 * m + t + 1], zed[:, i:i + 1], ZS, None, ALU.mult
                                ).then_inc(rstd_ready, 1)

            def boundary(name, gain_no, weight, src, last_slot, following, before=None, between=None):
                n = POST[name]
                dve.wait_ge(gain_landed, 16 * gain_no)
                for t in range(TILES):
                    if before:
                        before(t)
                    else:
                        dve.wait_ge((tile0_used, slot_used)[t], last_slot + 1)
                    norm_steps(2 * n + 1, t)
                    i = 2 * (2 * n + 1) + t
                    for half in range(2):
                        cols = slice(512 * half, 512 * half + 512)
                        if between and not t:
                            between[half]()
                        if t or n:
                            dve.wait_ge(x_ready, x_count(n - (not t), not t, half))
                        link(v.scalar_tensor_tensor(ytmp[:, half, :], src[:, t, cols], zed[:, i:i + 1],
                                                    gain_bc[:, cols], ALU.mult, ALU.mult))
                        v.scalar_tensor_tensor(x[:, t, cols], ytmp[:, half, :], weight * ZS, x[:, t, cols],
                                               ALU.mult, ALU.add).then_inc(x_ready, 1)
                    if between and not t:
                        t_units(following, t, (0,))
                        t_units(following, t, (1,))
                    else:
                        t_units(following, t)
                pre_norm(following, 0)
                pre_norm(following, 1)

            def ffn(name, gain_no, following):
                f, m, s0 = FFN_NO[name], PRE[name], S[name]
                if name != "F2":
                    dve.wait_ge(rstd_ready, 2 * m + 2)

                def iteration(n, turn):
                    def turns(per, c):
                        return c if turn is None else turn * per + c

                    def hidden(t):
                        dve.wait_ge(silu_ready, turns(4, 2 * NIT * f + 2 * n + t + 1))
                        if n and t == 0:
                            dve.wait_ge(ht_in_psum, turns(2, ht_count(f, n - 1)))
                        v.scalar_tensor_tensor(hs[:, t, :], gu[:, t, CH:2 * CH], rstd[:, 2 * m + t:2 * m + t + 1],
                                               sg[:, t, :], ALU.mult, ALU.mult).then_inc(h_ready, 1)

                    hidden(0)
                    if n < NIT - 1:
                        hidden(1)
                        dve.wait_ge(ht_hi_ready, turns(2, ht_count(f, n)))
                        v.tensor_tensor(hT_lo[:], tb[:, 0, :].rearrange("p (k c) -> p k c", k=2),
                                        hT_hi[:].bitcast(F32), ALU.subtract).then_inc(ht_lo_ready, 1)
                        return

                    def hidden_lo(t):
                        dve.wait_ge(ht_hi_ready, ht_count(f, n, t))
                        v.tensor_tensor((hT_lo, xT_lo)[t][:, 0:2, tok(t)],
                                        tb[:, t, 0:2 * P].rearrange("p (k c) -> p k c", k=2),
                                        (hT_hi, xT_hi)[t][:, 0:2, tok(t)].bitcast(F32), ALU.subtract
                                        ).then_inc(ht_lo_ready, 1)

                    hidden_lo(0)
                    boundary(name, gain_no, 0.5, acc, s0 + FFN_SLOTS - 1, following,
                             between=(lambda: hidden(1), lambda: hidden_lo(1)))

                for n in range(2):
                    iteration(n, None)
                    if n == 0 and name == "F0":
                        build_tables()
                with dve.Fori(0, (NIT - 3) // 2) as i:
                    for d in (0, 1):
                        iteration(2 + d, i)
                iteration(NIT - 1, None)

            def p_lo(layer):
                dve.wait_ge(pt_hi_ready, layer + 1)
                v.tensor_tensor(pT_lo[:], (acc[:, 1, 0:512], tb[:, 1, :])[layer].rearrange("p (k c) -> p k c", k=2),
                                pT_hi[:].bitcast(F32), ALU.subtract).then_inc(pt_lo_ready, 1)

            def ple(name, layer, gain_no, following):
                def gated(t):
                    dve.wait_ge(gate_ready, 4 * layer + 2 * t + 2)
                    v.tensor_tensor(hb[:, t, :], acc[:, t, :], gate_sb[:, t, :], ALU.mult).then_inc(hb_ready, 1)
                    dve.wait_ge(hb_ready, 2 * layer + t + 1)
                boundary(name, gain_no, 1.0, hb, None, following, before=gated)

            def mlstm():
                m, s0 = PRE["MI"], S["MI"]
                dve.wait_ge(rstd_ready, 2 * m + 2)

                def r(t):
                    return rstd[:, 2 * m + t:2 * m + t + 1]

                def take(c):
                    for t in range(TILES):
                        dve.wait_ge((tile0_used, slot_used)[t], s0 + 2 * c + 2)
                        dst = (m_qn[:, t, :], m_kn[:, t, :], m_v[:, t, 0:512], m_v[:, t, 512:1024])[c]
                        if c == 1:
                            v.tensor_scalar(dst, pair(c, t), r(t), float(MDK) ** -0.5, ALU.mult, ALU.mult
                                            ).then_inc(m_copied, 1)
                        else:
                            v.tensor_scalar(dst, pair(c, t), r(t), None, ALU.mult).then_inc(m_copied, 1)

                take(0)
                dve.wait_ge(m_gt_in_psum, 1)
                v.tensor_copy(m_gT, tb[0:8, 1, 256:512]).then_inc(m_gt_ready, 1)
                dve.wait_ge(m_gates_in_psum, 1)
                for t in range(TILES):
                    ins = v.scalar_tensor_tensor(m_g[:, t, :], tb[:, 1, 8 * t:8 * t + 8], r(t), bg_bc[:],
                                                 ALU.mult, ALU.add)
                link(ins)
                li, f = m_g[:, :, 0:MH], m_g[:, :, MH:2 * MH]
                v.scalar_tensor_tensor(m_e.rearrange("p (t h) -> p t h", t=2), f, -1.0, f, ALU.mult, ALU.max
                                       ).then_inc(m_absf, 1)
                take(1)
                dve.wait_ge(m_softlog, 1)
                v.scalar_tensor_tensor(m_lf.rearrange("p (t h) -> p t h", t=2), f, 0.0,
                                       m_l.rearrange("p (t h) -> p t h", t=2), ALU.min, ALU.subtract
                                       ).then_inc(m_logf, 1)
                dve.wait_ge(m_cum, 1)
                link(v.tensor_copy(m_b, tb[:, 1, 16:24]))
                link(v.tensor_tensor(m_a.rearrange("p (t h) -> p t h", t=2), li,
                                     m_b.rearrange("p (t h) -> p t h", t=2), ALU.subtract))

                def diag(t):
                    v.tensor_tensor(m_diag.rearrange("p (h c) -> p h c", h=MH),
                                    ident[:].unsqueeze(1).broadcast_to([P, MH, P]),
                                    m_a[:, 4 * t:4 * t + 4].unsqueeze(2).broadcast_to([P, MH, P]),
                                    ALU.mult).then_inc(m_diag_ready, 1)

                def causal_max(t):
                    dve.wait_ge(m_spread, t + 1)
                    link(v.tensor_tensor(m_am[:, t, :].rearrange("p (h c) -> p h c", h=MH),
                                         tb[:, 0, :].rearrange("p (h c) -> p h c", h=MH),
                                         causal[:, 0:P].unsqueeze(1).broadcast_to([P, MH, P]), ALU.add))
                    link(v.tensor_reduce(m_mx[:, 4 * t:4 * t + 4],
                                         m_am[:, t, :].rearrange("p (h c) -> p h c", h=MH), AX, ALU.max))

                diag(0)
                take(2)
                causal_max(0)
                v.tensor_scalar(m_negmx[:, 0:4], m_mx[:, 0:4], -1.0, None, ALU.mult).then_inc(m_am_ready, 1)
                link(v.tensor_copy(m_last[:, 0:4], m_b[:, 0:4]))
                v.tensor_copy(m_last[:, 4:8], m_mx[:, 0:4]).then_inc(m_last_rhs, 1)
                diag(1)
                take(3)
                dve.wait_ge(m_last_in_psum, 1)
                link(v.tensor_copy(m_lrow, tb[:, 1, 24:32]))
                link(v.tensor_tensor(m_prev, m_lrow[:, 0:4], m_lrow[:, 4:8], ALU.add))
                link(v.scalar_tensor_tensor(m_exp0[:, 0:4], m_b[:, 0:4], -1.0, m_mx[:, 0:4], ALU.mult, ALU.subtract))
                v.tensor_tensor(m_exp0[:, 4:8], m_a[:, 0:4], m_lrow[:, 4:8], ALU.subtract).then_inc(m_exps, 1)
                causal_max(1)
                link(v.tensor_tensor(m_mx[:, 4:8], m_mx[:, 4:8], m_prev, ALU.max))
                v.tensor_scalar(m_negmx[:, 4:8], m_mx[:, 4:8], -1.0, None, ALU.mult).then_inc(m_am_ready, 1)
                link(v.scalar_tensor_tensor(m_exp1[:, 0:4], m_b[:, 4:8], -1.0, m_mx[:, 4:8], ALU.mult, ALU.subtract))
                v.tensor_tensor(m_exp1[:, 4:8], m_prev, m_mx[:, 4:8], ALU.subtract).then_inc(m_exps, 1)
                dve.wait_ge(m_exped, 1)
                v.tensor_tensor(m_ksc.rearrange("p (h c) -> p h c", h=MH),
                                m_kn[:, 0, :].rearrange("p (h c) -> p h c", h=MH),
                                m_exp0[:, 4:8].unsqueeze(2).broadcast_to([P, MH, P]), ALU.mult
                                ).then_inc(m_ksc_ready, 1)

                def heads(ap):
                    return ap.rearrange("p (h c) -> p h c", h=MH)

                def per_head(ap):
                    return ap.unsqueeze(2).broadcast_to([P, MH, MDV])

                def weigh(t):
                    dve.wait_ge(m_scores_in_psum, t + 1)
                    dve.wait_ge(m_w_ready, t + 1)
                    link(v.tensor_tensor(m_am[:, t, :], tb[:, t, :], m_am[:, t, :], ALU.mult))
                    v.tensor_reduce(m_den[:, 4 * t:4 * t + 4], heads(m_am[:, t, :]), AX, ALU.add
                                    ).then_inc(m_p_ready, 1)

                weigh(0)
                dve.wait_ge(m_state_in_psum, 2)
                v.tensor_copy(m_n, acc[:, 1, 512:516]).then_inc(m_state_ready, 1)
                dve.wait_ge(m_inter_in_psum, 1)
                dve.wait_ge(m_exped, 2)
                v.tensor_tensor(m_qn_den, acc[:, 1, 516:520], m_exp1[:, 4:8], ALU.mult).then_inc(m_qn_den_ready, 1)
                dve.wait_ge(m_inter_in_psum, 2)
                link(v.tensor_tensor(heads(m_h[:, 1, :]), gu[:].rearrange("p a (b c) -> p (a b) c", b=2),
                                     per_head(m_exp1[:, 4:8]), ALU.mult))
                weigh(1)
                dve.wait_ge(m_p_ready, 2)
                link(v.tensor_tensor(m_den[:, 4:8], m_den[:, 4:8], m_qn_den, ALU.add))
                link(v.scalar_tensor_tensor(m_den, m_den, -1.0, m_den, ALU.mult, ALU.max))
                link(v.tensor_tensor(m_den[:, 0:4], m_den[:, 0:4], m_exp0[:, 0:4], ALU.max))
                link(v.tensor_tensor(m_den[:, 4:8], m_den[:, 4:8], m_exp1[:, 0:4], ALU.max))
                link(v.reciprocal(m_rden, m_den))
                dve.wait_ge(m_num_in_psum, 1)
                v.tensor_tensor(heads(m_h[:, 0, :]), gu[:].rearrange("p a (b c) -> p (a b) c", b=2),
                                per_head(m_rden[:, 0:4]), ALU.mult).then_inc(m_h_ready, 1)
                def second_h():
                    dve.wait_ge(m_num_in_psum, 2)
                    for half in range(2):
                        h1 = m_h[:, 1, 512 * half:512 * half + 512]
                        ins = v.tensor_tensor(h1, acc[:, half, 0:512], h1, ALU.add)
                    link(ins)
                    v.tensor_tensor(heads(m_h[:, 1, :]), heads(m_h[:, 1, :]), per_head(m_rden[:, 4:8]), ALU.mult
                                    ).then_inc(m_h_ready, 1)

                def gate_gain(c, t):
                    dve.wait_ge(m_o_gate, 2 * (c - 4) + t + 1)
                    cols = slice(512 * (c - 4), 512 * (c - 4) + 512)
                    return v.tensor_tensor(m_sig[:, t, cols], m_sig[:, t, cols], gain_bc[:, cols], ALU.mult)

                dve.wait_ge(gain_landed, 16 * 2)
                gate_gain(4, 0)
                link(gate_gain(4, 1))
                for t in range(TILES):
                    dve.wait_ge(m_hsums, t + 1)
                    c = slice(4 * t, 4 * t + 4)
                    rsqrt_steps(m_hssq[:, c], m_hmean[:, c], m_hz[:, c], nt_[:, 0:4], 1.0 / MDV)
                    for h in range(MH):
                        if h == 2:
                            link(gate_gain(5, t))
                        cols = slice(MDV * h, MDV * h + MDV)
                        ins = v.scalar_tensor_tensor(m_h[:, t, cols], m_h[:, t, cols],
                                                     m_hz[:, 4 * t + h:4 * t + h + 1], m_sig[:, t, cols],
                                                     ALU.mult, ALU.mult)
                    ins.then_inc(m_y_ready, 1)
                    if t == 0:
                        second_h()
                    t_units("MO", t)
                boundary("MO", 3, 1.0, acc, S["MO"] + 3, "F1")

            def diff():
                m, s0 = PRE["DQ"], S["DQ"]
                dve.wait_ge(d_landed, 32)
                for a in range(2):
                    link(v.tensor_tensor(lamv[:, 128 * a:128 * a + 64], lamv[:, 128 * a:128 * a + 64],
                                         lamv[:, 128 * a + 64:128 * a + 128], ALU.mult))
                v.tensor_reduce(lamp[:, 0:2], lamv.rearrange("p (a d) -> p a d", a=2)[:, :, 0:64], AX, ALU.add
                                ).then_inc(d_lam, 1)
                dve.wait_ge(d_lamexp, 1)
                link(v.tensor_tensor(lamp[:, 4:5], lamp[:, 3:4], lamp[:, 2:3], ALU.subtract))
                link(v.tensor_scalar(lamp[:, 5:6], lamp[:, 4:5], -LAM0, None, ALU.add))
                dve.wait_ge(rstd_ready, 2 * m + 2)
                for t in range(TILES):
                    dve.wait_ge((tile0_used, slot_used)[t], s0 + 4)
                    for half in range(2):
                        cols = slice(512 * half, 512 * half + 512)
                        v.tensor_scalar(qn[:, t, cols], acc[:, t, cols], rstd[:, 2 * m + t:2 * m + t + 1], 0.125,
                                        ALU.mult, ALU.mult).then_inc(d_qn_ready, 1)
                for step in range(DH + 1):
                    h = step
                    if h < DH:
                        dve.wait_ge(d_scores, h + 1)
                        if h >= 2:
                            dve.wait_ge(d_dif_ready, h - 1)
                        s, st = sc_[:, h % 2, :], dstat[:, h % 2, :]
                        for t in range(TILES):
                            for a in range(2):
                                cols = slice(P * t, P * t + P * (t + 1))
                                i = 4 + 2 * t + a
                                v.tensor_tensor_reduce(s[:, LCOLS * a + P * t:LCOLS * a + P * t + P * (t + 1)],
                                                       (tb, gu)[a][:, h % 2, cols], causal[:, cols], -1.0, 3.0e38,
                                                       ALU.add, ALU.min, st[:, i:i + 1]).then_inc(d_negmax, 1)
                    h = step - 1
                    if h >= 0:
                        dve.wait_ge(d_exped, h + 1)
                        s, st = sc_[:, h % 2, :], dstat[:, h % 2, :]
                        link(v.reciprocal(st[:, 12:16], st[:, 8:12]))
                        rr = st[:, 12:16].rearrange("p (t a) -> p t a", t=2)
                        link(v.tensor_scalar(rr[:, :, 1:2], rr[:, :, 1:2], lamp[:, 5:6], None, ALU.mult))
                        if h >= 2:
                            dve.wait_ge(d_dt_in_psum, h - 1)
                        d = dif[:, h % 2, :]
                        v.tensor_scalar(d[:, 0:P], s[:, 0:P], st[:, 12:13], None, ALU.mult)
                        link(v.tensor_scalar(d[:, P:LCOLS], s[:, P:LCOLS], st[:, 14:15], None, ALU.mult))
                        v.scalar_tensor_tensor(d[:, 0:P], s[:, LCOLS:LCOLS + P], st[:, 13:14], d[:, 0:P],
                                               ALU.mult, ALU.add)
                        v.scalar_tensor_tensor(d[:, P:LCOLS], s[:, LCOLS + P:2 * LCOLS], st[:, 15:16], d[:, P:LCOLS],
                                               ALU.mult, ALU.add).then_inc(d_dif_ready, 1)
                def norms(g):
                    dve.wait_ge(d_o_ready, 4 * g + 4)
                    c = 8 * g
                    rsqrt_steps(hstat[:, c:c + 8], hstat[:, 16 + c:24 + c], hstat[:, 32 + c:40 + c],
                                hstat[:, 48 + c:56 + c], 1.0 / P)

                def normed(g, t):
                    c = 32 + 8 * g + 4 * t
                    y = qn[:, t, 512 * g:512 * g + 512].rearrange("p (h c) -> p h c", h=4)
                    return v.tensor_tensor(y, y, hstat[:, c:c + 4].unsqueeze(2).broadcast_to([P, 4, P]), ALU.mult)

                norms(0)
                normed(0, 0).then_inc(d_y_ready, 1)
                t_units("DO", 0, (0,))
                norms(1)
                normed(1, 0).then_inc(d_y_ready, 1)
                t_units("DO", 0, (1,))
                normed(0, 1)
                normed(1, 1).then_inc(d_y_ready, 1)
                t_units("DO", 1)
                boundary("DO", 7, 1.0, acc, S["DO"] + 3, "F3")

            def hybrid():
                m, s0 = PRE["HI"], S["HI"]
                dve.wait_ge(rstd_ready, 2 * m + 2)

                def r(t):
                    return rstd[:, 2 * m + t:2 * m + t + 1]

                def bank(c, t):
                    return acc[:, t, 512 * (c % 2):512 * (c % 2) + 512]

                def step(k):
                    h = k
                    if h < AH:
                        dve.wait_ge(h_scores, h + 1)
                        if h >= 2:
                            dve.wait_ge(h_pt_in_psum, h - 1)
                        s, st = h_sc[:, h % 2, :], h_mx[:, h % 2, :]
                        link(v.scalar_tensor_tensor(s, rel[:], 2.0 ** (-8.0 * (h + 1) / AH), gu[:, h % 2, 0:LCOLS],
                                                    ALU.mult, ALU.add))
                        v.tensor_reduce(st[:, 0:1], s[:, 0:P], AX, ALU.max)
                        link(v.tensor_reduce(st[:, 1:2], s[:, P:LCOLS], AX, ALU.max))
                        v.tensor_scalar(st[:, 2:4], st[:, 0:2], -1.0, None, ALU.mult).then_inc(h_negmax, 1)
                    h = k - 1
                    if 0 <= h < AH:
                        dve.wait_ge(h_exped, h + 1)
                        s = h_sc[:, h % 2, :]
                        v.tensor_tensor_reduce(s[:, 0:P], s[:, 0:P], times[:, 0:P], 1.0, 0.0, ALU.mult, ALU.add,
                                               h_den[:, h % 4, 0:1])
                        link(v.tensor_tensor_reduce(s[:, P:LCOLS], s[:, P:LCOLS], times[:, P:LCOLS], 1.0, 0.0,
                                                    ALU.mult, ALU.add, h_den[:, h % 4, 1:2]))
                        v.reciprocal(h_rden[:, h % 4, :], h_den[:, h % 4, :]).then_inc(h_p_ready, 1)
                    h = k - 3
                    if 0 <= h < AH:
                        dve.wait_ge(h_pv_in_psum, h + 1)
                        at = AD * (h % 2)
                        v.tensor_tensor(h_o[:, h // 2, :, at:at + AD],
                                        gu[:, h % 2, LCOLS:512].rearrange("p (t c) -> p t c", t=2),
                                        h_rden[:, h % 4, :].unsqueeze(2).broadcast_to([P, TILES, AD]), ALU.mult
                                        ).then_inc(h_o_ready, 1)

                def take(c):
                    for t in range(TILES):
                        dve.wait_ge((tile0_used, slot_used)[t], s0 + 2 * c + 2)
                        if c in H_S_FREE:
                            dve.wait_ge(h_pl_in_psum, H_S_FREE[c] + t)
                        s = h_s[:, H_PLACE[c], t, :] if c in H_PLACE else None
                        if c < 2:
                            ins = v.tensor_scalar(s, bank(c, t), r(t), float(AD) ** -0.5, ALU.mult, ALU.mult)
                        elif c < 4 or c in (6, 8):
                            ins = v.tensor_scalar(s, bank(c, t), r(t), None, ALU.mult)
                        elif c < 6:
                            ins = v.tensor_scalar(h_v[:, t, 512 * (c - 4):512 * (c - 4) + 512], bank(c, t), r(t),
                                                  None, ALU.mult)
                        elif c in (7, 9):
                            ins = v.scalar_tensor_tensor(s, bank(c, t), r(t), s, ALU.mult, ALU.mult)
                        else:
                            dve.wait_ge(h_silu, H_SILU[c - 1] - 1 + t)
                            ins = v.scalar_tensor_tensor(s, bank(c, t), r(t), s, ALU.mult, ALU.mult)
                        ins.then_inc(h_evac, 1)

                def convolve(k):
                    dve.wait_ge(h_pl_ready, 10 + 2 * (k // 4))
                    z, u = h_zT[:, k, :], h_uT[:, k, :]
                    w = [gcol[:, CONVW + 8 * i + k:CONVW + 8 * i + k + 1] for i in range(3)]
                    link(v.tensor_scalar(z, u, w[2], None, ALU.mult))
                    link(v.scalar_tensor_tensor(z[:, 1:256], u[:, 0:255], w[1], z[:, 1:256], ALU.mult, ALU.add))
                    v.scalar_tensor_tensor(z[:, 2:256], u[:, 0:254], w[0], z[:, 2:256], ALU.mult, ALU.add
                                           ).then_inc(h_conv, 1)

                def z_units(c):
                    half = (c - 11) // 2
                    dve.wait_ge(h_conv, 4 * half + 4)
                    for t in range(TILES):
                        dve.wait_ge(h_pl_in_psum, H_UNIT_NO[c] + t + 1)
                        z = h_zT[:, 4 * half:4 * half + 4, tok(t)]
                        v.tensor_tensor(z, tb[:, 1, :].rearrange("p (k c) -> p k c", k=4), z, ALU.mult
                                        ).then_inc(h_z_ready, 1)

                def gate_before_sigmoid(c, t):
                    dve.wait_ge(h_bm_landed, 16)
                    dve.wait_ge((tile0_used, slot_used)[t], s0 + 2 * c + 2)
                    g = (h_gc, h_ga)[c // 18][:, t, 512 * (c % 2):512 * (c % 2) + 512]
                    v.scalar_tensor_tensor(g, bank(c, t), r(t), h_bm[:, 512 * (c - 16):512 * (c - 16) + 512],
                                           ALU.mult, ALU.add).then_inc(h_gpre, 1)

                steps = 0
                for c in range(18):
                    for j in range(2):
                        if H_UNITS_AT.get((c, j)) in (11, 13):
                            z_units(c - 1)
                        if c >= 5 and steps < AH + 3:
                            step(steps)
                            steps += 1
                        if (c, j) in H_CONVOLVE:
                            convolve(H_CONVOLVE[c, j])
                    if c < 10 or c in (11, 13):
                        take(c)
                    elif c in (14, 15):
                        dve.wait_ge(h_o_ready, AH)
                        for t in range(TILES):
                            dve.wait_ge(h_silu, H_SILU[c] - 1 + t)
                            o = h_o[:, 4 * (c - 14):4 * (c - 14) + 4, t, :]
                            v.tensor_tensor(o, o, h_s[:, H_PLACE[c], t, :].rearrange("p (k c) -> p k c", k=4),
                                            ALU.mult).then_inc(h_gated, 1)
                    elif c in (16, 17):
                        for t in range(TILES):
                            gate_before_sigmoid(c, t)
                for t in range(TILES):
                    gate_before_sigmoid(18, t)
                    gate_before_sigmoid(19, t)
                    for half in range(2):
                        dve.wait_ge(t_hi_ready, 4 * T["HC"] + 2 * t + half + 1)
                        at = (slice(4 * half, 4 * half + 4), tok(t))
                        v.tensor_tensor(xT_lo[:, at[0], at[1]], h_zT[:, at[0], at[1]],
                                        xT_hi[:, at[0], at[1]].bitcast(F32), ALU.subtract).then_inc(t_lo_ready, 1)
                dve.wait_ge(h_sig, 4)
                for t in range(TILES):
                    dve.wait_ge((tile0_used, slot_used)[t], S["HC"] + 4)
                    for half, src in enumerate((gu, tb)):
                        cols = slice(512 * half, 512 * half + 512)
                        ins = v.tensor_tensor(h_m[:, t, cols], src[:, t, :], h_gc[:, t, cols], ALU.mult)
                    link(ins)
                    t_units("HA", t)
                for t in range(TILES):
                    dve.wait_ge(h_sig, 4 + t + 1)
                    dve.wait_ge((tile0_used, slot_used)[t], S["HA"] + 4)
                    link(v.tensor_tensor(h_ga[:, t, :], acc[:, t, :], h_ga[:, t, :], ALU.mult))
                    v.tensor_tensor(h_m[:, t, :], h_m[:, t, :], h_ga[:, t, :], ALU.add).then_inc(h_m_ready, 1)
                    t_units("HO", t)
                dve.wait_ge(f_gain_landed, 16)
                for t in range(TILES):
                    dve.wait_ge((tile0_used, slot_used)[t], S["HO"] + 4)
                    for half, src in enumerate((gu, tb)):
                        cols = slice(512 * half, 512 * half + 512)
                        v.tensor_tensor(x[:, t, cols], src[:, t, :], x[:, t, cols], ALU.add
                                        ).then_inc(x_ready, 1)
                    norm_steps(FINAL_SUM, t)
                    i = 2 * FINAL_SUM + t
                    link(v.tensor_scalar(zed[:, i:i + 1], zed[:, i:i + 1], ZS, None, ALU.mult))
                    v.scalar_tensor_tensor(f_out[:, t, :], x[:, t, :], zed[:, i:i + 1], f_gain, ALU.mult, ALU.mult
                                           ).then_inc(out_ready, 1)

            def build_tables():
                dve.wait_ge(consts_ready, 12)
                fdist, m4, m16, fwin = (build[:, i, :] for i in range(4))
                v.tensor_scalar(iand_i[:, 0:LCOLS], iota_i, 3, None, ALU.bitwise_and)
                v.tensor_scalar(iand_i[:, LCOLS:2 * LCOLS], iota_i, 15, None, ALU.bitwise_and)
                link(v.tensor_scalar(fdist, iota_i, -256.0, None, ALU.add))
                v.tensor_scalar(m4, iand_i[:, 0:LCOLS], 0.0, None, ALU.is_equal)
                v.tensor_scalar(m16, iand_i[:, LCOLS:2 * LCOLS], 0.0, None, ALU.is_equal)
                link(v.tensor_scalar(fwin, fdist, float(P), None, ALU.is_le))
                link(v.tensor_tensor(m4, m4, m16, ALU.add))
                link(v.tensor_tensor(m4, m4, fwin, ALU.add))
                link(v.tensor_scalar(m16, fdist, 0.0, None, ALU.is_ge))
                link(v.tensor_tensor(times[:], m4, m16, ALU.mult))
                link(v.tensor_scalar(m4, times[:], 0.5, None, ALU.is_le))
                link(v.tensor_scalar(m4, m4, FAR, None, ALU.mult))
                v.tensor_tensor(rel[:], m4, fdist, ALU.subtract).then_inc(tables_ready, 1)
                dve.wait_ge(tables_ready, 1)

            def first_lo(slot):
                dve.wait_ge(hi_ready, slot.count())
                v.tensor_tensor(w_lo[:, slot.spl, :], w_raw[:, slot.raw, :],
                                w_hi[:, slot.spl, :].bitcast(F32), ALU.subtract).then_inc(lo_ready, 1)

            dve.wait_ge(gcol_in_psum, 1)
            v.tensor_copy(gcol[:, 0:P], acc[:, 0, 0:P]).then_inc(gcol_ready, 1)
            dve.wait_ge(gcol_ready, 1)
            dve.wait_ge(hi_ready, 1)
            v.tensor_tensor(w_lo[:, 0, SLOT // 2:], w_raw[:, 0, SLOT // 2:],
                            w_hi[:, 0, SLOT // 2:].bitcast(F32), ALU.subtract).then_inc(lo_half_ready, 1)
            t_units("F0", 0)
            dve.wait_ge(lo_ready, 1)
            first_lo(At(1))
            t_units("F0", 1)
            pre_norm("F0", 0)
            pre_norm("F0", 1)
            dve.wait_ge(gcol_in_psum, 2)
            v.tensor_copy(gcol[:, P:168], acc[:, 0, 512:552]).then_inc(gcol_ready, 1)
            dve.wait_ge(gcol_ready, 2)
            p_lo(0)
            dve.wait_ge(wg_split, 1)
            v.tensor_tensor(wg_lo[:], wg_raw[:], wg_hi[:].bitcast(F32), ALU.subtract).then_inc(wg_split, 1)
            ffn("F0", 1, "MI")
            mlstm()
            ffn("F1", 4, "P0")
            ple("P0", 0, 5, "KV")
            dve.wait_ge(rstd_ready, 2 * PRE["KV"] + 2)
            for g, dst in enumerate((kn, v_sh)):
                if g:
                    p_lo(1)
                for t in range(TILES):
                    for c in (2 * g, 2 * g + 1):
                        dve.wait_ge((tile0_used, slot_used)[t], S["KV"] + 2 * c + 2)
                        i = 2 * PRE["KV"] + t
                        v.tensor_scalar(dst[:, t, 512 * (c % 2):512 * (c % 2) + 512], pair(c, t),
                                        rstd[:, i:i + 1], None, ALU.mult).then_inc(kv_copied, 1)
                    if g:
                        t_units("F2", t)
            ffn("F2", 6, "DQ")
            diff()
            ffn("F3", 8, "P1")
            ple("P1", 1, 9, "HI")
            hybrid()

        @block.tensor
        def _(pe):
            mm = nc.tensor.matmul

            def has_t(q, t, half):
                pe.wait_ge(t_lo_ready, 4 * T[q] + 2 * t + half + 1)

            def across_tile(slot, half, t, out, q=None):
                pe.wait_ge(lo_ready, slot.count())
                if q:
                    has_t(q, t, half)
                for k in range(4):
                    wh = w_hi[:, slot.spl, 512 * k:512 * k + 512]
                    wl = w_lo[:, slot.spl, 512 * k:512 * k + 512]
                    xh, xl = xT_hi[:, 4 * half + k, tok(t)], xT_lo[:, 4 * half + k, tok(t)]
                    mm(out, xh, wh, start=(half == 0 and k == 0), stop=False)
                    mm(out, xh, wl, start=False, stop=False)
                    last = mm(out, xl, wh, start=False, stop=(half == 1 and k == 3))
                last.then_inc((tile0_used, slot_used)[t], 1)

            def across(slot, half, outs):
                for t in range(TILES):
                    across_tile(slot, half, t, outs[t])

            def by_tile(s0, count, q, outs, amid):
                for t in range(TILES):
                    for i in range(count):
                        across_tile(At(s0 + i), i % 2, t, outs(i // 2, t), q if i < 2 else None)
                        if i == max(1, count - 2) and amid[t]:
                            amid[t]()

            def down_tile(slot, a_hi, a_lo, t, first, final, amid=None):
                pe.wait_ge(lo_ready, slot.count())
                for k in range(2):
                    def w(ring, half):
                        return ring[:, slot.spl, D * k + 512 * half:D * k + 512 * half + 512]
                    st, sp_ = first and k == 0, final and k == 1
                    for half in range(2):
                        mm(acc[:, t, 512 * half:512 * half + 512], a_hi[:, k, tok(t)], w(w_hi, half),
                           start=st, stop=False)
                    for half in range(2):
                        mm(acc[:, t, 512 * half:512 * half + 512], a_hi[:, k, tok(t)], w(w_lo, half),
                           start=False, stop=False)
                    for half in range(2):
                        last = mm(acc[:, t, 512 * half:512 * half + 512], a_lo[:, k, tok(t)], w(w_hi, half),
                                  start=False, stop=sp_)
                    if k == 0 and amid:
                        amid()
                last.then_inc((tile0_used, slot_used)[t], 1)

            def t_units(q, t, src, wait, halves=(0, 1)):
                for half in halves:
                    u = 4 * T[q] + 2 * t + half
                    wait(half)
                    if psum_units(u) > 2:
                        pe.wait_ge(t_scaled, psum_units(u) - 2)
                    for k in range(4):
                        ins = nc.tensor.transpose(t_bank(q, t, half)[:, tok(k)], src(4 * half + k), ident[:])
                    ins.then_inc(t_in_psum, 1)

            def t_of_x(name, t, halves=(0, 1)):
                n = PRE[name]

                def wait(half):
                    if n:
                        pe.wait_ge(x_ready, x_count(n - 1, t, half))
                    elif half == 0:
                        pe.wait_ge(x_landed[t], 16)
                t_units(name, t, lambda k: x[:, t, tok(k)], wait, halves)

            def ffn(name, following):
                f, s0 = FFN_NO[name], S[name]

                def gate_up(n, turn, a):
                    if n:
                        pe.wait_ge(h_ready, 2 * NIT * f + 2 * n if turn is None else turn * 4 + 2 * NIT * f + 2 * n)
                    across(a, 0, [gu[:, t, :] for t in range(TILES)])
                    across(a.plus(1), 1, [gu[:, t, :] for t in range(TILES)])

                def down_n(n, turn, slot):
                    pe.wait_ge(ht_lo_ready, ht_count(f, n) if turn is None else turn * 2 + ht_count(f, n))
                    for t in range(TILES):
                        down_tile(slot, hT_hi, hT_lo, t, n == 0, False)

                def turn_h(n, turn):
                    pe.wait_ge(h_ready, 2 * NIT * f + 2 * n + 2 if turn is None
                               else turn * 4 + 2 * NIT * f + 2 * n + 2)
                    for k in range(2):
                        for t in range(TILES):
                            ins = nc.tensor.transpose(tb[:, 0, 256 * k + P * t:256 * k + P * t + P],
                                                      hs[:, t, tok(k)], ident[:])
                    ins.then_inc(ht_in_psum, 1)

                def second_tile():
                    if name == "F0":
                        turn_gains(2)
                        turn_p(0)
                    elif name != "F2":
                        t_of_x(name, 1)

                if name == "F2":
                    t_of_x(name, 1)

                by_tile(s0, 2, name, lambda c, t: gu[:, t, :], (second_tile, None))
                pe.wait_ge(h_ready, 2 * NIT * f + 1)
                across_tile(At(s0 + 2), 0, 0, gu[:, 0, :])
                turn_h(0, None)
                across_tile(At(s0 + 2), 0, 1, gu[:, 1, :])
                across(At(s0 + 3), 1, [gu[:, t, :] for t in range(TILES)])
                if name == "F0":
                    pe.wait_ge(gcol_ready, 2)
                    pe.wait_ge(pt_lo_ready, 1)
                down_n(0, None, At(s0 + 4))
                turn_h(1, None)
                with pe.Fori(0, (NIT - 3) // 2) as i:
                    for d in (0, 1):
                        gate_up(2 + d, i, At(s0 + 5 + 3 * d, i))
                        down_n(1 + d, i, At(s0 + 7 + 3 * d, i))
                        turn_h(2 + d, i)

                n, a = NIT - 1, At(s0 + FFN_SLOTS - 4)

                def turn_tile(t):
                    pe.wait_ge(h_ready, 2 * NIT * f + 2 * n + t + 1)
                    for k in range(2):
                        ins = nc.tensor.transpose(tb[:, t, tok(k)], hs[:, t, tok(k)], ident[:])
                    ins.then_inc(ht_in_psum, 1)

                pe.wait_ge(h_ready, 2 * NIT * f + 2 * n)
                across_tile(a, 0, 0, gu[:, 0, :])
                across_tile(a.plus(1), 1, 0, gu[:, 0, :])
                pe.wait_ge(ht_lo_ready, ht_count(f, n - 1))
                down_tile(a.plus(2), hT_hi, hT_lo, 0, False, False)
                turn_tile(0)
                across_tile(a, 0, 1, gu[:, 1, :])
                pe.wait_ge(ht_lo_ready, ht_count(f, n, 0))
                down_tile(a.plus(3), hT_hi, hT_lo, 0, False, True)
                across_tile(a.plus(1), 1, 1, gu[:, 1, :])
                down_tile(a.plus(2), hT_hi, hT_lo, 1, False, False, amid=lambda: turn_tile(1))
                pe.wait_ge(ht_lo_ready, ht_count(f, n, 1))
                down_tile(a.plus(3), xT_hi, xT_lo, 1, False, True, amid=lambda: t_of_x(following, 0, (0,)))
                t_of_x(following, 0, (1,))

            def acc_outs(c, t):
                return acc[:, t, 512 * c:512 * c + 512]

            def turn_p(layer):
                pe.wait_ge(p_landed, 16 * (layer + 1))
                dst = (acc[:, 1, 0:512], tb[:, 1, :])[layer]
                for k in range(2):
                    for t in range(TILES):
                        ins = nc.tensor.transpose(dst[:, 256 * k + P * t:256 * k + P * t + P],
                                                  p_nat[:, t, tok(k)], ident[:])
                ins.then_inc(pt_in_psum, 1)

            def ple(name, layer, following):
                s0 = S[name]
                pe.wait_ge(pt_lo_ready, layer + 1)
                for t in range(TILES):
                    pe.wait_ge(x_ready, x_count(PRE[name] - 1, t, 1))
                    down_tile(At(s0), pT_hi, pT_lo, t, True, True)
                    for i in range(4):
                        if i == 2 and t == 0:
                            t_of_x(name, 1)
                            pe.wait_ge(t_scaled, psum_units(4 * T[name] + 2))
                        if i == 3 and t == 1:
                            t_of_x(following, 0)
                        across_tile(At(s0 + 1 + i), i % 2, t, (gu, tb)[i // 2][:, t, :], name if i < 2 else None)

            def mlstm():
                s0 = S["MI"]

                def chunk(c, amid={}):
                    if c >= 3:
                        pe.wait_ge(m_copied, 2 * (c - 3) + 2)
                    for i in range(2 * TILES):
                        j, t = (i % 2, i // 2) if c == 5 else (i // 2, i % 2)
                        across_tile(At(s0 + 2 * c + j), j, t, pair(c, t))
                        if i in amid:
                            amid[i]()

                by_tile(s0, 4, "MI", pair, (lambda: t_of_x("MI", 1), None))
                pe.wait_ge(wg_split, 2)
                o = tb[0:8, 1, 256:512]
                for k in range(KT):
                    mm(o, wg_hi[:, k, :], xT_hi[:, k, :], start=(k == 0), stop=False)
                    mm(o, wg_lo[:, k, :], xT_hi[:, k, :], start=False, stop=False)
                    ins = mm(o, wg_hi[:, k, :], xT_lo[:, k, :], start=False, stop=(k == KT - 1))
                ins.then_inc(m_gt_in_psum, 1)

                def turn_gates():
                    pe.wait_ge(m_gt_ready, 1)
                    for t in range(TILES):
                        ins = nc.tensor.transpose(tb[:, 1, 8 * t:8 * t + 8], m_gT[:, tok(t)], ident[0:8, 0:8])
                    ins.then_inc(m_gates_in_psum, 1)

                def cumulate():
                    pe.wait_ge(m_logf, 1)
                    mm(tb[:, 1, 16:24], upto[:], m_lf, start=True, stop=True).then_inc(m_cum, 1)

                chunk(2, {0: turn_gates, 3: cumulate})

                def spread(t):
                    pe.wait_ge(m_diag_ready, t + 1)
                    if t:
                        pe.wait_ge(m_am_ready, t)
                    mm(tb[:, 0, :], ones[:], m_diag, start=True, stop=True).then_inc(m_spread, 1)

                chunk(3, {0: lambda: spread(0)})
                pe.wait_ge(m_last_rhs, 1)
                mm(tb[:, 1, 24:32], last_row[:], m_last, start=True, stop=True).then_inc(m_last_in_psum, 1)
                spread(1)

                def turn_qk(i):
                    pe.wait_ge(m_am_ready, 2)
                    for w in (2 * i, 2 * i + 1):
                        if i:
                            pe.wait_ge(m_pl_ready, w - 1)
                        for h in range(MH):
                            ins = nc.tensor.transpose(tb[:, w % 2, tok(h)], (m_qn, m_kn)[i][:, w % 2, tok(h)],
                                                      ident[:])
                        ins.then_inc(m_pl_in_psum, 1)

                def scores(t):
                    pe.wait_ge(m_pl_ready, 3 + t)
                    for h in range(MH):
                        ins = mm(tb[:, t, tok(h)], m_qT[:, h, tok(t)], m_kT[:, h, tok(t)], start=True, stop=True)
                    ins.then_inc(m_scores_in_psum, 1)

                def turn_weighted(t):
                    pe.wait_ge(m_p_ready, t + 1)
                    for h in range(MH):
                        ins = nc.tensor.transpose(tb[:, t, tok(h)], m_am[:, t, tok(h)], ident[:])
                    ins.then_inc(m_pt_in_psum, 1)

                def numerator(t, dst):
                    pe.wait_ge(m_pt_ready, t + 1)
                    for h in range(MH):
                        ins = mm(dst(h), m_PT[t][:, tok(h)], m_v[:, t, MDV * h:MDV * h + MDV],
                                 start=True, stop=True)
                    ins.then_inc(m_num_in_psum, 1)

                cs = gu[:].rearrange("p a (b c) -> p (a b) c", b=2)

                def state():
                    pe.wait_ge(m_ksc_ready, 1)
                    pe.wait_ge(m_copied, 8)
                    for h in range(MH):
                        ins = mm(cs[:, h, :], m_ksc[:, tok(h)], m_v[:, 0, MDV * h:MDV * h + MDV],
                                 start=True, stop=True)
                    ins.then_inc(m_state_in_psum, 1)
                    for h in range(MH):
                        ins = mm(acc[:, 1, 512 + h:513 + h], m_ksc[:, tok(h)], ones[:, 0:1], start=True, stop=True)
                    ins.then_inc(m_state_in_psum, 1)

                def on_state():
                    pe.wait_ge(m_pl_ready, 4)
                    pe.wait_ge(m_state_ready, 2)
                    for h in range(MH):
                        ins = mm(acc[:, 1, 516 + h:517 + h], m_qT[:, h, tok(1)], m_n[:, h:h + 1],
                                 start=True, stop=True)
                    ins.then_inc(m_inter_in_psum, 1)
                    for h in range(MH):
                        ins = mm(cs[:, h, :], m_qT[:, h, tok(1)], m_C[:, MDV * h:MDV * h + MDV],
                                 start=True, stop=True)
                    ins.then_inc(m_inter_in_psum, 1)

                def scores_and_state():
                    scores(0)
                    state()

                def on_state_and_scores():
                    on_state()
                    scores(1)
                    turn_weighted(0)

                def first_numerator():
                    pe.wait_ge(m_p_ready, 2)
                    numerator(0, lambda h: cs[:, h, :])
                    turn_weighted(1)
                    pe.wait_ge(m_qn_den_ready, 1)

                def second_numerator():
                    pe.wait_ge(m_o_gate, 2)
                    numerator(1, lambda h: acc[:, h // 2, MDV * (h % 2):MDV * (h % 2) + MDV])

                chunk(4, {0: lambda: turn_qk(0), 1: lambda: turn_qk(1), 2: scores_and_state,
                          3: on_state_and_scores})

                def t_of_h(t):
                    t_units("MO", t, lambda k: m_h[:, t, tok(k)], lambda half: pe.wait_ge(m_y_ready, t + 1))

                chunk(5, {0: first_numerator, 1: second_numerator, 2: lambda: t_of_h(0)})
                pe.wait_ge(m_h_ready, 2)
                by_tile(S["MO"], 4, "MO", acc_outs, (lambda: t_of_h(1), lambda: t_of_x("F1", 0)))

            def diff():
                def turn_q(t):
                    for w in (2 * t, 2 * t + 1):
                        pe.wait_ge(d_qn_ready, w + 1)
                        if t:
                            pe.wait_ge(d_pl_ready, w - 1)
                        for k in range(4):
                            ins = nc.tensor.transpose(tb[:, w % 2, tok(k)], qn[:, t, tok(4 * (w % 2) + k)], ident[:])
                        ins.then_inc(d_pl_in_psum, 1)

                by_tile(S["DQ"], 4, "DQ", acc_outs, (lambda: t_of_x("DQ", 1), lambda: turn_q(0)))
                turn_q(1)
                pe.wait_ge(d_pl_ready, 4)
                for step in range(DH + 3):
                    h = step
                    if h < DH:
                        if h >= 2:
                            pe.wait_ge(d_negmax, 4 * (h - 1))
                        for t in range(TILES):
                            for a in range(2):
                                b = slice(64 * a, 64 * a + 64)
                                o = (tb, gu)[a][:, h % 2, P * t:P * t + P * (t + 1)]
                                ins = mm(o, qT[b, h, tok(t)], kT[b, h, 0:P * (t + 1)], start=True, stop=True)
                        ins.then_inc(d_scores, 1)
                    h = step - 2
                    if 0 <= h < DH:
                        pe.wait_ge(d_dif_ready, h + 1)
                        if h >= 2:
                            pe.wait_ge(d_dt_ready, h - 1)
                        for i in range(3):
                            ins = nc.tensor.transpose(acc[:, 0, 512 * (h % 2) + P * i:512 * (h % 2) + P * i + P],
                                                      dif[:, h % 2, tok(i)], ident[:])
                        ins.then_inc(d_dt_in_psum, 1)
                    h = step - 3
                    if 0 <= h < DH:
                        pe.wait_ge(d_dt_ready, h + 1)
                        if h >= 2:
                            pe.wait_ge(d_o_ready, h - 1)
                        o = acc[:, 1, 512 * (h % 2):512 * (h % 2) + 2 * P]
                        mm(o[:, 0:P], difT[:, h % 2, 0:P], v_sh[:, 0, tok(h)], start=True, stop=True)
                        mm(o[:, P:2 * P], difT[:, h % 2, P:2 * P], v_sh[:, 0, tok(h)], start=True, stop=False)
                        mm(o[:, P:2 * P], difT[:, h % 2, 2 * P:3 * P], v_sh[:, 1, tok(h)], start=False, stop=True
                           ).then_inc(d_o_in_psum, 1)
                def t_of_o(t, halves=(0, 1)):
                    t_units("DO", t, lambda k: qn[:, t, tok(k)],
                            lambda half: pe.wait_ge(d_y_ready, 3 if t else half + 1), halves)

                t_of_o(0, (0,))
                for t in range(TILES):
                    for i in range(4):
                        across_tile(At(S["DO"] + i), i // 2, t, acc_outs(i % 2, t), "DO" if i % 2 == 0 else None)
                        if t == 0 and i == 0:
                            t_of_o(0, (1,))
                        if t == 0 and i == 2:
                            t_of_o(1)
                        if t == 1 and i == 2:
                            t_of_x("F3", 0)

            def hybrid():
                s0 = S["HI"]

                def step(k):
                    h = k
                    if h < AH:
                        if h == 0:
                            pe.wait_ge(h_pl_ready, 8)
                        if h >= 2:
                            pe.wait_ge(h_negmax, h - 1)
                        if h >= 4:
                            pe.wait_ge(h_o_ready, h - 3)
                        b = slice(AD * (h % 2), AD * (h % 2) + AD)
                        for t in range(TILES):
                            ins = mm(gu[:, h % 2, P * t:P * t + P * (t + 1)], h_qT[b, h // 2, tok(t)],
                                     h_kT[b, h // 2, 0:P * (t + 1)], start=True, stop=True)
                        ins.then_inc(h_scores, 1)
                    h = k - 2
                    if 0 <= h < AH:
                        pe.wait_ge(h_p_ready, h + 1)
                        if h >= 1:
                            pe.wait_ge(h_pt_ready, h)
                        for i in range(3):
                            ins = nc.tensor.transpose(tb[:, 0, tok(i)], h_sc[:, h % 2, tok(i)], ident[:])
                        ins.then_inc(h_pt_in_psum, 1)
                    h = k - 3
                    if 0 <= h < AH:
                        pe.wait_ge(h_pt_ready, h + 1)
                        if h + 2 < AH:
                            pe.wait_ge(h_negmax, h + 3)
                        if h >= AH - 2:
                            pe.wait_ge(h_o_ready, h - 1)
                        o = gu[:, h % 2, LCOLS:512]
                        pt = h_pT[:, h % 2, :]
                        vc = slice(AD * h, AD * h + AD)
                        mm(o[:, 0:AD], pt[:, 0:P], h_v[:, 0, vc], start=True, stop=True)
                        mm(o[:, AD:2 * AD], pt[:, P:2 * P], h_v[:, 0, vc], start=True, stop=False)
                        mm(o[:, AD:2 * AD], pt[:, 2 * P:3 * P], h_v[:, 1, vc], start=False, stop=True
                           ).then_inc(h_pv_in_psum, 1)

                def unit(c, t):
                    pe.wait_ge(h_evac, H_EVAC[c])
                    w = H_UNIT_NO[c] + t
                    if 0 < w <= 12:
                        pe.wait_ge(h_pl_ready, w)
                    elif w > 12:
                        pe.wait_ge(h_z_ready, w - 12)
                    for k in range(4):
                        ins = nc.tensor.transpose(tb[:, 1, tok(k)], h_s[:, H_PLACE[c], t, tok(k)], ident[:])
                    ins.then_inc(h_pl_in_psum, 1)

                by_tile(s0, 4, "HI", acc_outs, (lambda: t_of_x("HI", 1), None))
                steps = 0
                for c in range(2, 18):
                    if c - 2 in H_EVAC:
                        pe.wait_ge(h_evac, H_EVAC[c - 2])
                    elif c - 2 in H_SILU:
                        pe.wait_ge(h_silu, H_SILU[c - 2])
                    for j in range(2):
                        for t in range(TILES):
                            across_tile(At(s0 + 2 * c + j), j, t, acc_outs(c % 2, t))
                            if (c, j) in H_UNITS_AT:
                                unit(H_UNITS_AT[c, j], t)
                        if c >= 5 and steps < AH + 3:
                            step(steps)
                            steps += 1
                pe.wait_ge(h_gpre, 4)
                by_tile(s0 + 36, 4, None, acc_outs, (None, None))

                def t_of_a(t):
                    def wait(half):
                        pe.wait_ge(h_gated, 4)
                        pe.wait_ge(h_gpre, 4 + 2 * t + 2)
                    t_units("HA", t, lambda k: h_o[:, k, t, :], wait)

                def t_of_m(t):
                    t_units("HO", t, lambda k: h_m[:, t, tok(k)], lambda half: pe.wait_ge(h_m_ready, t + 1))

                def gu_tb(c, t):
                    return (gu, tb)[c][:, t, :]

                pe.wait_ge(h_o_ready, AH)
                pe.wait_ge(h_z_ready, 4)
                by_tile(S["HC"], 4, "HC", gu_tb, (None, lambda: t_of_a(0)))
                by_tile(S["HA"], 4, "HA", acc_outs, (lambda: t_of_a(1), lambda: t_of_m(0)))
                by_tile(S["HO"], 4, "HO", gu_tb, (lambda: t_of_m(1), None))

            def turn_gains(part):
                if part == 1:
                    pe.wait_ge(rows1_landed, 16)
                    nc.tensor.transpose(acc[:, 0, 0:P], rows1, ident[:]).then_inc(gcol_in_psum, 1)
                else:
                    pe.wait_ge(rows2_landed, 16 * 3)
                    nc.tensor.transpose(acc[:, 0, 512:552], rows2[0:40], ident[0:40, 0:40]
                                        ).then_inc(gcol_in_psum, 1)

            pe.wait_ge(consts_ready, 12)
            turn_gains(1)
            t_of_x("F0", 0)
            t_of_x("F0", 1)
            pe.wait_ge(lo_half_ready, 1)
            ffn("F0", "MI")
            mlstm()
            ffn("F1", "P0")
            ple("P0", 0, "KV")

            def turn_keys(t):
                pe.wait_ge(kv_copied, 4)
                for w in (2 * t, 2 * t + 1):
                    if t:
                        pe.wait_ge(kt_ready, w - 1)
                    for k in range(4):
                        ins = nc.tensor.transpose(acc[:, w % 2, tok(k)], kn[:, t, tok(4 * (w % 2) + k)], ident[:])
                    ins.then_inc(kt_in_psum, 1)

            def turn_keys_and_p():
                turn_keys(0)
                turn_p(1)
                turn_keys(1)

            def t_of_x_again():
                pe.wait_ge(pt_lo_ready, 2)
                t_of_x("F2", 0)

            by_tile(S["KV"], 4, "KV", pair, (lambda: t_of_x("KV", 1), None))
            pe.wait_ge(kv_copied, 3)
            by_tile(S["KV"] + 4, 4, None, lambda c, t: pair(c + 2, t), (turn_keys_and_p, t_of_x_again))
            ffn("F2", "DQ")
            diff()
            ffn("F3", "P1")
            ple("P1", 1, "HI")
            hybrid()


_INS = ["x", "p", "norm_g", "w_ffn_in", "w_ffn_out", "w_ple_proj", "w_ple_gate", "mlstm_w_in", "mlstm_b_gates",
        "mlstm_head_norm", "mlstm_w_out", "kv_norm", "w_kv", "diff_w_q", "diff_lambda", "diff_subln", "diff_w_out",
        "norm_g_2", "w_in_2", "b_merge_2", "conv_w_2", "w_out_conv_2", "w_out_attn_2", "w_o_2", "final_g_2"]


def kernel(**inputs):
    import numpy as _np
    import concourse.bacc as _bacc
    from concourse import mybir as _mybir
    from concourse.bass_utils import run_bass_kernel_spmd as _run

    nc = _bacc.Bacc("TRN2", target_bir_lowering=False, num_devices=1, dynamic_dma_scratch_size=1024)
    arrays, aps = {}, {}
    for name in _INS:
        a = _np.ascontiguousarray(inputs[name])
        arrays[f"in_{name}"] = a
        aps[name] = nc.dram_tensor(f"in_{name}", a.shape, _mybir.dt.from_np(a.dtype), kind="ExternalInput").ap()
    out = nc.dram_tensor("out_x", (1, 256, 1024), F32, kind="ExternalOutput").ap()
    program(nc, aps, out)
    r = _run(nc, [arrays], core_ids=[0])
    return r.results[0]["out_x"]
```
